# Optimizing a Trainium2 kernel written in Bass

```python
import jax, jax.numpy as jnp
from jax import lax
import numpy as np

D_MODEL = 1024
BATCH = 1
SEQ = 512
DEPTH = 1
DEC_BATCH = 8
DEC_SEQ = 4
PAST_LEN = 4096
PAGE_SIZE = 128

MIX_WIDTH = D_MODEL
GROUP_W = MIX_WIDTH // 4
D_FF = 2816
NORM_EPS = 1e-6
A_CONV = 3
A_COLS = 3 * GROUP_W
B_CONV = 31
B_LN_EPS = 1e-5
B_COLS = 2 * GROUP_W
C_HEAD = 64
C_HEADS = GROUP_W // C_HEAD
C_DECAY_LORA = 32
C_A_LORA = 32
C_V_LORA = 16
C_G_LORA = 64
C_GN_EPS = 64e-5
C_COLS = 3 * GROUP_W + C_DECAY_LORA + C_A_LORA + C_G_LORA
POOL_WINDOWS = (2, 4, 8, 16)
POOL_GROUPS = len(POOL_WINDOWS)
POOL_GW = GROUP_W // POOL_GROUPS
POOL_BUF = max(POOL_WINDOWS) - 1
D_COLS = GROUP_W
IN_COLS = A_COLS + B_COLS + C_COLS + D_COLS

kernel_name = 'hymba_style_conv_rwkv7_pool_macaron_decoder_step'

def rmsnorm(x, g):
    xf = x.astype(jnp.float32)
    y = xf * lax.rsqrt(jnp.mean(xf * xf, axis=-1, keepdims=True) + NORM_EPS)
    return (y * g.astype(jnp.float32)).astype(x.dtype)

def layernorm(x, g, b, eps):
    xf = x.astype(jnp.float32)
    mu = jnp.mean(xf, axis=-1, keepdims=True)
    var = jnp.mean(jnp.square(xf - mu), axis=-1, keepdims=True)
    return ((xf - mu) * lax.rsqrt(var + eps) * g + b).astype(x.dtype)

def swiglu(x, w_gate, w_up, w_down):
    return (jax.nn.silu(x @ w_gate) * (x @ w_up)) @ w_down

def causal_dwconv(u, buf, w):
    K, C = w.shape
    z = jnp.concatenate([buf.astype(u.dtype), u], axis=1)
    y = lax.conv_general_dilated(z, w[:, None, :].astype(u.dtype), window_strides=(1,),
                                 padding='VALID', dimension_numbers=('NWC', 'WIO', 'NWC'),
                                 feature_group_count=C)
    return y, z[:, -(K - 1):]

def wkv7_scan(S0, r, w, k, v, kk, a):
    def step(S, inp):
        r_t, w_t, k_t, v_t, kk_t, a_t = inp
        sa = jnp.einsum('bhij,bhj->bhi', S, -kk_t)
        S = (S * w_t[:, :, None, :] + sa[..., None] * (kk_t * a_t)[:, :, None, :]
             + v_t[..., None] * k_t[:, :, None, :])
        return S, jnp.einsum('bhij,bhj->bhi', S, r_t)
    xs = tuple(jnp.moveaxis(t, 1, 0) for t in (r, w, k, v, kk, a))
    S, ys = lax.scan(step, S0, xs)
    return jnp.moveaxis(ys, 0, 1), S

def rwkv7_mixer(pc, shift, S0, W, l, v_first):
    f32 = jnp.float32
    B, T, _ = pc.shape
    prev = jnp.concatenate([shift[:, None, :].astype(pc.dtype), pc[:, :-1]], axis=1)
    xm = pc + (prev - pc) * W['c_mu'][l]
    new_shift = pc[:, -1]
    o1 = GROUP_W; o2 = 2 * GROUP_W; o3 = 3 * GROUP_W
    o4 = o3 + C_DECAY_LORA; o5 = o4 + C_A_LORA
    r, k, v, wl, al, gl = jnp.split(xm, [o1, o2, o3, o4, o5], axis=-1)
    w_log = -jax.nn.softplus(-(W['c_w0'][l] + jnp.tanh(wl) @ W['c_w2'][l]).astype(f32)) - 0.5
    decay = jnp.exp(-jnp.exp(w_log))
    a = jax.nn.sigmoid((W['c_a0'][l] + al @ W['c_a2'][l]).astype(f32))
    g = jax.nn.sigmoid(gl) @ W['c_g2'][l]
    if l == 0:
        v_first = v
    else:
        vg = jax.nn.sigmoid(W['c_v0'][l - 1] + (v @ W['c_v1'][l - 1]) @ W['c_v2'][l - 1])
        v = v + (v_first - v) * vg
    heads = lambda t: t.astype(f32).reshape(B, T, C_HEADS, C_HEAD)
    kk = heads(k * W['c_k_k'][l])
    kk = kk * lax.rsqrt(jnp.maximum(jnp.sum(kk * kk, axis=-1, keepdims=True), 1e-24))
    k = k.astype(f32) * (1.0 + (a - 1.0) * W['c_k_a'][l].astype(f32))
    rh, kh, vh, ah, wh = heads(r), heads(k), heads(v), heads(a), heads(decay)
    y, S = wkv7_scan(S0.astype(f32), rh, wh, kh, vh, kk, ah)
    mu = jnp.mean(y, axis=-1, keepdims=True)
    var = jnp.mean(jnp.square(y - mu), axis=-1, keepdims=True)
    yn = ((y - mu) * lax.rsqrt(var + C_GN_EPS)).reshape(B, T, GROUP_W)
    yn = yn * W['c_ln_g'][l].astype(f32) + W['c_ln_b'][l].astype(f32)
    bonus = jnp.sum(rh * kh * W['c_r_k'][l].astype(f32), axis=-1, keepdims=True) * vh
    out = (yn + bonus.reshape(B, T, GROUP_W)) * g.astype(f32)
    return out.astype(pc.dtype), new_shift, S.astype(S0.dtype), v_first

def pool_mixer(u, buf, d_w, d_scale, past_len):
    f32 = jnp.float32
    B, T, C = u.shape
    z = jnp.concatenate([buf.astype(u.dtype), u], axis=1)
    zf = z.astype(f32)
    cs = jnp.concatenate([jnp.zeros((B, 1, C), f32), jnp.cumsum(zf, axis=1)], axis=1)
    pos = past_len + jnp.arange(T, dtype=jnp.int32)
    outs = []
    for gi, win in enumerate(POOL_WINDOWS):
        c0, c1 = gi * POOL_GW, (gi + 1) * POOL_GW
        s = (cs[:, POOL_BUF + 1:POOL_BUF + 1 + T, c0:c1]
             - cs[:, POOL_BUF + 1 - win:POOL_BUF + 1 - win + T, c0:c1])
        cnt = jnp.minimum(pos + 1, win).astype(f32)
        outs.append(s / cnt[None, :, None] - zf[:, POOL_BUF:, c0:c1])
    diff = jnp.stack(outs, axis=2)
    y = jnp.einsum('btgc,gcd->btgd', diff, d_w.astype(f32)).reshape(B, T, C) * d_scale.astype(f32)
    return y.astype(u.dtype), z[:, -POOL_BUF:]

def token_mixing(h, st, W, l, v_first, past_len):
    conv_a, conv_b, shift_c, wkv_c, pool_d = st
    proj = h @ W['w_in'][l]
    pa, pb, pc, pd = jnp.split(proj, [A_COLS, A_COLS + B_COLS, A_COLS + B_COLS + C_COLS], axis=-1)
    a_h, a_b, a_c = jnp.split(pa, 3, axis=-1)
    a_conv, new_conv_a = causal_dwconv(a_c * a_h, conv_a, W['a_conv_w'][l])
    y_a = a_b * a_conv
    b_val, b_gate = jnp.split(pb, 2, axis=-1)
    b_conv, new_conv_b = causal_dwconv(b_val * jax.nn.sigmoid(b_gate), conv_b, W['b_conv_w'][l])
    y_b = jax.nn.silu(layernorm(b_conv + W['b_conv_b'][l], W['b_ln_g'][l], W['b_ln_b'][l], B_LN_EPS))
    y_c, new_shift_c, new_wkv_c, v_first = rwkv7_mixer(pc, shift_c, wkv_c, W, l, v_first)
    y_d, new_pool_d = pool_mixer(pd, pool_d, W['d_w'][l], W['d_scale'][l], past_len)
    y = jnp.concatenate([y_a, y_b, y_c, y_d], axis=-1) @ W['w_out'][l]
    return y, (new_conv_a, new_conv_b, new_shift_c, new_wkv_c, new_pool_d), v_first

def run_trunk(x, states, W, past_len):
    v_first = None
    new = [[], [], [], [], []]
    for l in range(DEPTH):
        f1 = swiglu(rmsnorm(x, W['ffn1_pre_g'][l]), W['ffn1_w_gate'][l], W['ffn1_w_up'][l], W['ffn1_w_down'][l])
        x = x + 0.5 * rmsnorm(f1, W['ffn1_post_g'][l])
        st = tuple(s[l] for s in states)
        y, nst, v_first = token_mixing(rmsnorm(x, W['mix_pre_g'][l]), st, W, l, v_first, past_len)
        x = x + rmsnorm(y, W['mix_post_g'][l])
        f2 = swiglu(rmsnorm(x, W['ffn2_pre_g'][l]), W['ffn2_w_gate'][l], W['ffn2_w_up'][l], W['ffn2_w_down'][l])
        x = x + 0.5 * rmsnorm(f2, W['ffn2_post_g'][l])
        for lst, s in zip(new, nst):
            lst.append(s)
    return x, [jnp.stack(s) for s in new]

def setup_inputs(seed: int = 0) -> dict:
    key = jax.random.key(seed)
    ks = iter(jax.random.split(key, 64))
    f32 = jnp.float32
    def nrm(shape, scale):
        return scale * jax.random.normal(next(ks), shape, f32)
    def gain(shape):
        return 1.0 + 0.05 * jax.random.normal(next(ks), shape, f32)
    def unif(shape, lo, hi):
        return jax.random.uniform(next(ks), shape, f32, lo, hi)
    D, F, G = D_MODEL, D_FF, GROUP_W
    return {
        'x_prompt': nrm((BATCH, SEQ, D), 1.0),
        'x_sample': nrm((DEC_BATCH, DEC_SEQ, D), 1.0),
        'state_conv_a': nrm((DEPTH, DEC_BATCH, A_CONV - 1, G), 1.0),
        'state_conv_b': nrm((DEPTH, DEC_BATCH, B_CONV - 1, G), 0.5),
        'state_shift_c': nrm((DEPTH, DEC_BATCH, C_COLS), 1.0),
        'state_wkv_c': nrm((DEPTH, DEC_BATCH, C_HEADS, C_HEAD, C_HEAD), 0.3),
        'state_pool_d': nrm((DEPTH, DEC_BATCH, POOL_BUF, G), 1.0),
        'ffn1_pre_g': gain((DEPTH, D)),
        'ffn1_post_g': gain((DEPTH, D)),
        'ffn1_w_gate': nrm((DEPTH, D, F), D ** -0.5),
        'ffn1_w_up': nrm((DEPTH, D, F), D ** -0.5),
        'ffn1_w_down': nrm((DEPTH, F, D), F ** -0.5),
        'mix_pre_g': gain((DEPTH, D)),
        'mix_post_g': gain((DEPTH, D)),
        'w_in': nrm((DEPTH, D, IN_COLS), D ** -0.5),
        'w_out': nrm((DEPTH, MIX_WIDTH, D), MIX_WIDTH ** -0.5),
        'a_conv_w': nrm((DEPTH, A_CONV, G), A_CONV ** -0.5),
        'b_conv_w': nrm((DEPTH, B_CONV, G), B_CONV ** -0.5),
        'b_conv_b': nrm((DEPTH, G), 0.02),
        'b_ln_g': gain((DEPTH, G)),
        'b_ln_b': nrm((DEPTH, G), 0.02),
        'c_mu': unif((DEPTH, C_COLS), 0.0, 1.0),
        'c_w0': unif((DEPTH, G), -6.0, 0.0),
        'c_w2': nrm((DEPTH, C_DECAY_LORA, G), 0.1),
        'c_a0': nrm((DEPTH, G), 0.1),
        'c_a2': nrm((DEPTH, C_A_LORA, G), 0.1),
        'c_g2': nrm((DEPTH, C_G_LORA, G), C_G_LORA ** -0.5),
        'c_v0': nrm((DEPTH - 1, G), 0.1),
        'c_v1': nrm((DEPTH - 1, G, C_V_LORA), G ** -0.5),
        'c_v2': nrm((DEPTH - 1, C_V_LORA, G), 0.1),
        'c_k_k': 0.85 + nrm((DEPTH, G), 0.05),
        'c_k_a': 1.0 + nrm((DEPTH, G), 0.05),
        'c_r_k': nrm((DEPTH, C_HEADS, C_HEAD), 0.1),
        'c_ln_g': gain((DEPTH, G)),
        'c_ln_b': nrm((DEPTH, G), 0.02),
        'd_w': nrm((DEPTH, POOL_GROUPS, POOL_GW, POOL_GW), POOL_GW ** -0.5),
        'd_scale': 1.0 + nrm((DEPTH, G), 0.1),
        'ffn2_pre_g': gain((DEPTH, D)),
        'ffn2_post_g': gain((DEPTH, D)),
        'ffn2_w_gate': nrm((DEPTH, D, F), D ** -0.5),
        'ffn2_w_up': nrm((DEPTH, D, F), D ** -0.5),
        'ffn2_w_down': nrm((DEPTH, F, D), F ** -0.5),
    }

def reference(x_prompt, x_sample, state_conv_a, state_conv_b, state_shift_c, state_wkv_c, state_pool_d,
              ffn1_pre_g, ffn1_post_g, ffn1_w_gate, ffn1_w_up, ffn1_w_down,
              mix_pre_g, mix_post_g, w_in, w_out, a_conv_w, b_conv_w, b_conv_b, b_ln_g, b_ln_b,
              c_mu, c_w0, c_w2, c_a0, c_a2, c_g2, c_v0, c_v1, c_v2, c_k_k, c_k_a, c_r_k, c_ln_g, c_ln_b,
              d_w, d_scale, ffn2_pre_g, ffn2_post_g, ffn2_w_gate, ffn2_w_up, ffn2_w_down):
    W = dict(ffn1_pre_g=ffn1_pre_g, ffn1_post_g=ffn1_post_g, ffn1_w_gate=ffn1_w_gate,
             ffn1_w_up=ffn1_w_up, ffn1_w_down=ffn1_w_down, mix_pre_g=mix_pre_g, mix_post_g=mix_post_g,
             w_in=w_in, w_out=w_out, a_conv_w=a_conv_w, b_conv_w=b_conv_w, b_conv_b=b_conv_b,
             b_ln_g=b_ln_g, b_ln_b=b_ln_b, c_mu=c_mu, c_w0=c_w0, c_w2=c_w2, c_a0=c_a0, c_a2=c_a2,
             c_g2=c_g2, c_v0=c_v0, c_v1=c_v1, c_v2=c_v2, c_k_k=c_k_k, c_k_a=c_k_a, c_r_k=c_r_k,
             c_ln_g=c_ln_g, c_ln_b=c_ln_b, d_w=d_w, d_scale=d_scale, ffn2_pre_g=ffn2_pre_g,
             ffn2_post_g=ffn2_post_g, ffn2_w_gate=ffn2_w_gate, ffn2_w_up=ffn2_w_up, ffn2_w_down=ffn2_w_down)
    Bp = x_prompt.shape[0]
    dt = x_prompt.dtype
    p_states = (jnp.zeros((DEPTH, Bp, A_CONV - 1, GROUP_W), dt),
                jnp.zeros((DEPTH, Bp, B_CONV - 1, GROUP_W), dt),
                jnp.zeros((DEPTH, Bp, C_COLS), dt),
                jnp.zeros((DEPTH, Bp, C_HEADS, C_HEAD, C_HEAD), state_wkv_c.dtype),
                jnp.zeros((DEPTH, Bp, POOL_BUF, GROUP_W), dt))
    y_prompt, p_new = run_trunk(x_prompt, p_states, W, 0)
    s_states = (state_conv_a, state_conv_b, state_shift_c, state_wkv_c, state_pool_d)
    y_sample, s_new = run_trunk(x_sample, s_states, W, PAST_LEN)
    new_conv_a_p, new_conv_b_p, new_shift_c_p, new_wkv_c_p, new_pool_d_p = p_new
    new_conv_a_s, new_conv_b_s, new_shift_c_s, new_wkv_c_s, new_pool_d_s = s_new
    return (y_prompt, y_sample,
            new_conv_a_p, new_conv_b_p, new_shift_c_p, new_wkv_c_p, new_pool_d_p,
            new_conv_a_s, new_conv_b_s, new_shift_c_s, new_wkv_c_s, new_pool_d_s)


_drawn_inputs = setup_inputs


def setup_inputs(seed=0):
    import zlib

    import numpy as np

    out = dict(_drawn_inputs(seed))
    spreads = {}
    factors = {'b_conv_b': 4.788,
     'b_ln_g': 3.538,
     'b_ln_b': 21.526,
     'c_ln_g': 5.127,
     'c_ln_b': 27.356,
     'ffn2_post_g': 3.645,
     'd_scale': 2.769}
    for name, (base, spread) in spreads.items():
        noise = np.random.default_rng([zlib.crc32(name.encode()), seed]).standard_normal(out[name].shape)
        drawn = base * np.exp(spread * noise) if base else spread * noise
        out[name] = __import__('jax').numpy.asarray(drawn.astype(out[name].dtype))
    for name, factor in factors.items():
        out[name] = (out[name] * factor).astype(out[name].dtype)
    return out
```

```python
import numpy as np
from contextlib import ExitStack

import concourse.bass as bass
from concourse import mybir

F32 = mybir.dt.float32
F32R = mybir.dt.float32r
ALU = mybir.AluOpType
ACT = mybir.ActivationFunctionType
MUL, ADD, SUB = ALU.mult, ALU.add, ALU.subtract

P = 128
D = 1024
KD = D // P
NP_, NB, NT = 512, 8, 4
NS = NB * NT
N = NP_ + NS
H = N // 2
HP = NP_ - H
F = 2816
FT = F // P
GROUPS = ((0, 8), (8, 8), (16, 6))
G = 256
C = 64
NC_ = NP_ // C
LEVELS = (1, 2, 4, 8, 16, 32)
CD = float(np.exp(-0.5))
POOLW = (2, 4, 8, 16)
CONVB = 31

LORA, K0, K1, R0, R1, V0, V1, BV0, BV1, BG0, BG1, AC0, AC1, AH0, AH1, AB0, AB1, DD0, DD1 = range(19)
IN_TILES = (16, 12, 13, 10, 11, 14, 15, 6, 7, 8, 9, 4, 5, 0, 1, 2, 3, 17, 18)
NIN = len(IN_TILES)
C_TILE = (6, 2, 3, 0, 1, 4, 5)

PCOL = {}
_n = 0
for _name, _k in (("g0", 8), ("g1", 8), ("g2", 8), ("g3", 8), ("g4", 8), ("g5", 8), ("mu", 7), ("w0", 2), ("a0", 2),
                  ("kk", 2), ("ka", 2), ("rk", 2), ("cg", 2), ("cb", 2), ("bb", 2), ("bg", 2), ("bn", 2),
                  ("ds", 2), ("aw", 6), ("bw", 62)):
    PCOL[_name] = _n
    _n += _k
NPAR = _n
CCOL = {}
_n = 0
for _name, _k in (("ident", P), ("ones", P), ("hb", P), ("mask", 2 * P), ("lev", 6 * P), ("scan", N), ("cnt", 32),
                  ("wcol", 2), ("eps", 3), ("smask", 64), ("bsel", 8), ("idc", 64)):
    CCOL[_name] = _n
    _n += _k
NCON = _n
LORAW = 256
SCOL = {}
_n = 0
for _name, _k in (("shift", 7 * NB), ("u", 2 * NB * 2), ("z", 2 * NB * 30), ("d", 2 * NB * 15)):
    SCOL[_name] = _n
    _n += _k
NSTA = _n


def constants():
    c = np.zeros((P, NCON), np.float32)
    s, t = np.arange(P)[:, None], np.arange(P)[None, :]
    c[:, CCOL["ident"]:][:, :P] = s == t
    c[:, CCOL["ones"]:][:, :P] = 1
    c[:, CCOL["hb"]:][:, :P] = s // C == t // C
    c[:, CCOL["mask"]:][:, :P] = (s // C == t // C) & (s < t)
    c[:, CCOL["mask"] + P:][:, :P] = (s // C == t // C) & (s <= t)
    for n, b in enumerate(LEVELS):
        c[:, CCOL["lev"] + n * P:][:, :P] = (s // (2 * b) == t // (2 * b)) & (s // b != t // b) & (s < t)
    col = np.arange(N)
    start = np.where(col < NP_, col % C == 0, (col - NP_) % NT == 0)
    c[:, CCOL["scan"]:][:, :N] = 1 - start
    w = np.array(POOLW, np.float32)[(np.arange(2)[:, None] * P + np.arange(P)[None, :]) // 64]
    c[:, CCOL["wcol"]:][:, :2] = (1 / w).T
    for i in range(2):
        c[:, CCOL["cnt"] + 16 * i:][:, :16] = 1 / np.minimum(np.arange(16)[None, :] + 1, w[i][:, None])
    c[:, CCOL["eps"]:][:, :3] = (1e-6, 1e-5, 64e-5)
    c[:, CCOL["idc"]:][:, :C] = s % C == t[:, :C]
    s, t = s[:32], t[:, :32]
    c[:32, CCOL["smask"]:][:, :32] = (s // NT == t // NT) & (s < t)
    c[:32, CCOL["smask"] + 32:][:, :32] = (s // NT == t // NT) & (s <= t)
    c[:32, CCOL["bsel"]:][:, :8] = s // NT == np.arange(8)[None, :]
    return c


def program(nc, a, o):
    with ExitStack() as ctx:
        sems = {}

        def S(name):
            if name not in sems:
                sems[name] = ctx.enter_context(nc.semaphore(name))
            return sems[name]

        def sb(name, shape, dt=F32):
            return ctx.enter_context(nc.sbuf_tensor(name, [P] + shape, dt))

        x = sb("x", [KD, N])
        xh, xl = sb("xh", [KD, N], F32R), sb("xl", [KD, N], F32R)
        RAW, SPL = 2, 4
        raw = sb("raw", [RAW, KD, P])
        wh, wl = sb("wh", [SPL, KD, P], F32R), sb("wl", [SPL, KD, P], F32R)
        con = sb("con", [NCON])
        par = sb("par", [NPAR])
        lora_w = sb("lora_w", [LORAW])
        dwbd = sb("dwbd", [2, P])
        onemka = sb("onemka", [2])
        st = sb("st", [3, 24])
        ARENA = nc.sbuf_base + 31 & ~31
        END = nc.sbuf_usable_end
        spots = {"ffn": ARENA, "mix": ARENA}

        def at(space, name, shape, dt=F32, offset=None):
            size = 4 * int(np.prod(shape))
            off = spots[space] if offset is None else offset
            if offset is None:
                spots[space] += size + 31 & ~31
            assert off + size <= END, (name, off + size, END)
            return nc.alloc_sbuf_tensor_at(name, [P] + shape, dt, offset=off)

        f = at("ffn", "f", [KD, N])
        hh, hl = at("ffn", "hh", [8, N], F32R), at("ffn", "hl", [8, N], F32R)
        silu = at("ffn", "silu", [2, N])
        h32 = at("ffn", "h32", [2, N])
        sq = at("ffn", "sq", [2, N])
        ssq = at("ffn", "ssq", [N])
        rb = at("ffn", "rb", [N])
        tb = at("ffn", "tb", [2, N])
        mixf = at("mix", "mixf", [KD, N])
        ar = at("mix", "ar", [2, 2, N])
        bt = at("mix", "bt", [2, N])
        kt = at("mix", "kt", [2, N])
        bh = at("mix", "bh", [2, N])
        kh = at("mix", "kh", [2, N])
        v = at("mix", "v", [2, N])
        gg = at("mix", "gg", [2, N])
        bo = at("mix", "bo", [2, N])
        pend = at("mix", "pend", [2, 16])
        ya, yb, yd = mixf[:, 0:2, :], mixf[:, 2:4, :], mixf[:, 6:8, :]
        tmp2 = mixf[:, 4:6, :]
        W0 = spots["mix"]
        pc = at("mix", "pc", [7, 513 + 5 * NB])
        lo = at("mix", "lo", [N])
        lo2 = at("mix", "lo2", [N])
        kp = at("mix", "kp", [2, N])
        ll = at("mix", "ll", [2, N])
        ub = at("mix", "ub", [2, 514 + 6 * NB])
        zb = at("mix", "zb", [2, 542 + 34 * NB])
        DW = 527 + 19 * NB
        db = at("mix", "db", [2, DW], offset=W0)
        d1 = at("mix", "d1", [2, DW], offset=W0 + (8 * DW + 31 & ~31))
        d2 = at("mix", "d2", [2, DW], offset=W0 + 2 * (8 * DW + 31 & ~31))
        assert W0 + 3 * (8 * DW + 31 & ~31) <= W0 + 4 * 7 * (513 + 5 * NB) + 8 * N
        stap = at("mix", "stap", [NSTA])
        so = at("mix", "so", [64])
        spots["wkv"] = W0
        rhs = at("wkv", "rhs", [2, 2, P])
        bkv = at("wkv", "bkv", [2, 5, P])
        nak = at("wkv", "nak", [2, 2, 2, 2, P])
        nrb, akr = nak[:, :, :, 0], nak[:, :, :, 1]
        nlv = at("wkv", "nlv", [2, 2, 2, P])
        tt_ = at("wkv", "tt", [2, 2, 2, P])
        xx = at("wkv", "xx", [2, 2, P])
        tu = at("wkv", "tu", [2, 2, P])
        qt = at("wkv", "qt", [2, P])
        mt = at("wkv", "mt", [2, 2, C])
        sst = at("wkv", "sst", [2, NC_, C])
        s0t = at("wkv", "s0t", [2, NB, C])
        s1t = at("wkv", "s1t", [2, NB, C])
        smt = at("wkv", "smt", [2, NB, C])
        ex3 = (tmp2[:, 0, 0:NB * C], tmp2[:, 1, 0:NB * C], nlv[:, 0].rearrange("p a b c -> p (a b c)"))

        ps = ctx.enter_context(nc.psum_tensor("ps", [P, 8, 512], F32))

        def pair(n):
            return ps[:, 2 * n:2 * n + 2, 0:H]

        def C_(name, n=P, k=0, rows=P):
            return con[0:rows, CCOL[name] + k:CCOL[name] + k + n]

        def par_(name, k):
            return par[:, PCOL[name] + k:PCOL[name] + k + 1]

        ident, ones, hb = C_("ident"), C_("ones"), C_("hb")
        hsel = hb.rearrange("p (h c) -> p h c", h=2)[:, :, 0]

        def halves(t):
            return t.rearrange("p (a b) -> p a b", a=2)

        block = ctx.enter_context(nc.Block())

        FFN_UNITS = sum(2 * nf + KD for _, nf in GROUPS)
        MIX0 = FFN_UNITS
        FFN2 = MIX0 + NIN + KD + 1
        assert FFN_UNITS % 4 == 0 and FFN2 % 4 == 0
        SKIP = FFN2 - 1

        def load(sp, u0, i, s, src, k):
            sp.wait_ge(S("w_lo"), i * 4 + (u0 + s + 1))
            sp.dma_start(raw[:, s % RAW, 0:k, :].rearrange("p k n -> p (k n)"), src).then_inc(S(f"w_full{s % RAW}"), 16)

        def split_hi(act, u0, i, s, k, skip=0):
            loads = (u0 + s) // RAW + 1 - (SKIP % RAW == s % RAW and u0 + s > SKIP)
            act.wait_ge(S(f"w_full{s % RAW}"), i * 32 + 16 * loads)
            act.wait_ge(S("unit_done"), i * 4 + (u0 + s + 1))
            act.activation(wh[:, s % 4, 0:k, :], raw[:, s % RAW, 0:k, :], ACT.Copy
                           ).then_inc(S("w_hi"), 1 + skip)

        def split_lo(dve, u0, i, s, k, skip=0):
            dve.wait_ge(S("w_hi"), i * 4 + (u0 + s + 1))
            dve.tensor_tensor(wl[:, s % 4, 0:k, :], raw[:, s % RAW, 0:k, :], wh[:, s % 4, 0:k, :].bitcast(F32), SUB
                              ).then_inc(S("w_lo"), 1 + skip)

        def split_ready(pe, u0, i, s):
            pe.wait_ge(S("w_lo"), i * 4 + (u0 + s + 1 + RAW))

        def unit_done(eng, u0, i, s):
            eng.wait_ge(S("unit_done"), i * 4 + (u0 + s + 1 + SPL))

        def product(pe, out, s, k, right_h, right_l, before=None):
            for j in range(k):
                if before:
                    before(j)
                for n in range(2):
                    col = slice(n * H, n * H + H)
                    pe.matmul(out[:, n], wh[:, s, j], right_h[:, j, col], start=j == 0, stop=False)
                    pe.matmul(out[:, n], wh[:, s, j], right_l[:, j, col], start=False, stop=False)
                    last = pe.matmul(out[:, n], wl[:, s, j], right_h[:, j, col], start=False, stop=j == k - 1)
            return last

        def tok(t):
            return slice(128 * t, 128 * t + 128) if t < 4 else slice(N - 128, N)

        def stats_pe(pe, n):
            pe.wait_ge(S("n_ssq"), n + 1)
            for t in range(5):
                m = pe.matmul(ps[:, 6, t:t + 1], ssq[:, tok(t)], ones[:, 0:1], start=True, stop=True)
            m.then_inc(S("n_sum"), 1)
            pe.wait_ge(S("n_rec"), n + 1)
            for t in range(4):
                pe.matmul(ps[:, 7, tok(t)], st[:, 2, t:t + 1].to_broadcast([P, P]), ident, start=True, stop=True)
            pe.matmul(ps[:, 6, 0:NS], st[:, 2, 4:5].to_broadcast([P, P]), ident[:, P - NS:P],
                      start=True, stop=True).then_inc(S("n_spread"), 1)

        def stats_act(act, n):
            act.wait_ge(S("n_sum"), n + 1)
            act.activation(st[:, 1, 0:5], ps[:, 6, 0:5], ACT.Sqrt, scale=1.0 / D, bias=C_("eps", 1)
                           ).then_inc(S("n_root"), 1)
            act.wait_ge(S("n_spread"), n + 1)
            scale = 0.5 if n in (1, 5) else 1.0
            act.activation(rb[:, 0:512], ps[:, 7, 0:512], ACT.Copy, scale=scale)
            act.activation(rb[:, 512:N], ps[:, 6, 0:NS], ACT.Copy, scale=scale).then_inc(S("n_rb"), 1)

        def stats_dve(dve, n):
            dve.wait_ge(S("n_root"), n + 1)
            dve.reciprocal(st[:, 2, 0:5], st[:, 1, 0:5]).then_inc(S("n_rec"), 1)

        def squares_act(act, n, k, src):
            if k == 0:
                act.activation(ssq[:], src, ACT.Square).then_inc(S("n_sq"), 1)
            else:
                act.wait_ge(S("n_add"), 6 * n + max(k - 2, 0))
                act.activation(sq[:, k % 2], src, ACT.Square).then_inc(S("n_sq"), 1)

        def squares_dve(dve, n, k):
            dve.wait_ge(S("n_sq"), 8 * n + k + 1)
            dve.wait_ge(S("n_add"), 6 * n + k - 1)
            dve.tensor_tensor(ssq[:], ssq[:], sq[:, k % 2], ADD).then_inc(S("n_ssq" if k == KD - 1 else "n_add"), 1)

        def pre_act(act, n):
            b = KD * (n // 2)
            for k in range(KD):
                if n == 0:
                    act.wait_ge(S("in_x"), 16)
                else:
                    act.wait_ge(S("x_ready"), b - KD + k + 1)
                squares_act(act, n, k, x[:, k])
            stats_act(act, n)
            for k in range(KD):
                act.wait_ge(S("n_u"), b + k + 1)
                act.activation(xh[:, k], tb[:, k % 2], ACT.Copy).then_inc(S("n_xh"), 1)

        def pre_dve(dve, n):
            b = KD * (n // 2)
            for k in range(1, KD):
                squares_dve(dve, n, k)
            stats_dve(dve, n)
            dve.wait_ge(S("n_rb"), n + 1)
            for k in range(KD + 1):
                if k < KD:
                    if k >= 2:
                        dve.wait_ge(S("n_xl"), b + k - 1)
                    dve.scalar_tensor_tensor(tb[:, k % 2], x[:, k], par_(f"g{n}", k), rb[:], MUL, MUL
                                             ).then_inc(S("n_u"), 1)
                if k >= 1:
                    dve.wait_ge(S("n_xh"), b + k)
                    dve.tensor_tensor(xl[:, k - 1], tb[:, (k - 1) % 2], xh[:, k - 1].bitcast(F32), SUB
                                      ).then_inc(S("n_xl"), 1)

        def post_dve(dve, n):
            b = KD * (n // 2)
            stats_dve(dve, n)
            dve.wait_ge(S("n_rb"), n + 1)
            for k in range(KD + 1):
                if k < KD:
                    if k >= 2:
                        dve.wait_ge(S("x_ready"), b + k - 1)
                    dve.scalar_tensor_tensor(tb[:, k % 2], f[:, k], par_(f"g{n}", k), rb[:], MUL, MUL
                                             ).then_inc(S("n_t"), 1)
                if k >= 1:
                    dve.wait_ge(S("n_t"), b + k)
                    dve.tensor_tensor(x[:, k - 1], x[:, k - 1], tb[:, (k - 1) % 2], ADD).then_inc(S("x_ready"), 1)

        def ffn_sp(sp, q, u0):
            u = u0
            for g, (f0, nf) in enumerate(GROUPS):
                with sp.Fori(0, nf // 2) as i:
                    for s in range(4):
                        load(sp, u, i, s, a[f"w_gu{q}"][bass.ds(i * 4 + (2 * f0 + s), 1)].rearrange("a p n -> p (a n)"), KD)
                u += 2 * nf
                with sp.Fori(0, 2) as i:
                    for s in range(4):
                        load(sp, u, i, s, a[f"w_d{q}_{g}"][bass.ds(i * 4 + s, 1)].rearrange("a p n -> p (a n)"), nf)
                u += KD

        def ffn_pe(pe, q, u0, n):
            u, dn = u0, 0
            pe.wait_ge(S("n_xl"), KD * (n // 2 + 1))
            for g, (f0, nf) in enumerate(GROUPS):
                with pe.Fori(0, nf // 2) as i:
                    for s in range(4):
                        split_ready(pe, u, i, s)
                        pe.wait_ge(S(f"h_mul{q}"), i * 2 + (f0 + s // 2 + 1))
                        pe.wait_ge(S(f"d_out{q}"), dn + s + 1)
                        product(pe, pair(s), s, KD, xh, xl).then_inc(S("unit_done"), 1)
                u += 2 * nf

                def hidden_ready(j):
                    pe.wait_ge(S(f"h_lo{q}"), f0 + j + 1 + 2)

                with pe.Fori(0, 2) as i:
                    for s in range(4):
                        split_ready(pe, u, i, s)
                        pe.wait_ge(S(f"h_mul{q}"), f0 + nf + 2 - (s < 2))
                        pe.wait_ge(S(f"d_out{q}"), i * 4 + (dn + s + 1))
                        product(pe, pair(s), s, nf, hh, hl, hidden_ready if s == 0 else None
                                ).then_inc(S("unit_done"), 1)
                u += KD
                dn += KD

        def silu_act(act, q, u, i, f0, s):
            unit_done(act, u, i, 2 * s)
            act.wait_ge(S(f"h_mul{q}"), i * 2 + (f0 + s + 1))
            act.activation(halves(silu[:, s % 2]), pair(2 * (s % 2)), ACT.Silu).then_inc(S(f"silu{q}"), 1)

        def hidden_dve(dve, q, u, i, f0, s):
            unit_done(dve, u, i, 2 * s + 1)
            dve.wait_ge(S(f"silu{q}"), i * 2 + (f0 + s + 1))
            dve.wait_ge(S(f"h_lo{q}"), i * 2 + (f0 + s + 1))
            dve.tensor_tensor(halves(h32[:, s % 2]), halves(silu[:, s % 2]), pair(2 * (s % 2) + 1), MUL
                              ).then_inc(S(f"h_mul{q}"), 1)
            dve.wait_ge(S(f"h_mul{q}"), i * 2 + (f0 + s + 1 + 2))
            j = bass.ds(i * 2 + s, 1) if not isinstance(i, int) else slice(s, s + 1)
            one = "p a n -> p (a n)"
            dve.tensor_copy(hh[:, j].rearrange(one), h32[:, s % 2]).then_inc(S(f"h_hi{q}"), 1)
            dve.wait_ge(S(f"h_hi{q}"), i * 2 + (f0 + s + 1))
            dve.tensor_tensor(hl[:, j].rearrange(one), h32[:, s % 2], hh[:, j].rearrange(one).bitcast(F32), SUB
                              ).then_inc(S(f"h_lo{q}"), 1)

        def down_dve(dve, q, u, g, d, n):
            unit_done(dve, u, 0, d)
            if g == 0:
                dve.tensor_copy(halves(f[:, d]), pair(d % 4)).then_inc(S(f"d_out{q}"), 1)
            else:
                dve.wait_ge(S(f"d_out{q}"), 4 + KD * (g - 1) + d + 1)
                dve.tensor_tensor(halves(f[:, d]), pair(d % 4), halves(f[:, d]), ADD).then_inc(S(f"d_out{q}"), 1)
            if g == 2 and d >= 2:
                squares_dve(dve, n, d - 1)

        def down_act(act, q, g, d, n):
            if g == 2:
                act.wait_ge(S(f"d_out{q}"), 4 + 2 * KD + d + 1)
                squares_act(act, n, d, f[:, d])

        def ffn_act(act, q, u0, n, nxt, nk):
            u = u0
            for g, (f0, nf) in enumerate(GROUPS):
                for s in range(4):
                    if not (g == 0 and s < 2):
                        split_hi(act, u, 0, s, KD)
                silu_act(act, q, u, 0, f0, 0)
                with act.Fori(0, nf // 2 - 1) as i:
                    for s in range(4):
                        split_hi(act, u + 4, i, s, KD)
                        if s % 2:
                            silu_act(act, q, u, i, f0, 1 + s // 2)
                u += 2 * nf
                for s in range(KD):
                    split_hi(act, u, 0, s, nf)
                    if s == 1:
                        silu_act(act, q, u - 2 * nf, 0, f0, nf - 1)
                    if s >= 2:
                        down_act(act, q, g, s - 2, n)
                u += KD
                if g == 2:
                    for s in range(2):
                        if nxt is not None:
                            split_hi(act, nxt, 0, s, nk)
                        down_act(act, q, g, KD - 2 + s, n)

        def ffn_dve(dve, q, u0, n, nxt, nk):
            u = u0
            for g, (f0, nf) in enumerate(GROUPS):
                for s in range(4):
                    if not (g == 0 and s < 2):
                        split_lo(dve, u, 0, s, KD)
                    if g and s < 2:
                        down_dve(dve, q, u - KD, g - 1, KD - 2 + s, n)
                hidden_dve(dve, q, u, 0, f0, 0)
                with dve.Fori(0, nf // 2 - 1) as i:
                    for s in range(4):
                        split_lo(dve, u + 4, i, s, KD)
                        if s % 2:
                            hidden_dve(dve, q, u, i, f0, 1 + s // 2)
                u += 2 * nf
                for s in range(KD):
                    split_lo(dve, u, 0, s, nf)
                    if s == 1:
                        hidden_dve(dve, q, u - 2 * nf, 0, f0, nf - 1)
                    if s >= 2:
                        down_dve(dve, q, u, g, s - 2, n)
                u += KD
                if g == 2:
                    for s in range(2):
                        if nxt is not None:
                            split_lo(dve, nxt, 0, s, nk)
                        down_dve(dve, q, u - KD, g, KD - 2 + s, n)
                    squares_dve(dve, n, KD - 1)

        BY_DVE = (AH0, AH1, AB0, AB1)
        OUT0 = NIN

        def in_out(eng, m):
            if m in BY_DVE:
                eng.wait_ge(S("in_dve"), BY_DVE.index(m) + 1)
            else:
                eng.wait_ge(S("in_act"), sum(k not in BY_DVE for k in range(m + 1)))

        def steps(t, at_, pad):
            return t[..., at_:at_ + NB * (pad + NT)].rearrange("p (b c) -> p b c", c=pad + NT)[:, :, pad:]

        def comp(t):
            return t.rearrange("p (b c) -> p b c", c=NT)

        def pieces(dst, m, at_, pad):
            src = pair(m % 2)
            return ((dst[:, pad:pad + H], src[:, 0]), (dst[:, pad + H:pad + NP_], src[:, 1, 0:HP]),
                    (steps(dst, at_, pad), comp(src[:, 1, HP:H])))

        class Chain:

            def __init__(self, eng, name):
                self.eng, self.name, self.n = eng, name, 0

            def __call__(self, ins):
                self.n += 1
                ins.then_inc(S(self.name), 1)
                self.eng.wait_ge(S(self.name), self.n)

        def mixer_sp(sp):
            for m in range(NIN):
                load(sp, MIX0, 0, m, a["w_in"][m], KD)
                if m == 3:
                    sp.wait_ge(S("n_xl"), 2 * KD)
                    sp.dma_start(stap[:], a["sta"]).then_inc(S("in_sta"), 16)
            for m in range(4):
                load(sp, MIX0, 0, OUT0 + m, a["w_out"][m], KD)
            sp.wait_ge(S("glu"), 2)
            zs = zb[:, :, 542:].rearrange("p i (b c) -> p i b c", c=34)
            for i in range(2):
                sp.dma_start(o["o_b"][:, i, 0:30], zb[:, i, 512:542]).then_inc(S("out"), 16)
                sp.dma_start(o["o_b"][:, i, 30:].rearrange("p (b c) -> p b c", c=30), zs[:, i, :, 4:]).then_inc(S("out"), 16)
            sp.wait_ge(S("so"), 1)
            sp.dma_start(o["o_shift"], so[:, 0:7 * (1 + NB)].rearrange("p (i c) -> p i c", i=7)).then_inc(S("out"), 16)
            sp.wait_ge(S("au"), 2)
            us = ub[:, :, 514:].rearrange("p i (b c) -> p i b c", c=6)
            for i in range(2):
                sp.dma_start(o["o_a"][:, i, 0:2], ub[:, i, 512:514]).then_inc(S("out"), 16)
                sp.dma_start(o["o_a"][:, i, 2:].rearrange("p (b c) -> p b c", c=2), us[:, i, :, 4:]).then_inc(S("out"), 16)
            in_out(sp, DD1)
            ds_ = db[:, :, 527:].rearrange("p i (b c) -> p i b c", c=19)
            for i in range(2):
                sp.dma_start(o["o_d"][:, i, 0:15], db[:, i, 512:527]).then_inc(S("out"), 16)
                sp.dma_start(o["o_d"][:, i, 15:].rearrange("p (b c) -> p b c", c=15), ds_[:, i, :, 4:]).then_inc(S("out"), 16)
            sp.wait_ge(S("out"), 13 * 16)
            sp.wait_ge(S("diff"), 2)
            sp.dma_start(s0t[:], a["s0"]).then_inc(S("in_s0"), 16)
            for m in range(4, KD):
                load(sp, MIX0, 0, OUT0 + m, a["w_out"][m], KD)
            sp.wait_ge(S("r_end"), 1)
            sp.dma_start(o["o_sp"], sst[:, :, NC_ - 1]).then_inc(S("out"), 16)
            sp.wait_ge(S("q_s1"), 2)
            sp.dma_start(o["o_ss"], s1t[:]).then_inc(S("out"), 16)

        def mixer_pool(pool):
            pool.wait_ge(S("in_sta"), 16)
            z = lambda name, k, c: stap[:, SCOL[name]:SCOL[name] + 2 * NB * c].rearrange("p (i b c) -> p i b c", i=2, c=c)[:, k]
            pool.memset(pc[:, :, 0:1], 0.0)
            pool.tensor_copy(pc[:, :, 513:].rearrange("p i (b c) -> p i b c", c=5)[:, :, :, 0],
                             stap[:, 0:7 * NB].rearrange("p (i b) -> p i b", b=NB)).then_inc(S("pads"), 1)
            pool.memset(ub[:, :, 0:2], 0.0)
            pool.memset(zb[:, :, 0:30], 0.0)
            for i in range(2):
                pool.tensor_copy(ub[:, i, 514:].rearrange("p (b c) -> p b c", c=6)[:, :, 0:2], z("u", i, 2))
                last = pool.tensor_copy(zb[:, i, 542:].rearrange("p (b c) -> p b c", c=34)[:, :, 0:30], z("z", i, 30))
            last.then_inc(S("pads"), 1)
            in_out(pool, V1)
            s3 = so[:, 0:7 * (1 + NB)].rearrange("p (i c) -> p i c", i=7)
            pool.tensor_copy(s3[:, :, 0:1], pc[:, :, 512:513])
            pool.tensor_copy(s3[:, :, 1:], pc[:, :, 513:].rearrange("p i (b c) -> p i b c", c=5)[:, :, :, 4]).then_inc(S("so"), 1)
            pool.wait_ge(S("xm"), 7)
            pool.wait_ge(S("so"), 1)
            pool.memset(db[:, :, 0:15], 0.0)
            for i in range(2):
                last = pool.tensor_copy(db[:, i, 527:].rearrange("p (b c) -> p b c", c=19)[:, :, 0:15], z("d", i, 15))
            last.then_inc(S("pads"), 1)
            in_out(pool, DD1)
            pool.wait_ge(S("lora"), 6)
            pool.wait_ge(S("pads"), 3)
            pool.tensor_tensor(d1[:, :, 1:], db[:, :, 1:], db[:, :, :-1], ADD).then_inc(S("pool_d"), 1)
            pool.wait_ge(S("pool_d"), 1)
            pool.tensor_tensor(d2[:, :, 3:], d1[:, :, 3:], d1[:, :, 1:-2], ADD).then_inc(S("pool_d"), 1)
            pool.wait_ge(S("pool_d"), 2)
            pool.tensor_tensor(d1[:, 1, 7:], d2[:, 1, 7:], d2[:, 1, 3:-4], ADD).then_inc(S("pool_d"), 1)
            pool.wait_ge(S("pool_d"), 3)
            pool.tensor_tensor(d2[64:P, 1, 15:], d1[64:P, 1, 15:], d1[64:P, 1, 7:-8], ADD).then_inc(S("pool_d"), 1)
            for t in range(4):
                for l in range(6):
                    for p in range(2):
                        pool.wait_ge(S("r2"), 2 * t + p + 1)
                        if l >= 2:
                            wait_job(pool, t, 2 * l, p)
                        elif t:
                            wait_job(pool, t - 1, 10 + 2 * l, p)
                        pool.tensor_tensor(nlv[:, l % 2, p], nrb[:, p, :, 0],
                                           C_("lev", k=l * P).unsqueeze(1).to_broadcast([P, 2, P]), MUL
                                           ).then_inc(S("lev"), 1)
            for l in range(2):
                for p in range(2):
                    pool.wait_ge(S("q2"), p + 1)
                    wait_job(pool, 3, 10 + 2 * l, p)
                    pool.tensor_tensor(nlv[0:32, l, p, :, 0:32], nrb[0:32, p, :, 0, 0:32],
                                       C_("lev", 32, l * P, 32).unsqueeze(1).to_broadcast([32, 2, 32]), MUL
                                       ).then_inc(S("lev"), 1)

        NSTAGE = 20

        def wait_job(eng, t, s, p):
            eng.wait_ge(S("job"), (t * NSTAGE + s) * 2 + p + 1)

        def bank(s, p):
            return ps[:, (2 * s + p) % 8]

        def bank_free(pe, t, s, p):
            if s >= 4:
                pe.wait_ge(S(f"r{s - 4}"), 2 * t + p + 1)
            elif t:
                pe.wait_ge(S(f"r{NSTAGE + s - 4}"), 2 * (t - 1) + p + 1)

        def wkv_pe(pe, t):
            tok_ = slice(P * t, P * t + P)
            hp = [slice(0, 64), slice(64, P)]

            def job(s, p):
                bank_free(pe, t, s, p)
                return bank(s, p)

            for p in range(2):
                b = job(0, p)
                for k, src in enumerate((v[:, p], bh[:, p], kh[:, p], ar[:, p, 0])):
                    last = pe.transpose(b[:, P * k:P * k + P], src[:, tok_], ident)
                last.then_inc(S("job"), 1)
            for h in range(2):
                for p in range(2):
                    b = job(1 + h, p)
                    for k, left in enumerate((bt, kt)):
                        last = pe.matmul(b[:, 256 * k:256 * k + 256].rearrange("p (a b) -> p a b", a=2), left[hp[h], p, tok_],
                                         ar[hp[h], p, :, tok_], start=True, stop=True)
                    last.then_inc(S("job"), 1)
            for p in range(2):
                b = job(3, p)
                pe.wait_ge(S("lev"), t * 12 + p + 1)
                for h in range(2):
                    last = pe.matmul(b[:, P * h:P * h + P], nlv[:, 0, p, h], ident, start=True, stop=True)
                last.then_inc(S("job"), 1)
            for l in range(1, 6):
                for p in range(2):
                    b = job(2 + 2 * l, p)
                    pe.wait_ge(S("lev"), t * 12 + 2 * l + p + 1)
                    pe.wait_ge(S(f"r{1 + 2 * l}"), 2 * t + p + 1)
                    for h in range(2):
                        last = pe.matmul(b[:, P * h:P * h + P], nlv[:, l % 2, p, h], tt_[:, p, 0, h], start=True, stop=True)
                    last.then_inc(S("job"), 1)
                for p in range(2):
                    b = job(3 + 2 * l, p)
                    pe.wait_ge(S(f"r{2 + 2 * l}"), 2 * t + p + 1)
                    for h in range(2):
                        if l < 5:
                            pe.matmul(b[:, P * h:P * h + P], tt_[:, p, 1, h], xx[:, p, h], start=True, stop=True)
                        last = pe.matmul(b[:, 256 + P * h:256 + P * h + P], xx[:, p, h], tt_[:, p, 1, h], start=True, stop=True)
                    last.then_inc(S("job"), 1)
            for p in range(2):
                b = job(14, p)
                pe.wait_ge(S("r2"), 2 * t + p + 1)
                pe.wait_ge(S("r0"), 2 * t + p + 1)
                for h in range(2):
                    last = pe.matmul(b[:, C * h:C * h + C], akr[:, p, h, 0], bkv[:, p, 0, C * h:C * h + C], start=True, stop=True)
                last.then_inc(S("job"), 1)
            for p in range(2):
                b = job(15, p)
                pe.wait_ge(S("r13"), 2 * t + p + 1)
                pe.wait_ge(S("r14"), 2 * t + p + 1)
                for h in range(2):
                    last = pe.matmul(b[:, P * h:P * h + P], tt_[:, p, 1, h], rhs[:, p, h], start=True, stop=True)
                last.then_inc(S("job"), 1)
            for p in range(2):
                b = job(16, p)
                pe.wait_ge(S("r15"), 2 * t + p + 1)
                for h in range(2):
                    last = pe.matmul(b[hp[h], 0:P], tu[:, p, h, 0:C], nrb[:, p, h, 1], start=True, stop=True)
                for h in range(2):
                    last = pe.matmul(b[hp[h], P:2 * P].rearrange("p (c n) -> p c n", c=2), tu[:, p, h, 0:C],
                                     bkv[:, p, 1:5, C * h:C * h + C].rearrange("p (c k) n -> p c k n", c=2)[:, :, 0],
                                     start=True, stop=True)
                last.then_inc(S("job"), 1)
            for c in range(2):
                ch = 2 * t + c
                for p in range(2):
                    b = job(17 + c, p)
                    for h in range(2):
                        out = b[hp[h], 0:C]
                        pe.matmul(out, bkv[:, p, 1 + 2 * c, C * h:C * h + C], tu[:, p, h, C:P], start=True, stop=False)
                        last = pe.matmul(out, bkv[:, p, 2 + 2 * c, C * h:C * h + C], bkv[:, p, 0, C * h:C * h + C],
                                         start=False, stop=ch == 0)
                        if ch:
                            if h == 0:
                                pe.wait_ge(S("r16"), 2 * t + p + 1)
                                wait_state(pe, ch - 1, p)
                            last = pe.matmul(out, mt[hp[h], p, c], sst[hp[h], p, ch - 1], start=False, stop=True)
                    last.then_inc(S("job"), 1)
            for p in range(2):
                b = job(19, p)
                pe.wait_ge(S("r16"), 2 * t + p + 1)
                for h in range(2):
                    out = b[hp[h], 0:P]
                    pe.matmul(out, tu[:, p, h, C:P], nrb[:, p, h, 1], start=True, stop=False)
                    last = pe.matmul(out, bkv[:, p, 0, C * h:C * h + C], akr[:, p, h, 1], start=False, stop=False)
                    for c in range(2):
                        ch = 2 * t + c
                        if ch:
                            wait_state(pe, ch - 1, p)
                            cols = slice(C * c, C * c + C)
                            last = pe.matmul(b[hp[h], cols], sst[hp[h], p, ch - 1], qt[hp[h], p, cols], start=False, stop=c == 1)
                last.then_inc(S("job"), 1)

        def wait_state(pe, ch, p):
            pe.wait_ge(S(f"r{17 + ch % 2}"), 2 * (ch // 2) + p + 1)

        def wkv_act(act, t):
            def done(s, p):
                wait_job(act, t, s, p)
                return bank(s, p)

            for p in range(2):
                b = done(0, p)
                if t:
                    wait_job(act, t - 1, 19, p)
                act.activation(bkv[:, p, 0], b[:, 0:P], ACT.Copy)
                for c in range(2):
                    act.activation(bkv[:, p, 1 + 2 * c:3 + 2 * c], b[:, P:3 * P].rearrange("p (k c) -> p k c", k=2), ACT.Copy,
                                   scale=hb[:, C * c:C * c + 1])
                act.activation(rhs[:, p, :, 0:C], b[:, 3 * P:].rearrange("p (h c) -> p h c", h=2), ACT.Copy).then_inc(S("r0"), 1)
            for l in range(1, 6):
                for p in range(2):
                    s = 2 + 2 * l
                    b = done(s, p)
                    if l > 1:
                        wait_job(act, t, s - 1, p)
                    elif t:
                        wait_job(act, t - 1, 13, p)
                    act.activation(xx[:, p], b[:, 0:2 * P].rearrange("p (h c) -> p h c", h=2), ACT.Copy).then_inc(S(f"r{s}"), 1)
            for p in range(2):
                b = done(14, p)
                act.activation(rhs[:, p, :, C:P], b[:, 0:P].rearrange("p (h c) -> p h c", h=2), ACT.Copy).then_inc(S("r14"), 1)
            for p in range(2):
                b = done(15, p)
                act.activation(tu[:, p], b[:, 0:2 * P].rearrange("p (h c) -> p h c", h=2), ACT.Copy).then_inc(S("r15"), 1)
            for c in range(2):
                for p in range(2):
                    b = done(17 + c, p)
                    act.activation(sst[:, p, 2 * t + c], b[:, 0:C], ACT.Copy).then_inc(S(f"r{17 + c}"), 1)
            for p in range(2):
                b = done(19, p)
                act.activation(yc[:, p, P * t:P * t + P], b[:, 0:P], ACT.Copy).then_inc(S("r19"), 1)
            if t == 3:
                act.wait_ge(S("r18"), 8)
                act.sem_inc(S("r_end"), 1)

        yc = ar[:, :, 0, :]

        def wkv_dve(dve, t):
            tok_ = slice(P * t, P * t + P)

            def done(s, p):
                wait_job(dve, t, s, p)
                return bank(s, p)

            mask = C_("mask", 2 * P).unsqueeze(1).to_broadcast([P, 2, 2 * P])
            for h in range(2):
                for p in range(2):
                    b = done(1 + h, p)
                    if t:
                        wait_job(dve, t - 1, 19, p)
                        dve.wait_ge(S("lev"), (t - 1) * 12 + 10 + p + 1)
                    dve.tensor_tensor(nak[:, p, h].rearrange("p w k c -> p w (k c)"), b.rearrange("p (w c) -> p w c", w=2), mask, MUL
                                      ).then_inc(S(f"r{1 + h}"), 1)
            for p in range(2):
                b = done(3, p)
                if t:
                    wait_job(dve, t - 1, 15, p)
                idb = ident.unsqueeze(1).to_broadcast([P, 2, P])
                dve.tensor_tensor(tt_[:, p, 1], nlv[:, 0, p], idb, ADD)
                dve.tensor_tensor(tt_[:, p, 0], b[:, 0:2 * P].rearrange("p (h c) -> p h c", h=2), idb, ADD).then_inc(S("r3"), 1)
            for l in range(1, 6):
                for p in range(2):
                    s = 3 + 2 * l
                    b = done(s, p)
                    dve.wait_ge(S(f"r{s - 2}"), 2 * t + p + 1)
                    k = 0 if l < 5 else 1
                    both = tt_[:, p, k:2].rearrange("p k h c -> p (k h c)")
                    dve.tensor_tensor(both, b[:, 256 * k:512], both, ADD).then_inc(S(f"r{s}"), 1)
            for p in range(2):
                b = done(16, p)
                if t:
                    wait_job(dve, t - 1, 19, p)
                dve.tensor_tensor(qt[:, p], b[:, 0:P], ar[:, p, 1, tok_], ADD)
                for c in range(2):
                    ch = 2 * t + c
                    last = dve.scalar_tensor_tensor(mt[:, p, c], C_("idc", C), pend[:, p, ch:ch + 1], b[:, P + C * c:P + C * c + C],
                                                    MUL, ADD)
                last.then_inc(S("r16"), 1)

        DT = slice(NP_, N)
        QJ = 4 * NSTAGE * 2

        def wait_q(eng, s, p):
            eng.wait_ge(S("job"), QJ + 2 * s + p + 1)

        def q_pe(pe):
            hp = [slice(0, 64), slice(64, P)]

            def job(s, p):
                if s >= 4:
                    pe.wait_ge(S(f"q{s - 4}"), p + 1)
                else:
                    pe.wait_ge(S(f"r{NSTAGE + s - 4}"), 6 + p + 1)
                return bank(s, p)

            for p in range(2):
                b = job(0, p)
                for k, src in enumerate((v[:, p], bh[:, p], kh[:, p], ar[:, p, 0])):
                    last = pe.transpose(b[0:32, P * k:P * k + P], src[:, DT], ident)
                last.then_inc(S("job"), 1)
            for h in range(2):
                for p in range(2):
                    b = job(1 + h, p)
                    for k, left in enumerate((bt, kt)):
                        last = pe.matmul(b[0:32, 64 * k:64 * k + 64].rearrange("p (a b) -> p a b", a=2), left[hp[h], p, DT],
                                         ar[hp[h], p, :, DT], start=True, stop=True)
                    last.then_inc(S("job"), 1)
            for p in range(2):
                b = job(3, p)
                pe.wait_ge(S("lev"), 48 + p + 1)
                for h in range(2):
                    last = pe.matmul(b[0:32, 32 * h:32 * h + 32], nlv[0:32, 0, p, h, 0:32], ident[0:32, 0:32], start=True, stop=True)
                last.then_inc(S("job"), 1)
            for p in range(2):
                b = job(4, p)
                pe.wait_ge(S("lev"), 50 + p + 1)
                pe.wait_ge(S("q3"), p + 1)
                for h in range(2):
                    last = pe.matmul(b[0:32, 32 * h:32 * h + 32], nlv[0:32, 1, p, h, 0:32], tt_[0:32, p, 0, h, 0:32], start=True, stop=True)
                last.then_inc(S("job"), 1)
            for p in range(2):
                b = job(5, p)
                pe.wait_ge(S("q4"), p + 1)
                for h in range(2):
                    last = pe.matmul(b[0:32, 32 * h:32 * h + 32], xx[0:32, p, h, 0:32], tt_[0:32, p, 1, h, 0:32], start=True, stop=True)
                last.then_inc(S("job"), 1)
            for p in range(2):
                b = job(6, p)
                pe.wait_ge(S("q2"), p + 1)
                pe.wait_ge(S("q0"), p + 1)
                for h in range(2):
                    last = pe.matmul(b[0:32, C * h:C * h + C], akr[0:32, p, h, 0, 0:32], bkv[0:32, p, 0, C * h:C * h + C], start=True, stop=True)
                last.then_inc(S("job"), 1)
            for p in range(2):
                b = job(7, p)
                pe.wait_ge(S("q5"), p + 1)
                pe.wait_ge(S("q6"), p + 1)
                for h in range(2):
                    last = pe.matmul(b[0:32, P * h:P * h + P], tt_[0:32, p, 1, h, 0:32], rhs[0:32, p, h], start=True, stop=True)
                last.then_inc(S("job"), 1)
            for p in range(2):
                b = job(8, p)
                pe.wait_ge(S("q7"), p + 1)
                for h in range(2):
                    last = pe.matmul(b[hp[h], 0:32], tu[0:32, p, h, 0:C], nrb[0:32, p, h, 1, 0:32], start=True, stop=True)
                last.then_inc(S("job"), 1)
            for p in range(2):
                b9, b10 = job(9, p), job(10, p)
                for h in range(2):
                    pe.wait_ge(S("ex"), 2 * p + h + 1)
                    flat = lambda k: ex3[k][0:32]
                    last9 = pe.matmul(b9[hp[h], 0:512], tu[0:32, p, h, 0:C], flat(2), start=True, stop=True)
                    pe.matmul(b10[hp[h], 0:512], bkv[0:32, p, 1, C * h:C * h + C], flat(0), start=True, stop=False)
                    last = pe.matmul(b10[hp[h], 0:512], bkv[0:32, p, 2, C * h:C * h + C], flat(1), start=False, stop=False)
                    last.then_inc(S("ex_used"), 1)
            for p in range(2):
                b10 = bank(10, p)
                pe.wait_ge(S("in_s0"), 16)
                pe.wait_ge(S("q9"), p + 1)
                for h in range(2):
                    for n in range(NB):
                        last = pe.matmul(b10[hp[h], C * n:C * n + C], smt[hp[h], p, n], s0t[hp[h], p, n], start=False, stop=n == NB - 1)
                last.then_inc(S("q_sum"), 1)
            for p in range(2):
                b = job(11, p)
                pe.wait_ge(S("q8"), p + 1)
                for h in range(2):
                    out = b[hp[h], 0:32]
                    pe.matmul(out, tu[0:32, p, h, C:P], nrb[0:32, p, h, 1, 0:32], start=True, stop=False)
                    pe.matmul(out, bkv[0:32, p, 0, C * h:C * h + C], akr[0:32, p, h, 1, 0:32], start=False, stop=False)
                    for n in range(NB):
                        cols = slice(NT * n, NT * n + NT)
                        last = pe.matmul(b[hp[h], cols], s0t[hp[h], p, n], qt[hp[h], p, cols], start=False, stop=n == NB - 1)
                last.then_inc(S("q_sum"), 1)

        def q_act(act):
            def done(s, p):
                wait_q(act, s, p)
                return bank(s, p)

            two = "p (h c) -> p h c"
            for p in range(2):
                b = done(0, p)
                wait_job(act, 3, 19, p)
                act.activation(bkv[0:32, p, 0:3], b[0:32, 0:3 * P].rearrange("p (k c) -> p k c", k=3), ACT.Copy)
                act.activation(rhs[0:32, p, :, 0:C], b[0:32, 3 * P:].rearrange(two, h=2), ACT.Copy).then_inc(S("q0"), 1)
            for p in range(2):
                b = done(4, p)
                act.activation(xx[0:32, p, :, 0:32], b[0:32, 0:64].rearrange(two, h=2), ACT.Copy).then_inc(S("q4"), 1)
            for p in range(2):
                b = done(6, p)
                act.activation(rhs[0:32, p, :, C:P], b[0:32, 0:P].rearrange(two, h=2), ACT.Copy).then_inc(S("q6"), 1)
            for p in range(2):
                b = done(7, p)
                act.activation(tu[0:32, p], b[0:32, 0:2 * P].rearrange(two, h=2), ACT.Copy).then_inc(S("q7"), 1)
            for p in range(2):
                act.wait_ge(S("q_sum"), p + 1)
                act.activation(s1t[:, p].rearrange("p b c -> p (b c)"), bank(10, p), ACT.Copy).then_inc(S("q_s1"), 1)
            for p in range(2):
                act.wait_ge(S("q_sum"), 2 + p + 1)
                act.activation(yc[:, p, DT], bank(11, p)[:, 0:32], ACT.Copy).then_inc(S("q_y"), 1)

        def q_dve(dve):
            def done(s, p):
                wait_q(dve, s, p)
                return bank(s, p)

            mask = C_("smask", 64, rows=32).rearrange("p (k c) -> p k c", k=2)
            for h in range(2):
                for p in range(2):
                    b = done(1 + h, p)
                    wait_job(dve, 3, 19, p)
                    dve.wait_ge(S("lev"), 48)
                    for w in range(2):
                        last = dve.tensor_tensor(nak[0:32, p, h, w, :, 0:32], b[0:32, 64 * w:64 * w + 64].rearrange("p (k c) -> p k c", k=2),
                                                 mask, MUL)
                    last.then_inc(S(f"q{1 + h}"), 1)
            idb = C_("ident", 32, rows=32).unsqueeze(1).to_broadcast([32, 2, 32])
            two = "p (h c) -> p h c"
            for p in range(2):
                b = done(3, p)
                dve.tensor_tensor(tt_[0:32, p, 1, :, 0:32], nlv[0:32, 0, p, :, 0:32], idb, ADD)
                dve.tensor_tensor(tt_[0:32, p, 0, :, 0:32], b[0:32, 0:64].rearrange(two, h=2), idb, ADD).then_inc(S("q3"), 1)
            for p in range(2):
                b = done(5, p)
                dve.wait_ge(S("q3"), p + 1)
                t_ = tt_[0:32, p, 1, :, 0:32]
                dve.tensor_tensor(t_, b[0:32, 0:64].rearrange(two, h=2), t_, ADD).then_inc(S("q5"), 1)
            for p in range(2):
                b = done(8, p)
                dve.tensor_tensor(qt[:, p, 0:32], b[:, 0:32], ar[:, p, 1, DT], ADD).then_inc(S("q8"), 1)
            sel = C_("bsel", 8, rows=32).unsqueeze(2).to_broadcast([32, NB, C])
            for p in range(2):
                for h in range(2):
                    if 2 * p + h:
                        dve.wait_ge(S("ex_used"), 2 * p + h)
                    dve.wait_ge(S("q7"), p + 1)
                    for k, src in enumerate((tu[0:32, p, h, C:P], bkv[0:32, p, 0, C * h:C * h + C], bkv[0:32, p, 1, C * h:C * h + C])):
                        last = dve.tensor_tensor(ex3[k][0:32].rearrange("p (b c) -> p b c", c=C), src.unsqueeze(1).to_broadcast([32, NB, C]), sel, MUL)
                    last.then_inc(S("ex"), 1)
            for p in range(2):
                dve.wait_ge(S("ex_used"), 2 * p + 2)
                for n in range(NB):
                    last = dve.scalar_tensor_tensor(smt[:, p, n], C_("idc", C), pend[:, p, NC_ + n:NC_ + n + 1],
                                                    bank(9, p)[:, C * n:C * n + C], MUL, ADD)
                last.then_inc(S("q9"), 1)

        Y_ORDER = (0, 1, 6, 7, 2, 3, 4, 5)
        y32 = (ya[:, 0], ya[:, 1], yb[:, 0], yb[:, 1], mixf[:, 4], mixf[:, 5], yd[:, 0], yd[:, 1])

        def mixer_pe(pe):
            A, B = pair(2), pair(3)
            for m in range(NIN):
                split_ready(pe, MIX0, 0, m)
                if m == 0:
                    pe.wait_ge(S("n_xl"), 2 * KD)
                if m >= 2:
                    in_out(pe, m - 2)
                product(pe, pair(m % 2), m % 4, KD, xh, xl).then_inc(S("unit_done"), 1)
                if m in (3, 4, 5):
                    rows = (slice(0, 32), slice(32, 64), slice(64, P))[m - 3]
                    for p in range(2):
                        pe.wait_ge(S("lo2"), 1)
                        if m > 3:
                            pe.wait_ge(S("lora_out"), 2 * (m - 3) - 1 + p)
                        for n in range(2):
                            last = pe.matmul((A, B)[p][:, n], lora_w[rows, P * p:P * p + P],
                                             (lo if m == 4 else lo2)[rows, n * H:n * H + H], start=True, stop=True)
                        last.then_inc(S("lora"), 1)
                if m == 7:
                    pe.wait_ge(S("lora_out"), 5)
                    pe.wait_ge(S("kk_sq"), 2)
                    for p in range(2):
                        for t in range(5):
                            c = (p * 5 + t) * 2
                            last = pe.matmul(ps[:, 4, c:c + 2], kt[:, p, tok(t)], hsel, start=True, stop=True)
                    last.then_inc(S("kk_sum"), 1)
                if m == 8:
                    pe.wait_ge(S("kk_rec"), 1)
                    pe.wait_ge(S("lora_out"), 6)
                    for p in range(2):
                        spread_pe(pe, 4 + 2 * p, 5 + 2 * p, p).then_inc(S("kk_spread"), 1)
                if m == 10:
                    for p in range(2):
                        pe.wait_ge(S("kk"), p + 1)
                        pe.wait_ge(S("rk"), p + 1)
                        for n in range(2):
                            last = pe.matmul((A, B)[p][:, n], hb, bo[:, p, n * H:n * H + H], start=True, stop=True)
                        last.then_inc(S("bo_sum"), 1)
            in_out(pe, DD0)
            in_out(pe, DD1)
            in_out(pe, AB1)
            pe.wait_ge(S("bonus"), 2)
            pe.wait_ge(S("fac"), 2)
            for t in range(4):
                wkv_pe(pe, t)
            q_pe(pe)
            for p in range(2):
                pe.wait_ge(S("diff"), p + 1)
                pe.wait_ge(S("q_y"), 2)
                for n in range(2):
                    last = pe.matmul(pair(p)[:, n], dwbd[:, p], yd[:, p, n * H:n * H + H], start=True, stop=True)
                last.then_inc(S("d_map"), 1)
            pe.wait_ge(S("conv"), 1)
            for p in range(2):
                for n in range(2):
                    last = pe.matmul(pair(2)[:, n], ones, yb[:, p, n * H:n * H + H], start=p == 0, stop=p == 1)
            last.then_inc(S("b_mean"), 1)
            pe.wait_ge(S("b_sq"), 2)
            for t in range(5):
                for p in range(2):
                    last = pe.matmul(ps[:, 6, t:t + 1], tmp2[:, p, tok(t)], ones[:, 0:1], start=p == 0, stop=p == 1)
            last.then_inc(S("b_sum"), 1)
            pe.wait_ge(S("b_rec"), 1)
            for t in range(4):
                pe.matmul(ps[:, 7, tok(t)], st[:, 2, t:t + 1].to_broadcast([P, P]), ident, start=True, stop=True)
            pe.matmul(ps[:, 6, 0:NS], st[:, 2, 4:5].to_broadcast([P, P]), ident[:, P - NS:P], start=True, stop=True
                      ).then_inc(S("b_spread"), 1)
            for p in range(2):
                pe.wait_ge(S("d_out_y"), p + 1)
                for n in range(2):
                    last = pe.matmul(pair(p)[:, n], hb, yc[:, p, n * H:n * H + H], start=True, stop=True)
                last.then_inc(S("c_mean"), 1)
            pe.wait_ge(S("b_norm"), 2)
            pe.wait_ge(S("c_sq"), 2)
            for p in range(2):
                for t in range(5):
                    c = (p * 5 + t) * 2
                    last = pe.matmul(ps[:, 4, c:c + 2], kt[:, p, tok(t)], hsel, start=True, stop=True)
            last.then_inc(S("c_sum"), 1)
            pe.wait_ge(S("c_rec"), 1)
            for p in range(2):
                spread_pe(pe, 4 + 2 * p, 5 + 2 * p, p).then_inc(S("c_spread"), 1)
            for m in range(KD):
                split_ready(pe, MIX0, 0, OUT0 + m)
                if m == 0:
                    pe.wait_ge(S("y_lo"), KD)
                    pe.wait_ge(S("c_norm"), 2)
                if m >= 2:
                    pe.wait_ge(S("o_out"), m - 1)
                product(pe, pair(m % 2), (OUT0 + m) % 4, KD, xh, xl
                        ).then_inc(S("unit_done"), 2 if m == KD - 1 else 1)

        def spread_pe(pe, big, small, p):
            for t in range(5):
                out, right = (ps[:, big, tok(t)], ident) if t < 4 else (ps[:, small, 0:NS], ident[:, P - NS:P])
                for h in range(2):
                    c = (p * 5 + t) * 2 + h
                    last = pe.matmul(out[C * h:C * h + C], st[:, 2, c:c + 1].to_broadcast([P, C]), right, start=True, stop=True)
            return last

        def mixer_act(act):
            for m in range(NIN + 2):
                if 2 <= m:
                    split_hi(act, MIX0, 0, m, KD)
                n = m - 2
                if n >= 0 and n not in BY_DVE:
                    unit_done(act, MIX0, 0, n)
                    if n <= V1:
                        parts, func = pieces(pc[:, C_TILE[n]], n, 513, 1), ACT.Copy
                        parts = (parts[0], parts[1], (steps(pc[:, C_TILE[n]], 513, 1), parts[2][1]))
                    elif n in (BV0, BV1):
                        parts, func = pieces(zb[:, n - BV0], n, 542, 30), ACT.Copy
                    elif n in (BG0, BG1):
                        parts, func = ((halves(yb[:, n - BG0]), pair(n % 2)),), ACT.Sigmoid
                    elif n in (AC0, AC1):
                        parts, func = pieces(ub[:, n - AC0], n, 514, 2), ACT.Copy
                    else:
                        if n == DD0:
                            act.wait_ge(S("pads"), 3)
                        parts, func = pieces(db[:, n - DD0], n, 527, 15), ACT.Copy
                    for dst, src in parts:
                        last = act.activation(dst, src, func)
                    last.then_inc(S("in_act"), 1)
                if m == 3:
                    act.wait_ge(S("xm"), 1)
                    act.activation(lo2[0:32], lo[0:32], ACT.Tanh)
                    act.activation(lo2[64:P], lo[64:P], ACT.Sigmoid).then_inc(S("lo2"), 1)
                if m == 5:
                    for p in range(2):
                        act.wait_ge(S("lora"), p + 1)
                        act.activation(halves(bt[:, p]), pair(2 + p), ACT.Sigmoid, bias=par_("w0", p)).then_inc(S("lora_out"), 1)
                if m == 6:
                    for p in range(2):
                        act.wait_ge(S("lora"), 2 + p + 1)
                        act.activation(halves(bh[:, p]), pair(2 + p), ACT.Sigmoid, bias=par_("a0", p)).then_inc(S("lora_out"), 1)
                if m == 7:
                    for p in range(2):
                        act.wait_ge(S("lora"), 4 + p + 1)
                        act.activation(halves(gg[:, p]), pair(2 + p), ACT.Copy).then_inc(S("lora_out"), 1)
                    for p in range(2):
                        act.wait_ge(S("kkraw"), p + 1)
                        act.activation(kt[:, p], ar[:, p, 0], ACT.Square).then_inc(S("kk_sq"), 1)
                if m == 8:
                    act.wait_ge(S("kk_max"), 1)
                    act.activation(st[:, 1, 0:20], st[:, 0, 0:20], ACT.Sqrt).then_inc(S("kk_root"), 1)
                if m in (9, 10):
                    p = m - 9
                    act.wait_ge(S("dsum"), p + 1)
                    act.activation(pend[:, p, 0:NC_], ll[:, p, 0:NP_].rearrange("p (k c) -> p k c", c=C)[:, :, C - 1], ACT.Exp, scale=-CD)
                    act.activation(pend[:, p, NC_:], comp(ll[:, p, DT])[:, :, NT - 1], ACT.Exp, scale=-CD)
                    act.activation(kt[:, p], ll[:, p], ACT.Exp, scale=CD)
                    act.activation(bt[:, p], bt[:, p], ACT.Exp, scale=-CD)
                    act.activation(kh[:, p], kh[:, p], ACT.Exp, scale=-CD).then_inc(S("exps"), 1)
                    act.wait_ge(S("exps"), 2 * p + 1)
                    act.activation(ll[:, p], ll[:, p], ACT.Exp, scale=-CD).then_inc(S("exps"), 1)
            act.wait_ge(S("out"), 13 * 16)
            act.wait_ge(S("diff"), 2)
            for t in range(4):
                wkv_act(act, t)
            q_act(act)
            for p in range(2):
                act.wait_ge(S("d_map"), p + 1)
                act.activation(halves(yd[:, p]), pair(p), ACT.Copy, scale=par_("ds", p)).then_inc(S("d_out_y"), 1)
            for p in range(2):
                act.wait_ge(S("b_cen"), p + 1)
                act.activation(tmp2[:, p], yb[:, p], ACT.Square).then_inc(S("b_sq"), 1)
            act.wait_ge(S("b_sum"), 1)
            act.activation(st[:, 1, 0:5], ps[:, 6, 0:5], ACT.Sqrt, scale=1.0 / G, bias=C_("eps", 1, 1)).then_inc(S("b_root"), 1)
            for p in range(2):
                act.wait_ge(S("c_cen"), p + 1)
                act.activation(kt[:, p], yc[:, p], ACT.Square).then_inc(S("c_sq"), 1)
            act.wait_ge(S("c_sum"), 1)
            act.activation(st[:, 1, 0:20], ps[:, 4, 0:20], ACT.Sqrt, scale=1.0 / C, bias=C_("eps", 1, 2)).then_inc(S("c_root"), 1)
            for p in range(2):
                act.wait_ge(S("b_norm"), p + 1)
                act.activation(yb[:, p], yb[:, p], ACT.Silu, bias=par_("bn", p)).then_inc(S("b_y"), 1)
            for n, k in enumerate(Y_ORDER):
                if k in (0, 1):
                    act.wait_ge(S("ay"), 2)
                elif k in (6, 7):
                    act.wait_ge(S("d_out_y"), 2)
                elif k in (2, 3):
                    act.wait_ge(S("b_y"), 2)
                else:
                    act.wait_ge(S("c_y"), k - 3)
                act.activation(xh[:, k], y32[k], ACT.Copy).then_inc(S("y_hi"), 1)
            for m in range(2, KD + 2):
                if m < KD:
                    split_hi(act, MIX0, 0, OUT0 + m, KD, skip=m == KD - 1)
                else:
                    split_hi(act, FFN2, 0, m - KD, KD)
                act.wait_ge(S("o_out"), m - 1)
                squares_act(act, 3, m - 2, f[:, m - 2])

        def mixer_dve(dve):
            do = Chain(dve, "dve_steps")
            do(dve.tensor_scalar(onemka[:], par[:, PCOL["ka"]:PCOL["ka"] + 2], -1.0, 1.0, MUL, ADD))
            taps = 0

            def shifted(n):
                j, w = C_TILE[n], n % 2
                dst = {LORA: lo, K0: kp[:, 0], K1: kp[:, 1], R0: ar[:, 0, 1], R1: ar[:, 1, 1], V0: v[:, 0], V1: v[:, 1]}[n]
                row, t_ = pc[:, j], tmp2[:, w]
                four = row[:, 513:].rearrange("p (b c) -> p b c", c=5)
                in_out(dve, n)
                dve.wait_ge(S("pads"), 1)
                if n >= 2:
                    dve.wait_ge(S("xm"), n - 1)
                dve.tensor_tensor(t_[:, 0:NP_], row[:, 0:NP_], row[:, 1:513], SUB)
                do(dve.tensor_tensor(comp(t_[:, DT]), four[:, :, 0:4], four[:, :, 1:5], SUB))
                mu = par_("mu", j)
                dve.scalar_tensor_tensor(dst[:, 0:NP_], t_[:, 0:NP_], mu, row[:, 1:513], MUL, ADD)
                dve.scalar_tensor_tensor(comp(dst[:, DT]), comp(t_[:, DT]), mu, four[:, :, 1:5], MUL, ADD).then_inc(S("xm"), 1)

            def conv(k0, k1):
                for k in range(k0, k1):
                    for p in range(2):
                        w = par[:, PCOL["bw"] + 2 * k + p:PCOL["bw"] + 2 * k + p + 1]
                        z1 = zb[:, p, k:k + NP_]
                        z2 = zb[:, p, 542:].rearrange("p (b c) -> p b c", c=34)[:, :, k:k + NT]
                        y1, y2 = yb[:, p, 0:NP_], comp(yb[:, p, DT])
                        if k == 0:
                            dve.wait_ge(S("glu"), p + 1)
                            dve.tensor_scalar(y1, z1, w, par_("bb", p), MUL, ADD)
                            dve.tensor_scalar(y2, z2, w, par_("bb", p), MUL, ADD).then_inc(S("taps"), 1)
                        else:
                            dve.wait_ge(S("taps"), 2 * k + p - 1)
                            dve.scalar_tensor_tensor(y1, z1, w, y1, MUL, ADD)
                            dve.scalar_tensor_tensor(y2, z2, w, y2, MUL, ADD).then_inc(S("taps" if 2 * k + p < 61 else "conv"), 1)

            for m in range(NIN + 2):
                if 2 <= m:
                    split_lo(dve, MIX0, 0, m, KD)
                n = m - 2
                if 0 <= n <= V1:
                    shifted(n)
                if n in (BG0, BG1):
                    i = n - BG0
                    in_out(dve, n)
                    dve.wait_ge(S("pads"), 2)
                    z = zb[:, i]
                    dve.tensor_tensor(z[:, 30:542], z[:, 30:542], yb[:, i, 0:NP_], MUL)
                    zs = steps(z, 542, 30)
                    dve.tensor_tensor(zs, zs, comp(yb[:, i, DT]), MUL).then_inc(S("glu"), 1)
                if n in (AH0, AH1):
                    i = n - AH0
                    unit_done(dve, MIX0, 0, n)
                    in_out(dve, AC0 + i)
                    for dst, src in pieces(ub[:, i], n, 514, 2):
                        last = dve.tensor_tensor(dst, dst, src, MUL)
                    last.then_inc(S("in_dve"), 1)
                    dve.wait_ge(S("in_dve"), i + 1)
                    dve.sem_inc(S("au"), 1)
                    u1, u2 = ub[:, i, 0:514], ub[:, i, 514:].rearrange("p (b c) -> p b c", c=6)
                    for k in range(3):
                        w = par[:, PCOL["aw"] + 2 * k + i:PCOL["aw"] + 2 * k + i + 1]
                        y1, y2 = ya[:, i, 0:NP_], comp(ya[:, i, DT])
                        if k == 0:
                            dve.tensor_scalar(y1, u1[:, k:k + NP_], w, None, MUL)
                            do(dve.tensor_scalar(y2, u2[:, :, k:k + NT], w, None, MUL))
                        else:
                            dve.scalar_tensor_tensor(y1, u1[:, k:k + NP_], w, y1, MUL, ADD)
                            do(dve.scalar_tensor_tensor(y2, u2[:, :, k:k + NT], w, y2, MUL, ADD))
                if n in (AB0, AB1):
                    i = n - AB0
                    unit_done(dve, MIX0, 0, n)
                    dve.tensor_tensor(halves(ya[:, i]), pair(n % 2), halves(ya[:, i]), MUL).then_inc(S("in_dve"), 1)
                if m == 5:
                    for p in range(2):
                        dve.wait_ge(S("xm"), p + 2)
                        dve.tensor_scalar(ar[:, p, 0], kp[:, p], par_("kk", p), None, MUL).then_inc(S("kkraw"), 1)
                if m == 7:
                    for p in range(2):
                        dve.wait_ge(S("lora_out"), p + 1)
                        do(dve.tensor_tensor_scan(ll[:, p], C_("scan", N), bt[:, p], 0.0, MUL, ADD))
                        dve.tensor_tensor(bt[:, p], ll[:, p], bt[:, p], SUB)
                        l1, l2 = ll[:, p, 0:NP_].rearrange("p (k c) -> p k c", c=C), comp(ll[:, p, DT])
                        dve.tensor_tensor(kh[:, p, 0:NP_].rearrange("p (k c) -> p k c", c=C),
                                          l1[:, :, C - 1:C].to_broadcast([P, NC_, C]), l1, SUB)
                        dve.tensor_tensor(comp(kh[:, p, DT]), l2[:, :, NT - 1:NT].to_broadcast([P, NB, NT]), l2, SUB
                                          ).then_inc(S("dsum"), 1)
                if m == 8:
                    for p in range(2):
                        dve.wait_ge(S("lora_out"), 4)
                        dve.wait_ge(S("xm"), 7)
                        do(dve.tensor_scalar(tmp2[:, p], bh[:, p], par_("ka", p), onemka[:, p:p + 1], MUL, ADD))
                        do(dve.tensor_tensor(kp[:, p], kp[:, p], tmp2[:, p], MUL))
                        dve.scalar_tensor_tensor(bo[:, p], ar[:, p, 1], par_("rk", p), kp[:, p], MUL, MUL).then_inc(S("rk"), 1)
                    dve.wait_ge(S("kk_sum"), 1)
                    dve.tensor_scalar(st[:, 0, 0:20], ps[:, 4, 0:20], 1e-24, None, ALU.max).then_inc(S("kk_max"), 1)
                    dve.wait_ge(S("kk_root"), 1)
                    dve.reciprocal(st[:, 2, 0:20], st[:, 1, 0:20]).then_inc(S("kk_rec"), 1)
                if m == 10:
                    for p in range(2):
                        dve.wait_ge(S("kk_spread"), p + 1)
                        dve.tensor_tensor(ar[:, p, 0, 0:NP_], ps[:, 4 + 2 * p], ar[:, p, 0, 0:NP_], MUL)
                        dve.tensor_tensor(ar[:, p, 0, DT], ps[:, 5 + 2 * p, 0:NS], ar[:, p, 0, DT], MUL).then_inc(S("kk"), 1)
                        dve.wait_ge(S("kk"), p + 1)
                        do(dve.scalar_tensor_tensor(bh[:, p], ar[:, p, 0], -1.0, bh[:, p], MUL, MUL))
                if m == 12:
                    for p in range(2):
                        dve.wait_ge(S("bo_sum"), p + 1)
                        dve.tensor_tensor(halves(bo[:, p]), pair(2 + p), halves(v[:, p]), MUL).then_inc(S("bonus"), 1)
                if m in (12, 13):
                    p = m - 12
                    dve.wait_ge(S("exps"), 2 * p + 2)
                    dve.tensor_tensor(ar[:, p, 1], ar[:, p, 1], ll[:, p], MUL)
                    do(dve.tensor_tensor(ar[:, p, 0], ar[:, p, 0], bt[:, p], MUL))
                    do(dve.tensor_tensor(bt[:, p], bh[:, p], kt[:, p], MUL))
                    dve.tensor_tensor(bh[:, p], bh[:, p], kh[:, p], MUL)
                    dve.tensor_tensor(kt[:, p], kp[:, p], kt[:, p], MUL)
                    dve.tensor_tensor(kh[:, p], kp[:, p], kh[:, p], MUL).then_inc(S("fac"), 1)
                if m >= 14:
                    k0 = taps
                    taps = min(31, taps + 4)
                    conv(k0, taps)
            conv(taps, 31)
            dve.wait_ge(S("in_dve"), 4)
            dve.sem_inc(S("ay"), 2)
            dve.wait_ge(S("pool_d"), 4)
            for g in range(4):
                i, rows = g // 2, slice(64 * (g % 2), 64 * (g % 2) + 64)
                s_ = (d1, d2)[g % 2][rows, i]
                z, w = db[rows, i], con[rows, CCOL["wcol"] + i:CCOL["wcol"] + i + 1]
                cnt = con[rows, CCOL["cnt"] + 16 * i:CCOL["cnt"] + 16 * i + 16]
                dve.scalar_tensor_tensor(yd[rows, i, 16:NP_], s_[:, 31:527], w, z[:, 31:527], MUL, SUB)
                dve.scalar_tensor_tensor(comp(yd[rows, i, DT]), steps(s_, 527, 15), w, steps(z, 527, 15), MUL, SUB)
                do(dve.tensor_tensor(yd[rows, i, 0:16], s_[:, 15:31], cnt, MUL))
                last = dve.tensor_tensor(yd[rows, i, 0:16], yd[rows, i, 0:16], z[:, 15:31], SUB)
                if g % 2:
                    last.then_inc(S("diff"), 1)
                else:
                    do(last)
            dve.wait_ge(S("out"), 13 * 16)
            for t in range(4):
                wkv_dve(dve, t)
            q_dve(dve)
            dve.wait_ge(S("b_mean"), 1)
            for p in range(2):
                dve.scalar_tensor_tensor(halves(yb[:, p]), pair(2), -1.0 / G, halves(yb[:, p]), MUL, ADD).then_inc(S("b_cen"), 1)
            dve.wait_ge(S("b_root"), 1)
            dve.reciprocal(st[:, 2, 0:5], st[:, 1, 0:5]).then_inc(S("b_rec"), 1)
            for p in range(2):
                dve.wait_ge(S("c_mean"), p + 1)
                dve.scalar_tensor_tensor(halves(yc[:, p]), pair(p), -1.0 / C, halves(yc[:, p]), MUL, ADD).then_inc(S("c_cen"), 1)
            dve.wait_ge(S("b_spread"), 1)
            for p in range(2):
                g = par_("bg", p)
                dve.scalar_tensor_tensor(yb[:, p, 0:NP_], ps[:, 7], g, yb[:, p, 0:NP_], MUL, MUL)
                dve.scalar_tensor_tensor(yb[:, p, DT], ps[:, 6, 0:NS], g, yb[:, p, DT], MUL, MUL).then_inc(S("b_norm"), 1)
            dve.wait_ge(S("c_root"), 1)
            dve.reciprocal(st[:, 2, 0:20], st[:, 1, 0:20]).then_inc(S("c_rec"), 1)
            for p in range(2):
                g = par_("cg", p)
                dve.wait_ge(S("c_spread"), p + 1)
                dve.scalar_tensor_tensor(yc[:, p, 0:NP_], ps[:, 4 + 2 * p], g, yc[:, p, 0:NP_], MUL, MUL)
                dve.scalar_tensor_tensor(yc[:, p, DT], ps[:, 5 + 2 * p, 0:NS], g, yc[:, p, DT], MUL, MUL).then_inc(S("c_norm"), 1)
                dve.wait_ge(S("c_norm"), p + 1)
                do(dve.scalar_tensor_tensor(mixf[:, 4 + p], yc[:, p], par_("cb", p), bo[:, p], ADD, ADD))
                dve.tensor_tensor(mixf[:, 4 + p], mixf[:, 4 + p], gg[:, p], MUL).then_inc(S("c_y"), 1)
            for n, k in enumerate(Y_ORDER):
                dve.wait_ge(S("y_hi"), n + 1)
                dve.tensor_tensor(xl[:, k], y32[k], xh[:, k].bitcast(F32), SUB).then_inc(S("y_lo"), 1)
            dve.wait_ge(S("y_lo"), KD)
            for m in range(2, KD + 2):
                if m < KD:
                    split_lo(dve, MIX0, 0, OUT0 + m, KD, skip=m == KD - 1)
                else:
                    split_lo(dve, FFN2, 0, m - KD, KD)
                d = m - 2
                unit_done(dve, MIX0, 0, OUT0 + d)
                dve.tensor_copy(halves(f[:, d]), pair(d % 2)).then_inc(S("o_out"), 1)
                if d >= 2:
                    squares_dve(dve, 3, d - 1)
            squares_dve(dve, 3, KD - 1)

        @block.sync
        def _(sp):
            sp.dma_start(x[:], a["x"]).then_inc(S("in_x"), 16)
            sp.dma_start(con[:], a["con"]).then_inc(S("in_con"), 16)
            sp.dma_start(par[:], a["par"]).then_inc(S("in_con"), 16)
            sp.dma_start(lora_w[:], a["lora"]).then_inc(S("in_con"), 16)
            sp.dma_start(dwbd[:], a["dw"]).then_inc(S("in_con"), 16)
            ffn_sp(sp, 0, 0)
            mixer_sp(sp)
            ffn_sp(sp, 1, FFN2)
            for k in range(KD):
                sp.wait_ge(S("x_ready"), 2 * KD + k + 1)
                sp.dma_start(o["y"][:, k], x[:, k]).then_inc(S("out"), 16)
            sp.wait_ge(S("out"), (15 + KD) * 16)

        @block.tensor
        def _(pe):
            pe.sem_inc(S("unit_done"), SPL)
            pe.wait_ge(S("in_con"), 64)
            stats_pe(pe, 0)
            ffn_pe(pe, 0, 0, 0)
            stats_pe(pe, 1)
            stats_pe(pe, 2)
            mixer_pe(pe)
            stats_pe(pe, 3)
            stats_pe(pe, 4)
            ffn_pe(pe, 1, FFN2, 4)
            stats_pe(pe, 5)

        @block.gpsimd
        def _(pool):
            mixer_pool(pool)

        @block.scalar
        def _(act):
            for s in range(2):
                split_hi(act, 0, 0, s, KD)
            act.wait_ge(S("in_con"), 64)
            pre_act(act, 0)
            ffn_act(act, 0, 0, 1, MIX0, KD)
            stats_act(act, 1)
            pre_act(act, 2)
            mixer_act(act)
            stats_act(act, 3)
            pre_act(act, 4)
            ffn_act(act, 1, FFN2, 5, None, 0)
            stats_act(act, 5)

        @block.vector
        def _(dve):
            dve.sem_inc(S("w_lo"), RAW)
            for q in range(2):
                dve.sem_inc(S(f"h_mul{q}"), 2)
                dve.sem_inc(S(f"h_lo{q}"), 2)
                dve.sem_inc(S(f"d_out{q}"), 4)
            for s in range(2):
                split_lo(dve, 0, 0, s, KD)
            dve.wait_ge(S("in_con"), 64)
            pre_dve(dve, 0)
            ffn_dve(dve, 0, 0, 1, MIX0, KD)
            post_dve(dve, 1)
            pre_dve(dve, 2)
            mixer_dve(dve)
            post_dve(dve, 3)
            pre_dve(dve, 4)
            ffn_dve(dve, 1, FFN2, 5, None, 0)
            post_dve(dve, 5)


def _tiles(w):
    k, n = w.shape
    return np.ascontiguousarray(w.reshape(k // P, P, n // P, P).transpose(2, 1, 0, 3).reshape(n // P, P, k))


def _cols(v):
    return np.asarray(v).reshape(-1, P).T


def pack(inp):
    i = {k: np.asarray(v) for k, v in inp.items()}
    one = {k: v[0] for k, v in i.items() if v.shape[0] == 1}
    out = {}
    tokens = np.concatenate([i["x_prompt"].reshape(NP_, D), i["x_sample"].reshape(NS, D)])
    out["x"] = np.ascontiguousarray(tokens.T.reshape(KD, P, N).transpose(1, 0, 2))
    for q, n in enumerate(("ffn1", "ffn2")):
        g, u = _tiles(one[n + "_w_gate"]), _tiles(one[n + "_w_up"])
        out[f"w_gu{q}"] = np.ascontiguousarray(np.stack([g, u], 1).reshape(2 * FT, P, D))
        for g, (f0, nf) in enumerate(GROUPS):
            out[f"w_d{q}_{g}"] = _tiles(one[n + "_w_down"][f0 * P:(f0 + nf) * P])
    out["w_in"] = np.ascontiguousarray(_tiles(one["w_in"])[list(IN_TILES)])
    out["w_out"] = _tiles(one["w_out"])
    rows = {"g0": "ffn1_pre_g", "g1": "ffn1_post_g", "g2": "mix_pre_g", "g3": "mix_post_g", "g4": "ffn2_pre_g",
            "g5": "ffn2_post_g", "mu": "c_mu", "w0": "c_w0", "a0": "c_a0", "kk": "c_k_k", "ka": "c_k_a", "rk": "c_r_k",
            "cg": "c_ln_g", "cb": "c_ln_b", "bb": "b_conv_b", "bg": "b_ln_g", "bn": "b_ln_b", "ds": "d_scale",
            "aw": "a_conv_w", "bw": "b_conv_w"}
    out["par"] = np.ascontiguousarray(np.concatenate([_cols(one[rows[k]]) for k in PCOL], 1))
    out["lora"] = np.concatenate([one["c_w2"], one["c_a2"], one["c_g2"]])
    dw = np.zeros((P, 2, P), np.float32)
    for g in range(4):
        r = 64 * (g % 2)
        dw[r:r + 64, g // 2, r:r + 64] = one["d_w"][g]
    out["dw"] = dw
    out["con"] = constants()

    def feat(v):
        b, r, n = v.shape
        return v.reshape(b, r, n // P, P).transpose(3, 2, 0, 1).reshape(P, -1)
    out["sta"] = np.ascontiguousarray(np.concatenate([
        feat(i["state_shift_c"][0][:, None]), feat(i["state_conv_a"][0]), feat(i["state_conv_b"][0]),
        feat(i["state_pool_d"][0])], 1))
    w = i["state_wkv_c"][0].reshape(NB, 2, 2, C, C)
    out["s0"] = np.ascontiguousarray(w.transpose(2, 4, 1, 0, 3).reshape(P, 2, NB, C))
    return out


OUTS = {"y": (P, KD, N), "o_a": (P, 2, 2 + 2 * NB), "o_b": (P, 2, 30 + 30 * NB), "o_shift": (P, 7, 1 + NB),
        "o_d": (P, 2, 15 + 15 * NB), "o_sp": (P, 2, C), "o_ss": (P, 2, NB, C)}


def unpack(r):
    y = r["y"].transpose(1, 0, 2).reshape(D, N).T
    out = [y[:NP_].reshape(1, NP_, D), y[NP_:].reshape(NB, NT, D)]

    def rows(v, n):
        w = v.transpose(2, 1, 0).reshape(v.shape[2], -1)
        return w[:n][None, None], w[n:].reshape(1, NB, n, -1)
    a, b, d = rows(r["o_a"], 2), rows(r["o_b"], 30), rows(r["o_d"], 15)
    s = rows(r["o_shift"], 1)
    sp = r["o_sp"].reshape(2, C, 2, C).transpose(2, 0, 3, 1).reshape(1, 1, 4, C, C)
    ss = r["o_ss"].reshape(2, C, 2, NB, C).transpose(3, 2, 0, 4, 1).reshape(1, NB, 4, C, C)
    p = (a[0], b[0], s[0][:, :, 0], sp, d[0])
    q = (a[1], b[1], s[1][:, :, 0], ss, d[1])
    return tuple(np.ascontiguousarray(v) for v in (*out, *p, *q))


def kernel(**inputs):
    import concourse.bacc as bacc
    from concourse.bass_utils import run_bass_kernel_spmd as run

    nc = bacc.Bacc("TRN2", target_bir_lowering=False, num_devices=1)
    arrays = pack(inputs)
    a = {n: nc.dram_tensor("in_" + n, v.shape, F32, kind="ExternalInput").ap() for n, v in arrays.items()}
    o = {n: nc.dram_tensor("out_" + n, s, F32, kind="ExternalOutput").ap() for n, s in OUTS.items()}
    program(nc, a, o)
    r = run(nc, [{"in_" + n: v for n, v in arrays.items()}], core_ids=[0])
    return unpack({n: np.asarray(r.results[0]["out_" + n]) for n in OUTS})
```

```python
import numpy as np
from contextlib import ExitStack

import concourse.bass as bass
from concourse import mybir

F32 = mybir.dt.float32
F32R = mybir.dt.float32r
ALU = mybir.AluOpType
ACT = mybir.ActivationFunctionType
MUL, ADD, SUB = ALU.mult, ALU.add, ALU.subtract

P = 128
D = 1024
KD = D // P
NP_, NB, NT = 512, 8, 4
NS = NB * NT
N = NP_ + NS
H = N // 2
HP = NP_ - H
F = 2816
FT = F // P
GROUPS = ((0, 8), (8, 8), (16, 6))
G = 256
C = 64
NC_ = NP_ // C
LEVELS = (1, 2, 4, 8, 16, 32)
CD = float(np.exp(-0.5))
POOLW = (2, 4, 8, 16)
CONVB = 31

LORA, K0, K1, R0, R1, V0, V1, AC0, AC1, DD0, DD1, AH0, AH1, AB0, AB1, BV0, BV1, BG0, BG1 = range(19)
IN_TILES = (16, 12, 13, 10, 11, 14, 15, 4, 5, 17, 18, 0, 1, 2, 3, 6, 7, 8, 9)
NIN = len(IN_TILES)
C_TILE = (6, 2, 3, 0, 1, 4, 5)

PCOL = {}
_n = 0
for _name, _k in (("g0", 8), ("g1", 8), ("g2", 8), ("g3", 8), ("g4", 8), ("g5", 8), ("mu", 7), ("w0", 2), ("a0", 2),
                  ("kk", 2), ("ka", 2), ("rk", 2), ("cg", 2), ("cb", 2), ("bb", 2), ("bg", 2), ("bn", 2),
                  ("ds", 2), ("aw", 6), ("bw", 62)):
    PCOL[_name] = _n
    _n += _k
NPAR = _n
CCOL = {}
_n = 0
for _name, _k in (("ident", P), ("ones", P), ("hb", P), ("mask", 2 * P), ("lev", 6 * P), ("scan", N), ("cnt", 32),
                  ("wcol", 2), ("eps", 3), ("smask", 64), ("bsel", 8), ("idc", 64)):
    CCOL[_name] = _n
    _n += _k
NCON = _n
LORAW = 256
SCOL = {}
_n = 0
for _name, _k in (("shift", 7 * NB), ("u", 2 * NB * 2), ("z", 2 * NB * 30), ("d", 2 * NB * 15)):
    SCOL[_name] = _n
    _n += _k
NSTA = _n


def constants():
    c = np.zeros((P, NCON), np.float32)
    s, t = np.arange(P)[:, None], np.arange(P)[None, :]
    c[:, CCOL["ident"]:][:, :P] = s == t
    c[:, CCOL["ones"]:][:, :P] = 1
    c[:, CCOL["hb"]:][:, :P] = s // C == t // C
    c[:, CCOL["mask"]:][:, :P] = (s // C == t // C) & (s < t)
    c[:, CCOL["mask"] + P:][:, :P] = (s // C == t // C) & (s <= t)
    for n, b in enumerate(LEVELS):
        c[:, CCOL["lev"] + n * P:][:, :P] = (s // (2 * b) == t // (2 * b)) & (s // b != t // b) & (s < t)
    col = np.arange(N)
    start = np.where(col < NP_, col % C == 0, (col - NP_) % NT == 0)
    c[:, CCOL["scan"]:][:, :N] = 1 - start
    w = np.array(POOLW, np.float32)[(np.arange(2)[:, None] * P + np.arange(P)[None, :]) // 64]
    c[:, CCOL["wcol"]:][:, :2] = (1 / w).T
    for i in range(2):
        c[:, CCOL["cnt"] + 16 * i:][:, :16] = 1 / np.minimum(np.arange(16)[None, :] + 1, w[i][:, None])
    c[:, CCOL["eps"]:][:, :3] = (1e-6, 1e-5, 64e-5)
    c[:, CCOL["idc"]:][:, :C] = s % C == t[:, :C]
    s, t = s[:32], t[:, :32]
    c[:32, CCOL["smask"]:][:, :32] = (s // NT == t // NT) & (s < t)
    c[:32, CCOL["smask"] + 32:][:, :32] = (s // NT == t // NT) & (s <= t)
    c[:32, CCOL["bsel"]:][:, :8] = s // NT == np.arange(8)[None, :]
    return c


def program(nc, a, o):
    with ExitStack() as ctx:
        sems = {}

        def S(name):
            if name not in sems:
                sems[name] = ctx.enter_context(nc.semaphore(name))
            return sems[name]

        def sb(name, shape, dt=F32):
            return ctx.enter_context(nc.sbuf_tensor(name, [P] + shape, dt))

        x = sb("x", [KD, N])
        xh, xl = sb("xh", [KD, N], F32R), sb("xl", [KD, N], F32R)
        RAW, SPL = 2, 4
        raw = sb("raw", [RAW, KD, P])
        wh, wl = sb("wh", [SPL, KD, P], F32R), sb("wl", [SPL, KD, P], F32R)
        con = sb("con", [NCON])
        par = sb("par", [NPAR])
        lora_w = sb("lora_w", [LORAW])
        dwbd = sb("dwbd", [2, P])
        onemka = sb("onemka", [2])
        rb = sb("rb", [N])
        st = sb("st", [3, 24])
        ARENA = nc.sbuf_base + 31 & ~31
        END = nc.sbuf_usable_end
        spots = {"ffn": ARENA, "mix": ARENA}

        def at(space, name, shape, dt=F32, offset=None):
            size = 4 * int(np.prod(shape))
            off = spots[space] if offset is None else offset
            if offset is None:
                spots[space] += size + 31 & ~31
            assert off + size <= END, (name, off + size, END)
            return nc.alloc_sbuf_tensor_at(name, [P] + shape, dt, offset=off)

        f = at("ffn", "f", [KD, N])
        hh, hl = at("ffn", "hh", [8, N], F32R), at("ffn", "hl", [8, N], F32R)
        silu = at("ffn", "silu", [2, N])
        h32 = at("ffn", "h32", [2, N])
        sq = at("ffn", "sq", [2, N])
        ssq = at("ffn", "ssq", [N])
        tb3 = at("ffn", "tb3", [3, N])
        tb = tb3[:, 0:2]
        mixf = at("mix", "mixf", [KD, N])
        ar = at("mix", "ar", [2, 2, N])
        bt = at("mix", "bt", [2, N])
        kt = at("mix", "kt", [2, N])
        bh = at("mix", "bh", [2, N])
        kh = at("mix", "kh", [2, N])
        v = at("mix", "v", [2, N])
        gg = at("mix", "gg", [2, N])
        bo = at("mix", "bo", [2, N])
        pend = at("mix", "pend", [2, 16])
        ya, yb, yd = mixf[:, 0:2, :], mixf[:, 2:4, :], mixf[:, 6:8, :]
        tmp2 = mixf[:, 4:6, :]
        W0 = spots["mix"]
        pc = at("mix", "pc", [7, 513 + 5 * NB])
        lo = at("mix", "lo", [N])
        lo2 = at("mix", "lo2", [N])
        kp = at("mix", "kp", [2, N])
        ll = at("mix", "ll", [2, N])
        ub = at("mix", "ub", [2, 514 + 6 * NB])
        DW = 527 + 19 * NB
        db = at("mix", "db", [2, DW], offset=W0)
        d1 = at("mix", "d1", [2, DW], offset=W0 + (8 * DW + 31 & ~31))
        d2 = at("mix", "d2", [2, DW], offset=W0 + 2 * (8 * DW + 31 & ~31))
        assert W0 + 3 * (8 * DW + 31 & ~31) <= W0 + 4 * 7 * (513 + 5 * NB) + 8 * N
        stap = at("mix", "stap", [NSTA])
        so = at("mix", "so", [64])
        spots["wkv"] = W0
        rhs = at("wkv", "rhs", [2, 2, P])
        bkv = at("wkv", "bkv", [2, 5, P])
        nak = at("wkv", "nak", [2, 2, 2, 2, P])
        nrb, akr = nak[:, :, :, 0], nak[:, :, :, 1]
        nlv = at("wkv", "nlv", [2, 2, 2, P])
        tt_ = at("wkv", "tt", [2, 2, 2, P])
        xx = at("wkv", "xx", [2, 2, P])
        tu = at("wkv", "tu", [2, 2, P])
        qt = at("wkv", "qt", [2, P])
        mt = at("wkv", "mt", [2, 2, C])
        sst = at("wkv", "sst", [2, NC_, C])
        s0t = at("wkv", "s0t", [2, NB, C])
        smt = at("wkv", "smt", [2, NB, C])
        s1t = smt
        zb = at("wkv", "zb", [2, 542 + 34 * NB])
        ex3 = (tmp2[:, 0, 0:NB * C], tmp2[:, 1, 0:NB * C], nlv[:, 0].rearrange("p a b c -> p (a b c)"))

        ps = ctx.enter_context(nc.psum_tensor("ps", [P, 8, 512], F32))

        def pair(n):
            return ps[:, 2 * n:2 * n + 2, 0:H]

        def C_(name, n=P, k=0, rows=P):
            return con[0:rows, CCOL[name] + k:CCOL[name] + k + n]

        def par_(name, k):
            return par[:, PCOL[name] + k:PCOL[name] + k + 1]

        ident, ones, hb = C_("ident"), C_("ones"), C_("hb")
        hsel = hb.rearrange("p (h c) -> p h c", h=2)[:, :, 0]

        def halves(t):
            return t.rearrange("p (a b) -> p a b", a=2)

        block = ctx.enter_context(nc.Block())

        FFN_UNITS = sum(2 * nf + KD for _, nf in GROUPS)
        MIX0 = FFN_UNITS
        FFN2 = MIX0 + NIN + KD + 1
        assert FFN_UNITS % 4 == 0 and FFN2 % 4 == 0
        SKIP = FFN2 - 1

        def load(sp, u0, i, s, src, k):
            sp.wait_ge(S("w_lo"), i * 4 + (u0 + s + 1))
            sp.dma_start(raw[:, s % RAW, 0:k, :].rearrange("p k n -> p (k n)"), src).then_inc(S(f"w_full{s % RAW}"), 16)

        def split_hi(act, u0, i, s, k, skip=0):
            loads = (u0 + s) // RAW + 1 - (SKIP % RAW == s % RAW and u0 + s > SKIP)
            act.wait_ge(S(f"w_full{s % RAW}"), i * 32 + 16 * loads)
            act.wait_ge(S("unit_done"), i * 4 + (u0 + s + 1))
            act.activation(wh[:, s % 4, 0:k, :], raw[:, s % RAW, 0:k, :], ACT.Copy
                           ).then_inc(S("w_hi"), 1 + skip)

        def split_lo(dve, u0, i, s, k, skip=0):
            dve.wait_ge(S("w_hi"), i * 4 + (u0 + s + 1))
            dve.tensor_tensor(wl[:, s % 4, 0:k, :], raw[:, s % RAW, 0:k, :], wh[:, s % 4, 0:k, :].bitcast(F32), SUB
                              ).then_inc(S("w_lo"), 1 + skip)

        def split_ready(pe, u0, i, s):
            pe.wait_ge(S("w_lo"), i * 4 + (u0 + s + 1 + RAW))

        def unit_done(eng, u0, i, s):
            eng.wait_ge(S("unit_done"), i * 4 + (u0 + s + 1 + SPL))

        def product(pe, out, s, order, right_h, right_l, before=None, opens=True, closes=True):
            for j in order:
                if before:
                    before(j)
                for n in range(2):
                    col = slice(n * H, n * H + H)
                    pe.matmul(out[:, n], wh[:, s, j], right_h[:, j, col], start=opens and j == order[0], stop=False)
                    pe.matmul(out[:, n], wh[:, s, j], right_l[:, j, col], start=False, stop=False)
                    last = pe.matmul(out[:, n], wl[:, s, j], right_h[:, j, col], start=False, stop=closes and j == order[-1])
            return last

        def tok(t):
            return slice(128 * t, 128 * t + 128) if t < 4 else slice(N - 128, N)

        def sums_pe(pe, n):
            pe.wait_ge(S("n_ssq"), n + 1)
            for t in range(5):
                m = pe.matmul(ps[:, 6, t:t + 1], ssq[:, tok(t)], ones[:, 0:1], start=True, stop=True)
            m.then_inc(S("n_sum"), 1)

        def spread_root_pe(pe, n):
            pe.wait_ge(S("n_rec"), n + 1)
            for t in range(4):
                pe.matmul(ps[:, 7, tok(t)], st[:, 2, t:t + 1].to_broadcast([P, P]), ident, start=True, stop=True)
            pe.matmul(ps[:, 6, 0:NS], st[:, 2, 4:5].to_broadcast([P, P]), ident[:, P - NS:P],
                      start=True, stop=True).then_inc(S("n_spread"), 1)

        def stats_pe(pe, n):
            sums_pe(pe, n)
            spread_root_pe(pe, n)

        def root_act(act, n):
            if n in (1, 5):
                act.wait_ge(S("n_var"), n // 4 + 1)
                act.activation(st[:, 1, 0:5], st[:, 0, 0:5], ACT.Sqrt).then_inc(S("n_root"), 1)
            else:
                act.wait_ge(S("n_sum"), n + 1)
                act.activation(st[:, 1, 0:5], ps[:, 6, 0:5], ACT.Sqrt, scale=1.0 / D, bias=C_("eps", 1)
                               ).then_inc(S("n_root"), 1)

        def stats_act(act, n):
            root_act(act, n)
            rb_act(act, n)

        def rb_act(act, n):
            act.wait_ge(S("n_spread"), n + 1)
            scale = 0.5 if n in (1, 5) else 1.0
            act.activation(rb[:, 0:512], ps[:, 7, 0:512], ACT.Copy, scale=scale)
            act.activation(rb[:, 512:N], ps[:, 6, 0:NS], ACT.Copy, scale=scale).then_inc(S("n_rb"), 1)

        def stats_dve(dve, n):
            if n in (1, 5):
                dve.wait_ge(S("n_sum"), n + 1)
                dve.wait_ge(S("n_late"), n // 4 + 1)
                dve.scalar_tensor_tensor(st[:, 0, 0:5], ps[:, 6, 0:5], 1.0 / D, st[:, 0, 8:13], MUL, ADD).then_inc(S("n_var"), 1)
            dve.wait_ge(S("n_root"), n + 1)
            if n in (0, 4):
                dve.scalar_tensor_tensor(st[:, 0, 8:13], st[:, 1, 0:5], 1e-6, st[:, 1, 0:5], MUL, MUL).then_inc(S("n_late"), 1)
            dve.reciprocal(st[:, 2, 0:5], st[:, 1, 0:5]).then_inc(S("n_rec"), 1)

        def squares_act(act, n, k, src):
            if k == 0:
                act.activation(ssq[:], src, ACT.Square).then_inc(S("n_sq"), 1)
            else:
                act.wait_ge(S("n_add"), 6 * n + max(k - 2, 0))
                act.activation(sq[:, k % 2], src, ACT.Square).then_inc(S("n_sq"), 1)

        def squares_dve(dve, n, k):
            dve.wait_ge(S("n_sq"), 8 * n + k + 1)
            dve.wait_ge(S("n_add"), 6 * n + k - 1)
            dve.tensor_tensor(ssq[:], ssq[:], sq[:, k % 2], ADD).then_inc(S("n_ssq" if k == KD - 1 else "n_add"), 1)

        def x_wait(eng, n, k):
            if n == 0:
                eng.wait_ge(S(f"in_x{k}"), 16)
            else:
                eng.wait_ge(S("x_ready"), KD * (n // 2 - 1) + k + 1)

        def late_act(act, n):
            for k in range(KD):
                x_wait(act, n, k)
                act.activation(xh[:, k], x[:, k], ACT.Copy, scale=par_(f"g{n}", k)).then_inc(S("n_xh"), 1)

        def late_squares_act(act, n):
            for k in range(KD):
                squares_act(act, n, k, x[:, k])

        def late_dve(dve, n, k):
            dve.wait_ge(S("n_xh"), KD * (n // 2) + k + 1)
            dve.scalar_tensor_tensor(xl[:, k], x[:, k], par_(f"g{n}", k), xh[:, k].bitcast(F32), MUL, SUB
                                     ).then_inc(S("n_xl"), 1)

        def late_squares_dve(dve, n):
            for k in range(1, KD):
                squares_dve(dve, n, k)

        def by_dve(n, k):
            return n == 5 and k in (2, 5, 7)

        def post_pool(pool, n):
            b = KD * (n // 2)
            for k in range(KD):
                if by_dve(n, k):
                    continue
                pool.wait_ge(S("n_t"), b + k + 1)
                pool.tensor_tensor(x[:, k], x[:, k], tb3[:, k % 3] if n == 5 else tb[:, k % 2], ADD).then_inc(S("x_ready"), 1)

        def post_dve(dve, n):
            b = KD * (n // 2)
            stats_dve(dve, n)
            dve.wait_ge(S("n_rb"), n + 1)
            for k in range(KD if n == 5 else 0):
                if k >= 3 and by_dve(n, k - 3):
                    dve.wait_ge(S("x_last"), sum(by_dve(n, j) for j in range(k - 2)))
                elif k >= 3:
                    dve.wait_ge(S("x_ready"), b + sum(not by_dve(n, j) for j in range(k - 2)))
                dve.scalar_tensor_tensor(tb3[:, k % 3], f[:, k], par_(f"g{n}", k), rb[:], MUL, MUL).then_inc(S("n_t"), 1)
                if by_dve(n, k):
                    dve.wait_ge(S("n_t"), b + k + 1)
                    dve.tensor_tensor(x[:, k], x[:, k], tb3[:, k % 3], ADD).then_inc(S("x_last"), 1)
            for k in range(KD + 2 if n < 5 else 0):
                if k < KD:
                    if k >= 2:
                        dve.wait_ge(S("x_ready"), b + k - 1)
                    dve.scalar_tensor_tensor(tb[:, k % 2], f[:, k], par_(f"g{n}", k), rb[:], MUL, MUL
                                             ).then_inc(S("n_t"), 1)
                if k >= 2 and n < 5:
                    late_dve(dve, n + 1, k - 2)

        def ffn_sp(sp, q, u0):
            u = u0
            for g, (f0, nf) in enumerate(GROUPS):
                with sp.Fori(0, nf // 2) as i:
                    for s in range(4):
                        load(sp, u, i, s, a[f"w_gu{q}"][bass.ds(i * 4 + (2 * f0 + s), 1)].rearrange("a p n -> p (a n)"), KD)
                u += 2 * nf
                with sp.Fori(0, 2) as i:
                    for s in range(4):
                        load(sp, u, i, s, a[f"w_d{q}_{g}"][bass.ds(i * 4 + s, 1)].rearrange("a p n -> p (a n)"), nf)
                u += KD

        def ffn_pe(pe, q, u0, n):
            u, dn = u0, 0

            def input_ready(j):
                pe.wait_ge(S("n_xl"), KD * (n // 2) + j + 1)

            for s in range(4):
                split_ready(pe, u, 0, s)
                if s == 3:
                    pe.wait_ge(S("n_rb"), n + 1)
                product(pe, pair(s), s, range(KD), xh, xl, input_ready if s == 0 else None).then_inc(S("unit_done"), 1)
                if s == 1:
                    pe.wait_ge(S("in_con"), 48)
                    sums_pe(pe, n)
                if s == 2:
                    spread_root_pe(pe, n)
            for g, (f0, nf) in enumerate(GROUPS):
                with pe.Fori(0 if g else 1, nf // 2) as i:
                    for s in range(4):
                        split_ready(pe, u, i, s)
                        pe.wait_ge(S(f"h_mul{q}"), i * 2 + (f0 + s // 2 + 1))
                        pe.wait_ge(S(f"d_out{q}"), dn + s + 1)
                        product(pe, pair(s), s, range(KD), xh, xl).then_inc(S("unit_done"), 1)
                u += 2 * nf

                def hidden_ready(j):
                    pe.wait_ge(S(f"h_lo{q}"), f0 + j + 1 + 2)

                with pe.Fori(0, 2) as i:
                    for s in range(4):
                        split_ready(pe, u, i, s)
                        pe.wait_ge(S(f"h_mul{q}"), f0 + nf + 2 - (s < 2))
                        pe.wait_ge(S(f"d_out{q}"), i * 4 + (dn + s + 1))
                        product(pe, pair(s), s, range(nf), hh, hl, hidden_ready if s == 0 else None
                                ).then_inc(S("unit_done"), 1)
                u += KD
                dn += KD

        def silu_act(act, q, i, f0, s):
            act.wait_ge(S(f"gate{q}"), i * 2 + (f0 + s + 1))
            act.activation(silu[:, s % 2], silu[:, s % 2], ACT.Silu).then_inc(S(f"silu{q}"), 1)

        def hidden_dve(dve, q, u, i, f0, s):
            unit_done(dve, u, i, 2 * s)
            dve.wait_ge(S(f"h_mul{q}"), i * 2 + (f0 + s + 1))
            dve.wait_ge(S("n_rb"), 5 * q if q else 1)
            dve.tensor_tensor(halves(silu[:, s % 2]), pair(2 * (s % 2)), halves(rb[:]), MUL).then_inc(S(f"gate{q}"), 1)
            unit_done(dve, u, i, 2 * s + 1)
            dve.wait_ge(S(f"silu{q}"), i * 2 + (f0 + s + 1))
            dve.wait_ge(S(f"h_lo{q}"), i * 2 + (f0 + s + 1))
            dve.tensor_tensor(halves(h32[:, s % 2]), halves(silu[:, s % 2]), pair(2 * (s % 2) + 1), MUL
                              ).then_inc(S(f"h_mul{q}"), 1)
            dve.wait_ge(S(f"h_mul{q}"), i * 2 + (f0 + s + 1 + 2))
            j = bass.ds(i * 2 + s, 1) if not isinstance(i, int) else slice(s, s + 1)
            one = "p a n -> p (a n)"
            dve.tensor_copy(hh[:, j].rearrange(one), h32[:, s % 2]).then_inc(S(f"h_hi{q}"), 1)
            dve.wait_ge(S(f"h_hi{q}"), i * 2 + (f0 + s + 1))
            dve.tensor_tensor(hl[:, j].rearrange(one), h32[:, s % 2], hh[:, j].rearrange(one).bitcast(F32), SUB
                              ).then_inc(S(f"h_lo{q}"), 1)

        def down_dve(dve, q, u, g, d, n):
            unit_done(dve, u, 0, d)
            if g == 0:
                dve.tensor_copy(halves(f[:, d]), pair(d % 4)).then_inc(S(f"d_out{q}"), 1)
            else:
                dve.wait_ge(S(f"d_out{q}"), 4 + KD * (g - 1) + d + 1)
                dve.tensor_tensor(halves(f[:, d]), pair(d % 4), halves(f[:, d]), ADD).then_inc(S(f"d_out{q}"), 1)
            if g == 2 and d >= 2:
                squares_dve(dve, n, d - 1)

        def down_act(act, q, g, d, n):
            if g == 2:
                act.wait_ge(S(f"d_out{q}"), 4 + 2 * KD + d + 1)
                squares_act(act, n, d, f[:, d])

        def ffn_act(act, q, u0, n, nxt, nk):
            u = u0
            late_squares_act(act, n - 1)
            for g, (f0, nf) in enumerate(GROUPS):
                for s in range(4):
                    if not (g == 0 and s < 2):
                        split_hi(act, u, 0, s, KD)
                    if g == 0 and s == 3:
                        stats_act(act, n - 1)
                silu_act(act, q, 0, f0, 0)
                with act.Fori(0, nf // 2 - 1) as i:
                    for s in range(4):
                        split_hi(act, u + 4, i, s, KD)
                        if s % 2:
                            silu_act(act, q, i, f0, 1 + s // 2)
                u += 2 * nf
                for s in range(KD):
                    split_hi(act, u, 0, s, nf)
                    if s == 1:
                        silu_act(act, q, 0, f0, nf - 1)
                    if s >= 2:
                        down_act(act, q, g, s - 2, n)
                u += KD
                if g == 2:
                    for s in range(2):
                        if nxt is not None:
                            split_hi(act, nxt, 0, s, nk)
                        down_act(act, q, g, KD - 2 + s, n)

        def ffn_dve(dve, q, u0, n, nxt, nk):
            u = u0
            late_squares_dve(dve, n - 1)
            for g, (f0, nf) in enumerate(GROUPS):
                for s in range(4):
                    if not (g == 0 and s < 2):
                        split_lo(dve, u, 0, s, KD)
                    if g == 0 and s == 3:
                        stats_dve(dve, n - 1)
                    if g and s < 2:
                        down_dve(dve, q, u - KD, g - 1, KD - 2 + s, n)
                hidden_dve(dve, q, u, 0, f0, 0)
                with dve.Fori(0, nf // 2 - 1) as i:
                    for s in range(4):
                        split_lo(dve, u + 4, i, s, KD)
                        if s % 2:
                            hidden_dve(dve, q, u, i, f0, 1 + s // 2)
                u += 2 * nf
                for s in range(KD):
                    split_lo(dve, u, 0, s, nf)
                    if s == 1:
                        hidden_dve(dve, q, u - 2 * nf, 0, f0, nf - 1)
                    if s >= 2:
                        down_dve(dve, q, u, g, s - 2, n)
                u += KD
                if g == 2:
                    for s in range(2):
                        if nxt is not None:
                            split_lo(dve, nxt, 0, s, nk)
                        down_dve(dve, q, u - KD, g, KD - 2 + s, n)
                    squares_dve(dve, n, KD - 1)

        def in_pair(m):
            return 2 if m == 2 else m % 2

        OUT_R = 9
        OUT0 = NIN

        def in_out(eng, m):
            eng.wait_ge(S("in_dve"), m + 1)

        def steps(t, at_, pad):
            return t[..., at_:at_ + NB * (pad + NT)].rearrange("p (b c) -> p b c", c=pad + NT)[:, :, pad:]

        def comp(t):
            return t.rearrange("p (b c) -> p b c", c=NT)

        def pieces(dst, m, at_, pad):
            src = pair(in_pair(m))
            return ((dst[:, pad:pad + H], src[:, 0], rb[:, 0:H]), (dst[:, pad + H:pad + NP_], src[:, 1, 0:HP], rb[:, H:NP_]),
                    (steps(dst, at_, pad), comp(src[:, 1, HP:H]), comp(rb[:, NP_:N])))

        class Chain:

            def __init__(self, eng, name):
                self.eng, self.name, self.n = eng, name, 0

            def __call__(self, ins):
                self.n += 1
                ins.then_inc(S(self.name), 1)
                self.eng.wait_ge(S(self.name), self.n)

        def mixer_sp(sp):
            for m in range(NIN):
                load(sp, MIX0, 0, m, a["w_in"][m], KD)
            sp.wait_ge(S("so"), 1)
            sp.dma_start(o["o_shift"], so[:, 0:7 * (1 + NB)].rearrange("p (i c) -> p i c", i=7)).then_inc(S("out_r"), 16)
            sp.wait_ge(S("au"), 2)
            us = ub[:, :, 514:].rearrange("p i (b c) -> p i b c", c=6)
            for i in range(2):
                sp.dma_start(o["o_a"][:, i, 0:2], ub[:, i, 512:514]).then_inc(S("out_r"), 16)
                sp.dma_start(o["o_a"][:, i, 2:].rearrange("p (b c) -> p b c", c=2), us[:, i, :, 4:]).then_inc(S("out_r"), 16)
            in_out(sp, DD1)
            ds_ = db[:, :, 527:].rearrange("p i (b c) -> p i b c", c=19)
            for i in range(2):
                sp.dma_start(o["o_d"][:, i, 0:15], db[:, i, 512:527]).then_inc(S("out_r"), 16)
                sp.dma_start(o["o_d"][:, i, 15:].rearrange("p (b c) -> p b c", c=15), ds_[:, i, :, 4:]).then_inc(S("out_r"), 16)
            for m in range(4):
                load(sp, MIX0, 0, OUT0 + m, a["w_out"][m], KD)
            sp.wait_ge(S("out_r"), OUT_R * 16)
            sp.wait_ge(S("diff"), 2)
            sp.dma_start(s0t[:], a["s0"]).then_inc(S("in_s0"), 16)
            sp.wait_ge(S("glu"), 2)
            zs = zb[:, :, 542:].rearrange("p i (b c) -> p i b c", c=34)
            for i in range(2):
                sp.dma_start(o["o_b"][:, i, 0:30], zb[:, i, 512:542]).then_inc(S("out"), 16)
                sp.dma_start(o["o_b"][:, i, 30:].rearrange("p (b c) -> p b c", c=30), zs[:, i, :, 4:]).then_inc(S("out"), 16)
            for m in range(4, KD):
                load(sp, MIX0, 0, OUT0 + m, a["w_out"][m], KD)
            sp.wait_ge(S("r_end"), 1)
            sp.dma_start(o["o_sp"], sst[:, :, NC_ - 1]).then_inc(S("out"), 16)
            sp.wait_ge(S("q_s1"), 2)
            sp.dma_start(o["o_ss"], s1t[:]).then_inc(S("out"), 16)

        def mixer_pool(pool):
            pool.wait_ge(S("in_sta"), 16)
            pool.wait_ge(S("n_rb"), 3)
            z = lambda name, k, c: stap[:, SCOL[name]:SCOL[name] + 2 * NB * c].rearrange("p (i b c) -> p i b c", i=2, c=c)[:, k]
            pool.memset(pc[:, :, 0:1], 0.0)
            pool.tensor_copy(pc[:, :, 513:].rearrange("p i (b c) -> p i b c", c=5)[:, :, :, 0],
                             stap[:, 0:7 * NB].rearrange("p (i b) -> p i b", b=NB)).then_inc(S("pads"), 1)
            pool.memset(ub[:, :, 0:2], 0.0)
            pool.memset(zb[:, :, 0:30], 0.0)
            for i in range(2):
                pool.tensor_copy(ub[:, i, 514:].rearrange("p (b c) -> p b c", c=6)[:, :, 0:2], z("u", i, 2))
                last = pool.tensor_copy(zb[:, i, 542:].rearrange("p (b c) -> p b c", c=34)[:, :, 0:30], z("z", i, 30))
            last.then_inc(S("pads"), 1)
            in_out(pool, V1)
            s3 = so[:, 0:7 * (1 + NB)].rearrange("p (i c) -> p i c", i=7)
            pool.tensor_copy(s3[:, :, 0:1], pc[:, :, 512:513])
            pool.tensor_copy(s3[:, :, 1:], pc[:, :, 513:].rearrange("p i (b c) -> p i b c", c=5)[:, :, :, 4]).then_inc(S("so"), 1)
            pool.wait_ge(S("xm"), 7)
            pool.wait_ge(S("so"), 1)
            pool.memset(db[:, :, 0:15], 0.0)
            for i in range(2):
                last = pool.tensor_copy(db[:, i, 527:].rearrange("p (b c) -> p b c", c=19)[:, :, 0:15], z("d", i, 15))
            last.then_inc(S("pads"), 1)
            in_out(pool, DD1)
            pool.wait_ge(S("lora"), 6)
            pool.wait_ge(S("pads"), 3)
            pool.tensor_tensor(d1[:, :, 1:], db[:, :, 1:], db[:, :, :-1], ADD).then_inc(S("pool_d"), 1)
            pool.wait_ge(S("pool_d"), 1)
            pool.tensor_tensor(d2[:, :, 3:], d1[:, :, 3:], d1[:, :, 1:-2], ADD).then_inc(S("pool_d"), 1)
            pool.wait_ge(S("pool_d"), 2)
            pool.tensor_tensor(d1[:, 1, 7:], d2[:, 1, 7:], d2[:, 1, 3:-4], ADD).then_inc(S("pool_d"), 1)
            pool.wait_ge(S("pool_d"), 3)
            pool.tensor_tensor(d2[64:P, 1, 15:], d1[64:P, 1, 15:], d1[64:P, 1, 7:-8], ADD).then_inc(S("pool_d"), 1)
            for t in range(4):
                for l in range(6):
                    for p in range(2):
                        pool.wait_ge(S("r2"), 2 * t + p + 1)
                        if l >= 2:
                            wait_job(pool, t, 2 * l, p)
                        elif t:
                            wait_job(pool, t - 1, 10 + 2 * l, p)
                        pool.tensor_tensor(nlv[:, l % 2, p], nrb[:, p, :, 0],
                                           C_("lev", k=l * P).unsqueeze(1).to_broadcast([P, 2, P]), MUL
                                           ).then_inc(S("lev"), 1)
            for l in range(2):
                for p in range(2):
                    pool.wait_ge(S("q2"), p + 1)
                    wait_job(pool, 3, 10 + 2 * l, p)
                    pool.tensor_tensor(nlv[0:32, l, p, :, 0:32], nrb[0:32, p, :, 0, 0:32],
                                       C_("lev", 32, l * P, 32).unsqueeze(1).to_broadcast([32, 2, 32]), MUL
                                       ).then_inc(S("lev"), 1)

        NSTAGE = 20

        def wait_job(eng, t, s, p):
            eng.wait_ge(S("job"), (t * NSTAGE + s) * 2 + p + 1)

        def bank(s, p):
            return ps[:, (2 * s + p) % 8]

        def bank_free(pe, t, s, p):
            if s >= 4:
                pe.wait_ge(S(f"r{s - 4}"), 2 * t + p + 1)
            elif t:
                pe.wait_ge(S(f"r{NSTAGE + s - 4}"), 2 * (t - 1) + p + 1)

        def wkv_pe(pe, t):
            tok_ = slice(P * t, P * t + P)
            hp = [slice(0, 64), slice(64, P)]

            def job(s, p):
                bank_free(pe, t, s, p)
                return bank(s, p)

            for p in range(2):
                b = job(0, p)
                for k, src in enumerate((v[:, p], bh[:, p], kh[:, p], ar[:, p, 0])):
                    last = pe.transpose(b[:, P * k:P * k + P], src[:, tok_], ident)
                last.then_inc(S("job"), 1)
            for h in range(2):
                for p in range(2):
                    b = job(1 + h, p)
                    for k, left in enumerate((bt, kt)):
                        last = pe.matmul(b[:, 256 * k:256 * k + 256].rearrange("p (a b) -> p a b", a=2), left[hp[h], p, tok_],
                                         ar[hp[h], p, :, tok_], start=True, stop=True)
                    last.then_inc(S("job"), 1)
            for p in range(2):
                b = job(3, p)
                pe.wait_ge(S("lev"), t * 12 + p + 1)
                for h in range(2):
                    last = pe.matmul(b[:, P * h:P * h + P], nlv[:, 0, p, h], ident, start=True, stop=True)
                last.then_inc(S("job"), 1)
            for l in range(1, 6):
                for p in range(2):
                    b = job(2 + 2 * l, p)
                    pe.wait_ge(S("lev"), t * 12 + 2 * l + p + 1)
                    pe.wait_ge(S(f"r{1 + 2 * l}"), 2 * t + p + 1)
                    for h in range(2):
                        last = pe.matmul(b[:, P * h:P * h + P], nlv[:, l % 2, p, h], tt_[:, p, 0, h], start=True, stop=True)
                    last.then_inc(S("job"), 1)
                for p in range(2):
                    b = job(3 + 2 * l, p)
                    pe.wait_ge(S(f"r{2 + 2 * l}"), 2 * t + p + 1)
                    for h in range(2):
                        if l < 5:
                            pe.matmul(b[:, P * h:P * h + P], tt_[:, p, 1, h], xx[:, p, h], start=True, stop=True)
                        last = pe.matmul(b[:, 256 + P * h:256 + P * h + P], xx[:, p, h], tt_[:, p, 1, h], start=True, stop=True)
                    last.then_inc(S("job"), 1)
            for p in range(2):
                b = job(14, p)
                pe.wait_ge(S("r2"), 2 * t + p + 1)
                pe.wait_ge(S("r0"), 2 * t + p + 1)
                for h in range(2):
                    last = pe.matmul(b[:, C * h:C * h + C], akr[:, p, h, 0], bkv[:, p, 0, C * h:C * h + C], start=True, stop=True)
                last.then_inc(S("job"), 1)
            for p in range(2):
                b = job(15, p)
                pe.wait_ge(S("r13"), 2 * t + p + 1)
                pe.wait_ge(S("r14"), 2 * t + p + 1)
                for h in range(2):
                    last = pe.matmul(b[:, P * h:P * h + P], tt_[:, p, 1, h], rhs[:, p, h], start=True, stop=True)
                last.then_inc(S("job"), 1)
            for p in range(2):
                b = job(16, p)
                pe.wait_ge(S("r15"), 2 * t + p + 1)
                for h in range(2):
                    last = pe.matmul(b[hp[h], 0:P], tu[:, p, h, 0:C], nrb[:, p, h, 1], start=True, stop=True)
                for h in range(2):
                    last = pe.matmul(b[hp[h], P:2 * P].rearrange("p (c n) -> p c n", c=2), tu[:, p, h, 0:C],
                                     bkv[:, p, 1:5, C * h:C * h + C].rearrange("p (c k) n -> p c k n", c=2)[:, :, 0],
                                     start=True, stop=True)
                last.then_inc(S("job"), 1)
            for c in range(2):
                ch = 2 * t + c
                for p in range(2):
                    b = job(17 + c, p)
                    for h in range(2):
                        out = b[hp[h], 0:C]
                        pe.matmul(out, bkv[:, p, 1 + 2 * c, C * h:C * h + C], tu[:, p, h, C:P], start=True, stop=False)
                        last = pe.matmul(out, bkv[:, p, 2 + 2 * c, C * h:C * h + C], bkv[:, p, 0, C * h:C * h + C],
                                         start=False, stop=ch == 0)
                        if ch:
                            if h == 0:
                                pe.wait_ge(S("r16"), 2 * t + p + 1)
                                wait_state(pe, ch - 1, p)
                            last = pe.matmul(out, mt[hp[h], p, c], sst[hp[h], p, ch - 1], start=False, stop=True)
                    last.then_inc(S("job"), 1)
            for p in range(2):
                b = job(19, p)
                pe.wait_ge(S("r16"), 2 * t + p + 1)
                for h in range(2):
                    out = b[hp[h], 0:P]
                    pe.matmul(out, tu[:, p, h, C:P], nrb[:, p, h, 1], start=True, stop=False)
                    last = pe.matmul(out, bkv[:, p, 0, C * h:C * h + C], akr[:, p, h, 1], start=False, stop=False)
                    for c in range(2):
                        ch = 2 * t + c
                        if ch:
                            wait_state(pe, ch - 1, p)
                            cols = slice(C * c, C * c + C)
                            last = pe.matmul(b[hp[h], cols], sst[hp[h], p, ch - 1], qt[hp[h], p, cols], start=False, stop=c == 1)
                last.then_inc(S("job"), 1)

        def wait_state(pe, ch, p):
            pe.wait_ge(S(f"r{17 + ch % 2}"), 2 * (ch // 2) + p + 1)

        def wkv_act(act, t):
            def done(s, p):
                wait_job(act, t, s, p)
                return bank(s, p)

            for p in range(2):
                b = done(0, p)
                if t:
                    wait_job(act, t - 1, 19, p)
                act.activation(bkv[:, p, 0], b[:, 0:P], ACT.Copy)
                for c in range(2):
                    act.activation(bkv[:, p, 1 + 2 * c:3 + 2 * c], b[:, P:3 * P].rearrange("p (k c) -> p k c", k=2), ACT.Copy,
                                   scale=hb[:, C * c:C * c + 1])
                act.activation(rhs[:, p, :, 0:C], b[:, 3 * P:].rearrange("p (h c) -> p h c", h=2), ACT.Copy).then_inc(S("r0"), 1)
            for l in range(1, 6):
                for p in range(2):
                    s = 2 + 2 * l
                    b = done(s, p)
                    if l > 1:
                        wait_job(act, t, s - 1, p)
                    elif t:
                        wait_job(act, t - 1, 13, p)
                    act.activation(xx[:, p], b[:, 0:2 * P].rearrange("p (h c) -> p h c", h=2), ACT.Copy).then_inc(S(f"r{s}"), 1)
            for p in range(2):
                b = done(14, p)
                act.activation(rhs[:, p, :, C:P], b[:, 0:P].rearrange("p (h c) -> p h c", h=2), ACT.Copy).then_inc(S("r14"), 1)
            for p in range(2):
                b = done(15, p)
                act.activation(tu[:, p], b[:, 0:2 * P].rearrange("p (h c) -> p h c", h=2), ACT.Copy).then_inc(S("r15"), 1)
            for c in range(2):
                for p in range(2):
                    b = done(17 + c, p)
                    act.activation(sst[:, p, 2 * t + c], b[:, 0:C], ACT.Copy).then_inc(S(f"r{17 + c}"), 1)
            for p in range(2):
                b = done(19, p)
                act.activation(yc[:, p, P * t:P * t + P], b[:, 0:P], ACT.Copy).then_inc(S("r19"), 1)
            if t == 3:
                act.wait_ge(S("r18"), 8)
                act.sem_inc(S("r_end"), 1)

        yc = ar[:, :, 0, :]

        def wkv_dve(dve, t, fill):
            tok_ = slice(P * t, P * t + P)

            def done(s, p):
                wait_job(dve, t, s, p)
                return bank(s, p)

            mask = C_("mask", 2 * P).unsqueeze(1).to_broadcast([P, 2, 2 * P])
            for h in range(2):
                for p in range(2):
                    b = done(1 + h, p)
                    if t:
                        wait_job(dve, t - 1, 19, p)
                        dve.wait_ge(S("lev"), (t - 1) * 12 + 10 + p + 1)
                    dve.tensor_tensor(nak[:, p, h].rearrange("p w k c -> p w (k c)"), b.rearrange("p (w c) -> p w c", w=2), mask, MUL
                                      ).then_inc(S(f"r{1 + h}"), 1)
                if h:
                    fill()
            for p in range(2):
                b = done(3, p)
                if t:
                    wait_job(dve, t - 1, 15, p)
                idb = ident.unsqueeze(1).to_broadcast([P, 2, P])
                dve.tensor_tensor(tt_[:, p, 1], nlv[:, 0, p], idb, ADD)
                dve.tensor_tensor(tt_[:, p, 0], b[:, 0:2 * P].rearrange("p (h c) -> p h c", h=2), idb, ADD).then_inc(S("r3"), 1)
            fill()
            for l in range(1, 6):
                for p in range(2):
                    s = 3 + 2 * l
                    b = done(s, p)
                    dve.wait_ge(S(f"r{s - 2}"), 2 * t + p + 1)
                    k = 0 if l < 5 else 1
                    both = tt_[:, p, k:2].rearrange("p k h c -> p (k h c)")
                    dve.tensor_tensor(both, b[:, 256 * k:512], both, ADD).then_inc(S(f"r{s}"), 1)
                fill()
            for p in range(2):
                b = done(16, p)
                if t:
                    wait_job(dve, t - 1, 19, p)
                dve.tensor_tensor(qt[:, p], b[:, 0:P], ar[:, p, 1, tok_], ADD)
                for c in range(2):
                    ch = 2 * t + c
                    last = dve.scalar_tensor_tensor(mt[:, p, c], C_("idc", C), pend[:, p, ch:ch + 1], b[:, P + C * c:P + C * c + C],
                                                    MUL, ADD)
                last.then_inc(S("r16"), 1)
            fill()

        DT = slice(NP_, N)
        QJ = 4 * NSTAGE * 2

        def wait_q(eng, s, p):
            eng.wait_ge(S("job"), QJ + 2 * s + p + 1)

        def q_pe(pe):
            hp = [slice(0, 64), slice(64, P)]

            def job(s, p):
                if s >= 4:
                    pe.wait_ge(S(f"q{s - 4}"), p + 1)
                else:
                    pe.wait_ge(S(f"r{NSTAGE + s - 4}"), 6 + p + 1)
                return bank(s, p)

            for p in range(2):
                b = job(0, p)
                for k, src in enumerate((v[:, p], bh[:, p], kh[:, p], ar[:, p, 0])):
                    last = pe.transpose(b[0:32, P * k:P * k + P], src[:, DT], ident)
                last.then_inc(S("job"), 1)
            for h in range(2):
                for p in range(2):
                    b = job(1 + h, p)
                    for k, left in enumerate((bt, kt)):
                        last = pe.matmul(b[0:32, 64 * k:64 * k + 64].rearrange("p (a b) -> p a b", a=2), left[hp[h], p, DT],
                                         ar[hp[h], p, :, DT], start=True, stop=True)
                    last.then_inc(S("job"), 1)
            for p in range(2):
                b = job(3, p)
                pe.wait_ge(S("lev"), 48 + p + 1)
                for h in range(2):
                    last = pe.matmul(b[0:32, 32 * h:32 * h + 32], nlv[0:32, 0, p, h, 0:32], ident[0:32, 0:32], start=True, stop=True)
                last.then_inc(S("job"), 1)
            job(4, 1)
            pe.wait_ge(S("conv"), 1)
            for p in range(2):
                for n in range(2):
                    last = pe.matmul(pair(0)[:, n], ones, yb[:, p, n * H:n * H + H], start=p == 0, stop=p == 1)
            last.then_inc(S("job"), 2)
            for p in range(2):
                b = job(5, p)
                pe.wait_ge(S("lev"), 50 + p + 1)
                pe.wait_ge(S("q3"), p + 1)
                for h in range(2):
                    last = pe.matmul(b[0:32, 32 * h:32 * h + 32], nlv[0:32, 1, p, h, 0:32], tt_[0:32, p, 0, h, 0:32], start=True, stop=True)
                last.then_inc(S("job"), 1)
            for p in range(2):
                b = job(6, p)
                pe.wait_ge(S("q5"), p + 1)
                for h in range(2):
                    last = pe.matmul(b[0:32, 32 * h:32 * h + 32], xx[0:32, p, h, 0:32], tt_[0:32, p, 1, h, 0:32], start=True, stop=True)
                last.then_inc(S("job"), 1)
            job(7, 1)
            pe.wait_ge(S("b_sq"), 2)
            for t in range(5):
                for p in range(2):
                    last = pe.matmul(ps[:, 6, t:t + 1], tmp2[:, p, tok(t)], ones[:, 0:1], start=p == 0, stop=p == 1)
            last.then_inc(S("job"), 2)
            for p in range(2):
                b = job(8, p)
                pe.wait_ge(S("q2"), p + 1)
                pe.wait_ge(S("q0"), p + 1)
                for h in range(2):
                    last = pe.matmul(b[0:32, C * h:C * h + C], akr[0:32, p, h, 0, 0:32], bkv[0:32, p, 0, C * h:C * h + C], start=True, stop=True)
                last.then_inc(S("job"), 1)
            for p in range(2):
                b = job(9, p)
                pe.wait_ge(S("q6"), p + 1)
                pe.wait_ge(S("q8"), p + 1)
                for h in range(2):
                    last = pe.matmul(b[0:32, P * h:P * h + P], tt_[0:32, p, 1, h, 0:32], rhs[0:32, p, h], start=True, stop=True)
                last.then_inc(S("job"), 1)
            job(10, 1)
            pe.wait_ge(S("b_rec"), 1)
            for t in range(4):
                pe.matmul(ps[:, 4, tok(t)], st[:, 2, t:t + 1].to_broadcast([P, P]), ident, start=True, stop=True)
            pe.matmul(ps[:, 5, 0:NS], st[:, 2, 4:5].to_broadcast([P, P]), ident[:, P - NS:P], start=True, stop=True
                      ).then_inc(S("job"), 2)
            for p in range(2):
                b = job(11, p)
                pe.wait_ge(S("q9"), p + 1)
                for h in range(2):
                    last = pe.matmul(b[hp[h], 0:32], tu[0:32, p, h, 0:C], nrb[0:32, p, h, 1, 0:32], start=True, stop=True)
                last.then_inc(S("job"), 1)
            for p in range(2):
                b12, b13 = job(12, p), job(13, p)
                for h in range(2):
                    pe.wait_ge(S("ex"), 2 * p + h + 1)
                    flat = lambda k: ex3[k][0:32]
                    pe.matmul(b12[hp[h], 0:512], tu[0:32, p, h, 0:C], flat(2), start=True, stop=True)
                    pe.matmul(b13[hp[h], 0:512], bkv[0:32, p, 1, C * h:C * h + C], flat(0), start=True, stop=False)
                    last = pe.matmul(b13[hp[h], 0:512], bkv[0:32, p, 2, C * h:C * h + C], flat(1), start=False, stop=False)
                    last.then_inc(S("ex_used"), 1)
            for p in range(2):
                b13 = bank(13, p)
                pe.wait_ge(S("in_s0"), 16)
                pe.wait_ge(S("q12"), p + 1)
                for h in range(2):
                    for n in range(NB):
                        last = pe.matmul(b13[hp[h], C * n:C * n + C], smt[hp[h], p, n], s0t[hp[h], p, n], start=False, stop=n == NB - 1)
                last.then_inc(S("q_sum"), 1)
            for p in range(2):
                b = job(14, p)
                pe.wait_ge(S("q11"), p + 1)
                for h in range(2):
                    out = b[hp[h], 0:32]
                    pe.matmul(out, tu[0:32, p, h, C:P], nrb[0:32, p, h, 1, 0:32], start=True, stop=False)
                    pe.matmul(out, bkv[0:32, p, 0, C * h:C * h + C], akr[0:32, p, h, 1, 0:32], start=False, stop=False)
                    for n in range(NB):
                        cols = slice(NT * n, NT * n + NT)
                        last = pe.matmul(b[hp[h], cols], s0t[hp[h], p, n], qt[hp[h], p, cols], start=False, stop=n == NB - 1)
                last.then_inc(S("q_sum"), 1)

        def q_act(act):
            def done(s, p):
                wait_q(act, s, p)
                return bank(s, p)

            two = "p (h c) -> p h c"
            for p in range(2):
                b = done(0, p)
                wait_job(act, 3, 19, p)
                act.activation(bkv[0:32, p, 0:3], b[0:32, 0:3 * P].rearrange("p (k c) -> p k c", k=3), ACT.Copy)
                act.activation(rhs[0:32, p, :, 0:C], b[0:32, 3 * P:].rearrange(two, h=2), ACT.Copy).then_inc(S("q0"), 1)
            for p in range(2):
                act.wait_ge(S("b_cen"), p + 1)
                act.activation(tmp2[:, p], yb[:, p], ACT.Square).then_inc(S("b_sq"), 1)
            for p in range(2):
                b = done(5, p)
                act.activation(xx[0:32, p, :, 0:32], b[0:32, 0:64].rearrange(two, h=2), ACT.Copy).then_inc(S("q5"), 1)
            wait_q(act, 7, 1)
            act.activation(st[:, 1, 0:5], ps[:, 6, 0:5], ACT.Sqrt, scale=1.0 / G, bias=C_("eps", 1, 1)).then_inc(S("q7"), 2)
            for p in range(2):
                b = done(8, p)
                act.activation(rhs[0:32, p, :, C:P], b[0:32, 0:P].rearrange(two, h=2), ACT.Copy).then_inc(S("q8"), 1)
            for p in range(2):
                b = done(9, p)
                act.activation(tu[0:32, p], b[0:32, 0:2 * P].rearrange(two, h=2), ACT.Copy).then_inc(S("q9"), 1)
            for p in range(2):
                act.wait_ge(S("b_norm"), p + 1)
                act.activation(yb[:, p], yb[:, p], ACT.Silu, bias=par_("bn", p)).then_inc(S("b_y"), 1)
            for n in (4, 5):
                act.wait_ge(S("b_y"), n - 3)
                split_y_hi(act, n)
            for p in range(2):
                act.wait_ge(S("q_sum"), p + 1)
                act.activation(s1t[:, p].rearrange("p b c -> p (b c)"), bank(13, p), ACT.Copy).then_inc(S("q_s1"), 1)
            for p in range(2):
                act.wait_ge(S("q_sum"), 2 + p + 1)
                act.activation(yc[:, p, DT], bank(14, p)[:, 0:32], ACT.Copy).then_inc(S("q_y"), 1)

        def q_dve(dve):
            def done(s, p):
                wait_q(dve, s, p)
                return bank(s, p)

            mask = C_("smask", 64, rows=32).rearrange("p (k c) -> p k c", k=2)
            for h in range(2):
                for p in range(2):
                    b = done(1 + h, p)
                    wait_job(dve, 3, 19, p)
                    dve.wait_ge(S("lev"), 48)
                    for w in range(2):
                        last = dve.tensor_tensor(nak[0:32, p, h, w, :, 0:32], b[0:32, 64 * w:64 * w + 64].rearrange("p (k c) -> p k c", k=2),
                                                 mask, MUL)
                    last.then_inc(S(f"q{1 + h}"), 1)
            idb = C_("ident", 32, rows=32).unsqueeze(1).to_broadcast([32, 2, 32])
            two = "p (h c) -> p h c"
            for p in range(2):
                b = done(3, p)
                dve.tensor_tensor(tt_[0:32, p, 1, :, 0:32], nlv[0:32, 0, p, :, 0:32], idb, ADD)
                dve.tensor_tensor(tt_[0:32, p, 0, :, 0:32], b[0:32, 0:64].rearrange(two, h=2), idb, ADD).then_inc(S("q3"), 1)
            wait_q(dve, 4, 1)
            for p in range(2):
                dve.scalar_tensor_tensor(halves(yb[:, p]), pair(0), -1.0 / G, halves(yb[:, p]), MUL, ADD).then_inc(S("b_cen"), 1)
            dve.wait_ge(S("b_cen"), 2)
            dve.sem_inc(S("q4"), 2)
            for p in range(2):
                b = done(6, p)
                dve.wait_ge(S("q3"), p + 1)
                t_ = tt_[0:32, p, 1, :, 0:32]
                dve.tensor_tensor(t_, b[0:32, 0:64].rearrange(two, h=2), t_, ADD).then_inc(S("q6"), 1)
            dve.wait_ge(S("q7"), 2)
            dve.reciprocal(st[:, 2, 0:5], st[:, 1, 0:5]).then_inc(S("b_rec"), 1)
            wait_q(dve, 10, 1)
            for p in range(2):
                g = par_("bg", p)
                dve.scalar_tensor_tensor(yb[:, p, 0:NP_], ps[:, 4], g, yb[:, p, 0:NP_], MUL, MUL)
                dve.scalar_tensor_tensor(yb[:, p, DT], ps[:, 5, 0:NS], g, yb[:, p, DT], MUL, MUL).then_inc(S("b_norm"), 1)
            dve.wait_ge(S("b_norm"), 2)
            dve.sem_inc(S("q10"), 2)
            for p in range(2):
                b = done(11, p)
                dve.tensor_tensor(qt[:, p, 0:32], b[:, 0:32], ar[:, p, 1, DT], ADD).then_inc(S("q11"), 1)
            sel = C_("bsel", 8, rows=32).unsqueeze(2).to_broadcast([32, NB, C])
            for p in range(2):
                for h in range(2):
                    if 2 * p + h:
                        dve.wait_ge(S("ex_used"), 2 * p + h)
                    dve.wait_ge(S("q9"), p + 1)
                    for k, src in enumerate((tu[0:32, p, h, C:P], bkv[0:32, p, 0, C * h:C * h + C], bkv[0:32, p, 1, C * h:C * h + C])):
                        last = dve.tensor_tensor(ex3[k][0:32].rearrange("p (b c) -> p b c", c=C), src.unsqueeze(1).to_broadcast([32, NB, C]), sel, MUL)
                    last.then_inc(S("ex"), 1)
            for p in range(2):
                dve.wait_ge(S("ex_used"), 2 * p + 2)
                for n in range(NB):
                    last = dve.scalar_tensor_tensor(smt[:, p, n], C_("idc", C), pend[:, p, NC_ + n:NC_ + n + 1],
                                                    bank(12, p)[:, C * n:C * n + C], MUL, ADD)
                last.then_inc(S("q12"), 1)

        Y_ORDER = (0, 1, 6, 7, 2, 3, 4, 5)
        y32 = (ya[:, 0], ya[:, 1], yb[:, 0], yb[:, 1], mixf[:, 4], mixf[:, 5], yd[:, 0], yd[:, 1])

        def split_y_hi(act, n):
            act.activation(xh[:, Y_ORDER[n]], y32[Y_ORDER[n]], ACT.Copy).then_inc(S("y_hi"), 1)

        def split_y_lo(dve, n):
            dve.wait_ge(S("y_hi"), n + 1)
            k = Y_ORDER[n]
            dve.tensor_tensor(xl[:, k], y32[k], xh[:, k].bitcast(F32), SUB).then_inc(S("y_lo"), 1)

        def mixer_pe(pe):
            A, B = pair(2), pair(3)

            def input_ready(j):
                pe.wait_ge(S("n_xl"), KD + j + 1)

            for m in range(NIN):
                split_ready(pe, MIX0, 0, m)
                if m >= 3:
                    in_out(pe, {3: 1, 4: 0}.get(m, m - 2))
                product(pe, pair(in_pair(m)), m % 4, range(KD), xh, xl, input_ready if m == 0 else None
                        ).then_inc(S("unit_done"), 1)
                if m == 1:
                    sums_pe(pe, 2)
                if m == 2:
                    spread_root_pe(pe, 2)
                if m in (4, 5, 6):
                    rows = (slice(0, 32), slice(32, 64), slice(64, P))[m - 4]
                    in_out(pe, 2)
                    pe.wait_ge(S("n_rb"), 3)
                    for p in range(2):
                        pe.wait_ge(S("lo2"), 1)
                        if m > 4:
                            pe.wait_ge(S("lora_out"), 2 * (m - 4) - 1 + p)
                        for n in range(2):
                            last = pe.matmul((A, B)[p][:, n], lora_w[rows, P * p:P * p + P],
                                             (lo if m == 5 else lo2)[rows, n * H:n * H + H], start=True, stop=True)
                        last.then_inc(S("lora"), 1)
                if m == 7:
                    pe.wait_ge(S("lora_out"), 5)
                    pe.wait_ge(S("kk_sq"), 2)
                    for p in range(2):
                        for t in range(5):
                            c = (p * 5 + t) * 2
                            last = pe.matmul(ps[:, 4, c:c + 2], kt[:, p, tok(t)], hsel, start=True, stop=True)
                    last.then_inc(S("kk_sum"), 1)
                if m == 8:
                    pe.wait_ge(S("kk_rec"), 1)
                    pe.wait_ge(S("lora_out"), 6)
                    for p in range(2):
                        spread_pe(pe, 4 + 2 * p, 5 + 2 * p, p).then_inc(S("kk_spread"), 1)
                if m == 10:
                    for p in range(2):
                        pe.wait_ge(S("kk"), p + 1)
                        pe.wait_ge(S("rk"), p + 1)
                        for n in range(2):
                            last = pe.matmul((A, B)[p][:, n], hb, bo[:, p, n * H:n * H + H], start=True, stop=True)
                        last.then_inc(S("bo_sum"), 1)
                if m == 17:
                    pe.wait_ge(S("bonus"), 2)
                    for p in range(2):
                        pe.wait_ge(S("diff"), p + 1)
                        for n in range(2):
                            last = pe.matmul((A, B)[p][:, n], dwbd[:, p], yd[:, p, n * H:n * H + H], start=True, stop=True)
                        last.then_inc(S("d_map"), 1)
            in_out(pe, BG1)
            pe.wait_ge(S("d_out_y"), 2)
            pe.wait_ge(S("fac"), 2)
            for t in range(4):
                wkv_pe(pe, t)
            q_pe(pe)
            for p in range(2):
                pe.wait_ge(S("q_y"), 2)
                for n in range(2):
                    last = pe.matmul(pair(2 + p)[:, n], hb, yc[:, p, n * H:n * H + H], start=True, stop=True)
                last.then_inc(S("c_mean"), 1)
            early, late = Y_ORDER[:6], Y_ORDER[6:]
            pe.wait_ge(S("q_s1"), 2)
            pe.wait_ge(S("y_lo"), 6)
            split_ready(pe, MIX0, 0, OUT0)
            product(pe, pair(0), OUT0 % 4, early, xh, xl, closes=False)
            pe.wait_ge(S("c_sq"), 2)
            for p in range(2):
                for t in range(5):
                    c = (p * 5 + t) * 2
                    last = pe.matmul(ps[:, 4, c:c + 2], kt[:, p, tok(t)], hsel, start=True, stop=True)
            last.then_inc(S("c_sum"), 1)
            split_ready(pe, MIX0, 0, OUT0 + 1)
            product(pe, pair(1), (OUT0 + 1) % 4, early, xh, xl, closes=False)
            pe.wait_ge(S("c_rec"), 1)
            for p in range(2):
                spread_pe(pe, 4 + 2 * p, 5 + 2 * p, p).then_inc(S("c_spread"), 1)

            def y_ready(j):
                pe.wait_ge(S("y_lo"), Y_ORDER.index(j) + 1)

            for m in range(2):
                product(pe, pair(m), (OUT0 + m) % 4, late, xh, xl, y_ready, opens=False).then_inc(S("unit_done"), 1)
            for m in range(2, KD):
                split_ready(pe, MIX0, 0, OUT0 + m)
                pe.wait_ge(S("o_out"), m - 1)
                product(pe, pair(m % 2), (OUT0 + m) % 4, Y_ORDER, xh, xl
                        ).then_inc(S("unit_done"), 2 if m == KD - 1 else 1)

        def spread_pe(pe, big, small, p):
            for t in range(5):
                out, right = (ps[:, big, tok(t)], ident) if t < 4 else (ps[:, small, 0:NS], ident[:, P - NS:P])
                for h in range(2):
                    c = (p * 5 + t) * 2 + h
                    last = pe.matmul(out[C * h:C * h + C], st[:, 2, c:c + 1].to_broadcast([P, C]), right, start=True, stop=True)
            return last

        def mixer_act(act):
            late_squares_act(act, 2)
            for m in (2, 3):
                split_hi(act, MIX0, 0, m, KD)
            stats_act(act, 2)
            for m in range(3, NIN + 2):
                if m >= 4:
                    split_hi(act, MIX0, 0, m, KD)
                if m >= BG0 + 2:
                    in_out(act, m - 2)
                    act.activation(yb[:, m - 2 - BG0], yb[:, m - 2 - BG0], ACT.Sigmoid).then_inc(S("b_gate"), 1)
                if m == 19:
                    for p in range(2):
                        act.wait_ge(S("d_map"), p + 1)
                        act.activation(halves(yd[:, p]), pair(2 + p), ACT.Copy, scale=par_("ds", p)).then_inc(S("d_out_y"), 1)
                if m == 3:
                    act.wait_ge(S("xm"), 1)
                    act.activation(lo2[0:32], lo[0:32], ACT.Tanh)
                    act.activation(lo2[64:P], lo[64:P], ACT.Sigmoid).then_inc(S("lo2"), 1)
                if m == 5:
                    for p in range(2):
                        act.wait_ge(S("lora"), p + 1)
                        act.activation(halves(bt[:, p]), pair(2 + p), ACT.Sigmoid, bias=par_("w0", p)).then_inc(S("lora_out"), 1)
                if m == 6:
                    for p in range(2):
                        act.wait_ge(S("lora"), 2 + p + 1)
                        act.activation(halves(bh[:, p]), pair(2 + p), ACT.Sigmoid, bias=par_("a0", p)).then_inc(S("lora_out"), 1)
                if m == 7:
                    for p in range(2):
                        act.wait_ge(S("lora"), 4 + p + 1)
                        act.activation(halves(gg[:, p]), pair(2 + p), ACT.Copy).then_inc(S("lora_out"), 1)
                    for p in range(2):
                        act.wait_ge(S("kkraw"), p + 1)
                        act.activation(kt[:, p], ar[:, p, 0], ACT.Square).then_inc(S("kk_sq"), 1)
                if m == 8:
                    act.wait_ge(S("kk_max"), 1)
                    act.activation(st[:, 1, 0:20], st[:, 0, 0:20], ACT.Sqrt).then_inc(S("kk_root"), 1)
                if m in (9, 10):
                    p = m - 9
                    act.wait_ge(S("dsum"), p + 1)
                    act.activation(pend[:, p, 0:NC_], ll[:, p, 0:NP_].rearrange("p (k c) -> p k c", c=C)[:, :, C - 1], ACT.Exp, scale=-CD)
                    act.activation(pend[:, p, NC_:], comp(ll[:, p, DT])[:, :, NT - 1], ACT.Exp, scale=-CD)
                    act.activation(kt[:, p], ll[:, p], ACT.Exp, scale=CD)
                    act.activation(bt[:, p], bt[:, p], ACT.Exp, scale=-CD)
                    act.activation(kh[:, p], kh[:, p], ACT.Exp, scale=-CD).then_inc(S("exps"), 1)
                    act.wait_ge(S("exps"), 2 * p + 1)
                    act.activation(ll[:, p], ll[:, p], ACT.Exp, scale=-CD).then_inc(S("exps"), 1)
            act.wait_ge(S("out_r"), OUT_R * 16)
            act.wait_ge(S("diff"), 2)
            for t in range(4):
                wkv_act(act, t)
                if t == 0:
                    unit_done(act, MIX0, 0, NIN - 1)
                    in_out(act, AB1)
                    act.wait_ge(S("d_out_y"), 2)
                    for n in range(4):
                        split_y_hi(act, n)
                    for m in (2, 3):
                        split_hi(act, MIX0, 0, OUT0 + m, KD)
            q_act(act)
            for p in range(2):
                act.wait_ge(S("c_cen"), p + 1)
                act.activation(kt[:, p], yc[:, p], ACT.Square).then_inc(S("c_sq"), 1)
            act.wait_ge(S("c_sum"), 1)
            act.activation(st[:, 1, 0:20], ps[:, 4, 0:20], ACT.Sqrt, scale=1.0 / C, bias=C_("eps", 1, 2)).then_inc(S("c_root"), 1)
            for p in range(2):
                act.wait_ge(S("c_y"), p + 1)
                split_y_hi(act, 6 + p)
            for m in range(2, KD + 2):
                if 4 <= m < KD:
                    split_hi(act, MIX0, 0, OUT0 + m, KD, skip=m == KD - 1)
                elif m >= KD:
                    split_hi(act, FFN2, 0, m - KD, KD)
                act.wait_ge(S("o_out"), m - 1)
                squares_act(act, 3, m - 2, f[:, m - 2])

        def mixer_dve(dve):
            do = Chain(dve, "dve_steps")
            do(dve.tensor_scalar(onemka[:], par[:, PCOL["ka"]:PCOL["ka"] + 2], -1.0, 1.0, MUL, ADD))
            taps = 0

            def shifted(n):
                j, w = C_TILE[n], n % 2
                dst = {LORA: lo, K0: kp[:, 0], K1: kp[:, 1], R0: ar[:, 0, 1], R1: ar[:, 1, 1], V0: v[:, 0], V1: v[:, 1]}[n]
                row, t_ = pc[:, j], tmp2[:, w]
                four = row[:, 513:].rearrange("p (b c) -> p b c", c=5)
                in_out(dve, n)
                dve.wait_ge(S("pads"), 1)
                if n >= 2:
                    dve.wait_ge(S("xm"), n - 1)
                dve.tensor_tensor(t_[:, 0:NP_], row[:, 0:NP_], row[:, 1:513], SUB)
                do(dve.tensor_tensor(comp(t_[:, DT]), four[:, :, 0:4], four[:, :, 1:5], SUB))
                mu = par_("mu", j)
                dve.scalar_tensor_tensor(dst[:, 0:NP_], t_[:, 0:NP_], mu, row[:, 1:513], MUL, ADD)
                dve.scalar_tensor_tensor(comp(dst[:, DT]), comp(t_[:, DT]), mu, four[:, :, 1:5], MUL, ADD).then_inc(S("xm"), 1)

            def conv(k0, k1):
                for k in range(k0, k1):
                    for p in range(2):
                        w = par[:, PCOL["bw"] + 2 * k + p:PCOL["bw"] + 2 * k + p + 1]
                        z1 = zb[:, p, k:k + NP_]
                        z2 = zb[:, p, 542:].rearrange("p (b c) -> p b c", c=34)[:, :, k:k + NT]
                        y1, y2 = yb[:, p, 0:NP_], comp(yb[:, p, DT])
                        if k == 0:
                            dve.wait_ge(S("glu"), p + 1)
                            dve.tensor_scalar(y1, z1, w, par_("bb", p), MUL, ADD)
                            dve.tensor_scalar(y2, z2, w, par_("bb", p), MUL, ADD).then_inc(S("taps"), 1)
                        else:
                            dve.wait_ge(S("taps"), 2 * k + p - 1)
                            dve.scalar_tensor_tensor(y1, z1, w, y1, MUL, ADD)
                            dve.scalar_tensor_tensor(y2, z2, w, y2, MUL, ADD).then_inc(S("taps" if 2 * k + p < 61 else "conv"), 1)

            def pool_means():
                dve.wait_ge(S("pool_d"), 4)
                for g in range(4):
                    i, rows = g // 2, slice(64 * (g % 2), 64 * (g % 2) + 64)
                    s_ = (d1, d2)[g % 2][rows, i]
                    z, w = db[rows, i], con[rows, CCOL["wcol"] + i:CCOL["wcol"] + i + 1]
                    cnt = con[rows, CCOL["cnt"] + 16 * i:CCOL["cnt"] + 16 * i + 16]
                    dve.scalar_tensor_tensor(yd[rows, i, 16:NP_], s_[:, 31:527], w, z[:, 31:527], MUL, SUB)
                    dve.scalar_tensor_tensor(comp(yd[rows, i, DT]), steps(s_, 527, 15), w, steps(z, 527, 15), MUL, SUB)
                    do(dve.tensor_tensor(yd[rows, i, 0:16], s_[:, 15:31], cnt, MUL))
                    last = dve.tensor_tensor(yd[rows, i, 0:16], yd[rows, i, 0:16], z[:, 15:31], SUB)
                    if g % 2:
                        last.then_inc(S("diff"), 1)
                    else:
                        do(last)

            def leave(n):
                unit_done(dve, MIX0, 0, n)
                if n <= V1:
                    parts = pieces(pc[:, C_TILE[n]], n, 513, 1)
                elif n in (BV0, BV1):
                    parts = pieces(zb[:, n - BV0], n, 542, 30)
                elif n in (AC0, AC1):
                    parts = pieces(ub[:, n - AC0], n, 514, 2)
                elif n in (DD0, DD1):
                    dve.wait_ge(S("pads"), 3)
                    parts = pieces(db[:, n - DD0], n, 527, 15)
                elif n in (AH0, AH1):
                    parts = pieces(ub[:, n - AH0], n, 514, 2)
                    in_out(dve, AC0 + n - AH0)
                    for dst, src, r in parts:
                        last = dve.tensor_tensor(dst, dst, src, MUL)
                    do(last)
                    parts = tuple((dst, dst, r) for dst, _, r in parts)
                elif n in (AB0, AB1):
                    ya_ = halves(ya[:, n - AB0])
                    do(dve.tensor_tensor(ya_, pair(in_pair(n)), ya_, MUL))
                    parts = ((ya_, ya_, halves(rb[:])),)
                else:
                    parts = ((halves(yb[:, n - BG0]), pair(in_pair(n)), halves(rb[:])),)
                for dst, src, r in parts:
                    last = dve.tensor_tensor(dst, src, r, MUL)
                last.then_inc(S("in_dve"), 1)

            late_squares_dve(dve, 2)
            for m in (2, 3):
                split_lo(dve, MIX0, 0, m, KD)
            stats_dve(dve, 2)
            dve.wait_ge(S("n_rb"), 3)
            for m in range(2, NIN + 2):
                if m >= 4:
                    split_lo(dve, MIX0, 0, m, KD)
                n = m - 2
                leave(n)
                if n <= V1:
                    shifted(n)
                if n in (BG0, BG1):
                    i = n - BG0
                    dve.wait_ge(S("b_gate"), i + 1)
                    dve.wait_ge(S("pads"), 2)
                    z = zb[:, i]
                    dve.tensor_tensor(z[:, 30:542], z[:, 30:542], yb[:, i, 0:NP_], MUL)
                    zs = steps(z, 542, 30)
                    dve.tensor_tensor(zs, zs, comp(yb[:, i, DT]), MUL).then_inc(S("glu"), 1)
                if n in (AH0, AH1):
                    i = n - AH0
                    in_out(dve, n)
                    dve.sem_inc(S("au"), 1)
                    u1, u2 = ub[:, i, 0:514], ub[:, i, 514:].rearrange("p (b c) -> p b c", c=6)
                    for k in range(3):
                        w = par[:, PCOL["aw"] + 2 * k + i:PCOL["aw"] + 2 * k + i + 1]
                        y1, y2 = ya[:, i, 0:NP_], comp(ya[:, i, DT])
                        if k == 0:
                            dve.tensor_scalar(y1, u1[:, k:k + NP_], w, None, MUL)
                            do(dve.tensor_scalar(y2, u2[:, :, k:k + NT], w, None, MUL))
                        else:
                            dve.scalar_tensor_tensor(y1, u1[:, k:k + NP_], w, y1, MUL, ADD)
                            do(dve.scalar_tensor_tensor(y2, u2[:, :, k:k + NT], w, y2, MUL, ADD))
                if m == 5:
                    for p in range(2):
                        dve.wait_ge(S("xm"), p + 2)
                        dve.tensor_scalar(ar[:, p, 0], kp[:, p], par_("kk", p), None, MUL).then_inc(S("kkraw"), 1)
                if m == 7:
                    for p in range(2):
                        dve.wait_ge(S("lora_out"), p + 1)
                        do(dve.tensor_tensor_scan(ll[:, p], C_("scan", N), bt[:, p], 0.0, MUL, ADD))
                        dve.tensor_tensor(bt[:, p], ll[:, p], bt[:, p], SUB)
                        l1, l2 = ll[:, p, 0:NP_].rearrange("p (k c) -> p k c", c=C), comp(ll[:, p, DT])
                        dve.tensor_tensor(kh[:, p, 0:NP_].rearrange("p (k c) -> p k c", c=C),
                                          l1[:, :, C - 1:C].to_broadcast([P, NC_, C]), l1, SUB)
                        dve.tensor_tensor(comp(kh[:, p, DT]), l2[:, :, NT - 1:NT].to_broadcast([P, NB, NT]), l2, SUB
                                          ).then_inc(S("dsum"), 1)
                if m == 8:
                    for p in range(2):
                        dve.wait_ge(S("lora_out"), 4)
                        dve.wait_ge(S("xm"), 7)
                        do(dve.tensor_scalar(tmp2[:, p], bh[:, p], par_("ka", p), onemka[:, p:p + 1], MUL, ADD))
                        do(dve.tensor_tensor(kp[:, p], kp[:, p], tmp2[:, p], MUL))
                        dve.scalar_tensor_tensor(bo[:, p], ar[:, p, 1], par_("rk", p), kp[:, p], MUL, MUL).then_inc(S("rk"), 1)
                    dve.wait_ge(S("kk_sum"), 1)
                    dve.tensor_scalar(st[:, 0, 0:20], ps[:, 4, 0:20], 1e-24, None, ALU.max).then_inc(S("kk_max"), 1)
                    dve.wait_ge(S("kk_root"), 1)
                    dve.reciprocal(st[:, 2, 0:20], st[:, 1, 0:20]).then_inc(S("kk_rec"), 1)
                if m == 10:
                    for p in range(2):
                        dve.wait_ge(S("kk_spread"), p + 1)
                        dve.tensor_tensor(ar[:, p, 0, 0:NP_], ps[:, 4 + 2 * p], ar[:, p, 0, 0:NP_], MUL)
                        dve.tensor_tensor(ar[:, p, 0, DT], ps[:, 5 + 2 * p, 0:NS], ar[:, p, 0, DT], MUL).then_inc(S("kk"), 1)
                        dve.wait_ge(S("kk"), p + 1)
                        do(dve.scalar_tensor_tensor(bh[:, p], ar[:, p, 0], -1.0, bh[:, p], MUL, MUL))
                if m == 12:
                    for p in range(2):
                        dve.wait_ge(S("bo_sum"), p + 1)
                        dve.tensor_tensor(halves(bo[:, p]), pair(2 + p), halves(v[:, p]), MUL).then_inc(S("bonus"), 1)
                if m in (12, 13):
                    p = m - 12
                    dve.wait_ge(S("exps"), 2 * p + 2)
                    dve.tensor_tensor(ar[:, p, 1], ar[:, p, 1], ll[:, p], MUL)
                    do(dve.tensor_tensor(ar[:, p, 0], ar[:, p, 0], bt[:, p], MUL))
                    do(dve.tensor_tensor(bt[:, p], bh[:, p], kt[:, p], MUL))
                    dve.tensor_tensor(bh[:, p], bh[:, p], kh[:, p], MUL)
                    dve.tensor_tensor(kt[:, p], kp[:, p], kt[:, p], MUL)
                    dve.tensor_tensor(kh[:, p], kp[:, p], kh[:, p], MUL).then_inc(S("fac"), 1)
                if m == 16:
                    pool_means()
            def fill():
                nonlocal taps
                k0, taps = taps, min(31, taps + 1)
                conv(k0, taps)

            dve.wait_ge(S("out_r"), OUT_R * 16)
            for t in range(4):
                wkv_dve(dve, t, fill)
                if t == 0:
                    for n in range(4):
                        split_y_lo(dve, n)
                    for m in (2, 3):
                        split_lo(dve, MIX0, 0, OUT0 + m, KD)
            q_dve(dve)
            for n in (4, 5):
                split_y_lo(dve, n)
            for p in range(2):
                dve.wait_ge(S("c_mean"), p + 1)
                dve.scalar_tensor_tensor(halves(yc[:, p]), pair(2 + p), -1.0 / C, halves(yc[:, p]), MUL, ADD).then_inc(S("c_cen"), 1)
            dve.wait_ge(S("c_root"), 1)
            dve.reciprocal(st[:, 2, 0:20], st[:, 1, 0:20]).then_inc(S("c_rec"), 1)
            for p in range(2):
                g = par_("cg", p)
                dve.wait_ge(S("c_spread"), p + 1)
                dve.scalar_tensor_tensor(yc[:, p, 0:NP_], ps[:, 4 + 2 * p], g, yc[:, p, 0:NP_], MUL, MUL)
                dve.scalar_tensor_tensor(yc[:, p, DT], ps[:, 5 + 2 * p, 0:NS], g, yc[:, p, DT], MUL, MUL).then_inc(S("c_norm"), 1)
                dve.wait_ge(S("c_norm"), p + 1)
                do(dve.scalar_tensor_tensor(mixf[:, 4 + p], yc[:, p], par_("cb", p), bo[:, p], ADD, ADD))
                dve.tensor_tensor(mixf[:, 4 + p], mixf[:, 4 + p], gg[:, p], MUL).then_inc(S("c_y"), 1)
            for n in (6, 7):
                split_y_lo(dve, n)
            for m in range(2, KD + 2):
                if 4 <= m < KD:
                    split_lo(dve, MIX0, 0, OUT0 + m, KD, skip=m == KD - 1)
                elif m >= KD:
                    split_lo(dve, FFN2, 0, m - KD, KD)
                d = m - 2
                unit_done(dve, MIX0, 0, OUT0 + d)
                dve.tensor_copy(halves(f[:, d]), pair(d % 2)).then_inc(S("o_out"), 1)
                if d >= 2:
                    squares_dve(dve, 3, d - 1)
            squares_dve(dve, 3, KD - 1)

        @block.sync
        def _(sp):
            sp.dma_start(par[:], a["par"]).then_inc(S("in_par"), 16)
            ffn_sp(sp, 0, 0)
            mixer_sp(sp)
            ffn_sp(sp, 1, FFN2)
            for k in range(KD):
                if by_dve(5, k):
                    sp.wait_ge(S("x_last"), sum(by_dve(5, j) for j in range(k + 1)))
                else:
                    sp.wait_ge(S("x_ready"), 2 * KD + sum(not by_dve(5, j) for j in range(k + 1)))
                sp.dma_start(o["y"][:, k], x[:, k]).then_inc(S("out"), 16)
            sp.wait_ge(S("out"), (6 + KD) * 16)

        @block.tensor
        def _(pe):
            pe.sem_inc(S("unit_done"), SPL)
            ffn_pe(pe, 0, 0, 0)
            stats_pe(pe, 1)
            mixer_pe(pe)
            stats_pe(pe, 3)
            ffn_pe(pe, 1, FFN2, 4)
            stats_pe(pe, 5)

        @block.gpsimd
        def _(pool):
            post_pool(pool, 1)
            mixer_pool(pool)
            post_pool(pool, 3)
            post_pool(pool, 5)

        @block.scalar
        def _(act):
            for k in range(KD):
                act.dma_start(x[:, k], a["x"][:, k]).then_inc(S(f"in_x{k}"), 16)
            act.dma_start(con[:], a["con"]).then_inc(S("in_con"), 16)
            act.dma_start(lora_w[:], a["lora"]).then_inc(S("in_con"), 16)
            act.dma_start(dwbd[:], a["dw"]).then_inc(S("in_con"), 16)
            act.dma_start(stap[:], a["sta"]).then_inc(S("in_sta"), 16)
            split_hi(act, 0, 0, 0, KD)
            act.wait_ge(S("in_par"), 16)
            late_act(act, 0)
            split_hi(act, 0, 0, 1, KD)
            act.wait_ge(S("in_con"), 48)
            ffn_act(act, 0, 0, 1, MIX0, KD)
            stats_act(act, 1)
            late_act(act, 2)
            mixer_act(act)
            stats_act(act, 3)
            late_act(act, 4)
            ffn_act(act, 1, FFN2, 5, None, 0)
            stats_act(act, 5)

        @block.vector
        def _(dve):
            dve.sem_inc(S("w_lo"), RAW)
            for q in range(2):
                dve.sem_inc(S(f"h_mul{q}"), 2)
                dve.sem_inc(S(f"h_lo{q}"), 2)
                dve.sem_inc(S(f"d_out{q}"), 4)
            split_lo(dve, 0, 0, 0, KD)
            for k in range(KD):
                late_dve(dve, 0, k)
            split_lo(dve, 0, 0, 1, KD)
            ffn_dve(dve, 0, 0, 1, MIX0, KD)
            post_dve(dve, 1)
            mixer_dve(dve)
            post_dve(dve, 3)
            ffn_dve(dve, 1, FFN2, 5, None, 0)
            post_dve(dve, 5)


def _tiles(w):
    k, n = w.shape
    return np.ascontiguousarray(w.reshape(k // P, P, n // P, P).transpose(2, 1, 0, 3).reshape(n // P, P, k))


def _cols(v):
    return np.asarray(v).reshape(-1, P).T


def pack(inp):
    i = {k: np.asarray(v) for k, v in inp.items()}
    one = {k: v[0] for k, v in i.items() if v.shape[0] == 1}
    out = {}
    tokens = np.concatenate([i["x_prompt"].reshape(NP_, D), i["x_sample"].reshape(NS, D)])
    out["x"] = np.ascontiguousarray(tokens.T.reshape(KD, P, N).transpose(1, 0, 2))
    for q, n in enumerate(("ffn1", "ffn2")):
        g, u = _tiles(one[n + "_w_gate"]), _tiles(one[n + "_w_up"])
        out[f"w_gu{q}"] = np.ascontiguousarray(np.stack([g, u], 1).reshape(2 * FT, P, D))
        for g, (f0, nf) in enumerate(GROUPS):
            out[f"w_d{q}_{g}"] = _tiles(one[n + "_w_down"][f0 * P:(f0 + nf) * P])
    out["w_in"] = np.ascontiguousarray(_tiles(one["w_in"])[list(IN_TILES)])
    out["w_out"] = _tiles(one["w_out"])
    rows = {"g0": "ffn1_pre_g", "g1": "ffn1_post_g", "g2": "mix_pre_g", "g3": "mix_post_g", "g4": "ffn2_pre_g",
            "g5": "ffn2_post_g", "mu": "c_mu", "w0": "c_w0", "a0": "c_a0", "kk": "c_k_k", "ka": "c_k_a", "rk": "c_r_k",
            "cg": "c_ln_g", "cb": "c_ln_b", "bb": "b_conv_b", "bg": "b_ln_g", "bn": "b_ln_b", "ds": "d_scale",
            "aw": "a_conv_w", "bw": "b_conv_w"}
    out["par"] = np.ascontiguousarray(np.concatenate([_cols(one[rows[k]]) for k in PCOL], 1))
    out["lora"] = np.concatenate([one["c_w2"], one["c_a2"], one["c_g2"]])
    dw = np.zeros((P, 2, P), np.float32)
    for g in range(4):
        r = 64 * (g % 2)
        dw[r:r + 64, g // 2, r:r + 64] = one["d_w"][g]
    out["dw"] = dw
    out["con"] = constants()

    def feat(v):
        b, r, n = v.shape
        return v.reshape(b, r, n // P, P).transpose(3, 2, 0, 1).reshape(P, -1)
    out["sta"] = np.ascontiguousarray(np.concatenate([
        feat(i["state_shift_c"][0][:, None]), feat(i["state_conv_a"][0]), feat(i["state_conv_b"][0]),
        feat(i["state_pool_d"][0])], 1))
    w = i["state_wkv_c"][0].reshape(NB, 2, 2, C, C)
    out["s0"] = np.ascontiguousarray(w.transpose(2, 4, 1, 0, 3).reshape(P, 2, NB, C))
    return out


OUTS = {"y": (P, KD, N), "o_a": (P, 2, 2 + 2 * NB), "o_b": (P, 2, 30 + 30 * NB), "o_shift": (P, 7, 1 + NB),
        "o_d": (P, 2, 15 + 15 * NB), "o_sp": (P, 2, C), "o_ss": (P, 2, NB, C)}


def unpack(r):
    y = r["y"].transpose(1, 0, 2).reshape(D, N).T
    out = [y[:NP_].reshape(1, NP_, D), y[NP_:].reshape(NB, NT, D)]

    def rows(v, n):
        w = v.transpose(2, 1, 0).reshape(v.shape[2], -1)
        return w[:n][None, None], w[n:].reshape(1, NB, n, -1)
    a, b, d = rows(r["o_a"], 2), rows(r["o_b"], 30), rows(r["o_d"], 15)
    s = rows(r["o_shift"], 1)
    sp = r["o_sp"].reshape(2, C, 2, C).transpose(2, 0, 3, 1).reshape(1, 1, 4, C, C)
    ss = r["o_ss"].reshape(2, C, 2, NB, C).transpose(3, 2, 0, 4, 1).reshape(1, NB, 4, C, C)
    p = (a[0], b[0], s[0][:, :, 0], sp, d[0])
    q = (a[1], b[1], s[1][:, :, 0], ss, d[1])
    return tuple(np.ascontiguousarray(v) for v in (*out, *p, *q))


def kernel(**inputs):
    import concourse.bacc as bacc
    from concourse.bass_utils import run_bass_kernel_spmd as run

    nc = bacc.Bacc("TRN2", target_bir_lowering=False, num_devices=1)
    arrays = pack(inputs)
    a = {n: nc.dram_tensor("in_" + n, v.shape, F32, kind="ExternalInput").ap() for n, v in arrays.items()}
    o = {n: nc.dram_tensor("out_" + n, s, F32, kind="ExternalOutput").ap() for n, s in OUTS.items()}
    program(nc, a, o)
    r = run(nc, [{"in_" + n: v for n, v in arrays.items()}], core_ids=[0])
    return unpack({n: np.asarray(r.results[0]["out_" + n]) for n in OUTS})
```

```python
import numpy as np
from contextlib import ExitStack

import concourse.bass as bass
from concourse import mybir

F32 = mybir.dt.float32
F32R = mybir.dt.float32r
ALU = mybir.AluOpType
ACT = mybir.ActivationFunctionType
MUL, ADD, SUB = ALU.mult, ALU.add, ALU.subtract

P = 128
D = 1024
KD = D // P
NP_, NB, NT = 512, 8, 4
NS = NB * NT
N = NP_ + NS
H = N // 2
HP = NP_ - H
F = 2816
FT = F // P
GROUPS = ((0, 8), (8, 8), (16, 6))
G = 256
C = 64
NC_ = NP_ // C
LEVELS = (1, 2, 4, 8, 16, 32)
CD = float(np.exp(-0.5))
POOLW = (2, 4, 8, 16)
CONVB = 31

LORA, K0, K1, R0, R1, V0, V1, AC0, AC1, DD0, DD1, AH0, AH1, AB0, AB1, BV0, BV1, BG0, BG1 = range(19)
IN_TILES = (16, 12, 13, 10, 11, 14, 15, 4, 5, 17, 18, 0, 1, 2, 3, 6, 7, 8, 9)
NIN = len(IN_TILES)
C_TILE = (6, 2, 3, 0, 1, 4, 5)

PCOL = {}
_n = 0
for _name, _k in (("g0", 8), ("g1", 8), ("g2", 8), ("g3", 8), ("g4", 8), ("g5", 8), ("mu", 7), ("w0", 2), ("a0", 2),
                  ("kk", 2), ("ka", 2), ("rk", 2), ("cg", 2), ("cb", 2), ("bb", 2), ("bg", 2), ("bn", 2),
                  ("ds", 2), ("aw", 6), ("bw", 62)):
    PCOL[_name] = _n
    _n += _k
NPAR = _n
CCOL = {}
_n = 0
for _name, _k in (("ident", P), ("ones", P), ("hb", P), ("mask", 2 * P), ("lev", 6 * P), ("scan", N), ("cnt", 32),
                  ("wcol", 2), ("eps", 3), ("smask", 64), ("bsel", 8), ("idc", 64)):
    CCOL[_name] = _n
    _n += _k
NCON = _n
LORAW = 256
SCOL = {}
_n = 0
for _name, _k in (("shift", 7 * NB), ("u", 2 * NB * 2), ("z", 2 * NB * 30), ("d", 2 * NB * 15)):
    SCOL[_name] = _n
    _n += _k
NSTA = _n


def constants():
    c = np.zeros((P, NCON), np.float32)
    s, t = np.arange(P)[:, None], np.arange(P)[None, :]
    c[:, CCOL["ident"]:][:, :P] = s == t
    c[:, CCOL["ones"]:][:, :P] = 1
    c[:, CCOL["hb"]:][:, :P] = s // C == t // C
    c[:, CCOL["mask"]:][:, :P] = (s // C == t // C) & (s < t)
    c[:, CCOL["mask"] + P:][:, :P] = (s // C == t // C) & (s <= t)
    for n, b in enumerate(LEVELS):
        c[:, CCOL["lev"] + n * P:][:, :P] = (s // (2 * b) == t // (2 * b)) & (s // b != t // b) & (s < t)
    col = np.arange(N)
    start = np.where(col < NP_, col % C == 0, (col - NP_) % NT == 0)
    c[:, CCOL["scan"]:][:, :N] = 1 - start
    w = np.array(POOLW, np.float32)[(np.arange(2)[:, None] * P + np.arange(P)[None, :]) // 64]
    c[:, CCOL["wcol"]:][:, :2] = (1 / w).T
    for i in range(2):
        c[:, CCOL["cnt"] + 16 * i:][:, :16] = 1 / np.minimum(np.arange(16)[None, :] + 1, w[i][:, None])
    c[:, CCOL["eps"]:][:, :3] = (1e-6, 1e-5, 64e-5)
    c[:, CCOL["idc"]:][:, :C] = s % C == t[:, :C]
    s, t = s[:32], t[:, :32]
    c[:32, CCOL["smask"]:][:, :32] = (s // NT == t // NT) & (s < t)
    c[:32, CCOL["smask"] + 32:][:, :32] = (s // NT == t // NT) & (s <= t)
    c[:32, CCOL["bsel"]:][:, :8] = s // NT == np.arange(8)[None, :]
    return c


def program(nc, a, o):
    with ExitStack() as ctx:
        sems = {}

        def S(name):
            if name not in sems:
                sems[name] = ctx.enter_context(nc.semaphore(name))
            return sems[name]

        def sb(name, shape, dt=F32):
            return ctx.enter_context(nc.sbuf_tensor(name, [P] + shape, dt))

        x = sb("x", [KD, N])
        XH = nc.sbuf_base + 31 & ~31
        xh, xl = sb("xh", [KD, N], F32R), sb("xl", [KD, N], F32R)
        RAW, SPL = 2, 4
        raw = sb("raw", [RAW, KD, P])
        wh, wl = sb("wh", [SPL, KD, P], F32R), sb("wl", [SPL, KD, P], F32R)
        con = sb("con", [NCON])
        par = sb("par", [NPAR])
        lora_w = sb("lora_w", [LORAW])
        dwbd = sb("dwbd", [2, P])
        onemka = sb("onemka", [2])
        rb = sb("rb", [N])
        st = sb("st", [3, 24])
        ARENA = nc.sbuf_base + 31 & ~31
        END = nc.sbuf_usable_end
        spots = {"ffn": ARENA, "mix": ARENA}

        def at(space, name, shape, dt=F32, offset=None):
            size = 4 * int(np.prod(shape))
            off = spots[space] if offset is None else offset
            if offset is None:
                spots[space] += size + 31 & ~31
            assert off + size <= END, (name, off + size, END)
            return nc.alloc_sbuf_tensor_at(name, [P] + shape, dt, offset=off)

        f = at("ffn", "f", [KD, N])
        hh, hl = at("ffn", "hh", [8, N], F32R), at("ffn", "hl", [8, N], F32R)
        silu = at("ffn", "silu", [2, N])
        h32 = at("ffn", "h32", [2, N])
        sq = at("ffn", "sq", [2, N])
        ssq = at("ffn", "ssq", [N])
        tb3 = at("ffn", "tb3", [3, N])
        tb = tb3[:, 0:2]
        mixf = at("mix", "mixf", [KD, N])
        ar = at("mix", "ar", [2, 2, N])
        bt = at("mix", "bt", [2, N])
        kt = at("mix", "kt", [2, N])
        bh = at("mix", "bh", [2, N])
        kh = at("mix", "kh", [2, N])
        v = at("mix", "v", [2, N])
        gg = at("mix", "gg", [2, N])
        bo = at("mix", "bo", [2, N])
        pend = at("mix", "pend", [2, 16])
        ya, yb, yd = mixf[:, 0:2, :], mixf[:, 2:4, :], mixf[:, 6:8, :]
        tmp2 = mixf[:, 4:6, :]
        W0 = spots["mix"]
        pc = at("mix", "pc", [7, 513 + 5 * NB])
        lo = at("mix", "lo", [N])
        lo2 = at("mix", "lo2", [N])
        kp = at("mix", "kp", [2, N])
        ll = at("mix", "ll", [2, N])
        ub = at("mix", "ub", [2, 514 + 6 * NB])
        DW = 527 + 19 * NB
        db = at("mix", "db", [2, DW], offset=W0)
        d1 = at("mix", "d1", [2, DW], offset=W0 + (8 * DW + 31 & ~31))
        d2 = at("mix", "d2", [2, DW], offset=W0 + 2 * (8 * DW + 31 & ~31))
        assert W0 + 3 * (8 * DW + 31 & ~31) <= W0 + 4 * 7 * (513 + 5 * NB) + 8 * N
        stap = at("mix", "stap", [NSTA])
        so = at("mix", "so", [64])
        spots["wkv"] = W0
        rhs = at("wkv", "rhs", [2, 2, P])
        bkv = at("wkv", "bkv", [2, 5, P])
        nak = at("wkv", "nak", [2, 2, 2, 2, P])
        nrb, akr = nak[:, :, :, 0], nak[:, :, :, 1]
        nlv = at("wkv", "nlv", [2, 2, 2, P])
        tt_ = at("wkv", "tt", [2, 2, 2, P])
        xx = at("wkv", "xx", [2, 2, P])
        tu = at("wkv", "tu", [2, 2, P])
        qt = at("wkv", "qt", [2, P])
        mt = at("wkv", "mt", [2, 2, C])
        sst = at("wkv", "sst", [2, NC_, C])
        s0t = at("wkv", "s0t", [2, NB, C])
        smt = at("wkv", "smt", [2, NB, C])
        s1t = smt
        zb = at("wkv", "zb", [2, 542 + 34 * NB])
        spots["xh"], spots["xl"] = XH + 2 * 4 * N, XH + (KD + 2) * 4 * N
        qnak = at("xh", "qnak", [2, 2, 2, 2, NS])
        qnrb, qakr = qnak[:, :, :, 0], qnak[:, :, :, 1]
        qbkv = at("xh", "qbkv", [2, 3, P])
        qrhs = at("xh", "qrhs", [2, 2, P])
        qtt = at("xh", "qtt", [2, 2, 2, NS])
        assert spots["xh"] <= XH + 6 * 4 * N
        qnlv = at("xl", "qnlv", [2, 2, 2, NS])
        qxx = at("xl", "qxx", [2, 2, NS])
        qtu = at("xl", "qtu", [2, 2, P])
        qqt = at("xl", "qqt", [2, NS])
        qex = at("xl", "qex", [NB * C])
        assert spots["xl"] <= XH + (KD + 6) * 4 * N
        whole = "p a b c -> p (a b c)"
        ex3 = ((tmp2[:, 0, 0:NB * C], tmp2[:, 1, 0:NB * C], qex),
               (nlv[:, 0].rearrange(whole), nlv[:, 1].rearrange(whole), xx.rearrange(whole)))

        ps = ctx.enter_context(nc.psum_tensor("ps", [P, 8, 512], F32))

        def pair(n):
            return ps[:, 2 * n:2 * n + 2, 0:H]

        def C_(name, n=P, k=0, rows=P):
            return con[0:rows, CCOL[name] + k:CCOL[name] + k + n]

        def par_(name, k):
            return par[:, PCOL[name] + k:PCOL[name] + k + 1]

        ident, ones, hb = C_("ident"), C_("ones"), C_("hb")
        hsel = hb.rearrange("p (h c) -> p h c", h=2)[:, :, 0]

        def halves(t):
            return t.rearrange("p (a b) -> p a b", a=2)

        block = ctx.enter_context(nc.Block())

        FFN_UNITS = sum(2 * nf + KD for _, nf in GROUPS)
        MIX0 = FFN_UNITS
        FFN2 = MIX0 + NIN + KD + 1
        assert FFN_UNITS % 4 == 0 and FFN2 % 4 == 0
        SKIP = FFN2 - 1

        def load(sp, u0, i, s, src, k):
            sp.wait_ge(S("w_lo"), i * 4 + (u0 + s + 1))
            sp.dma_start(raw[:, s % RAW, 0:k, :].rearrange("p k n -> p (k n)"), src).then_inc(S(f"w_full{s % RAW}"), 16)

        def split_hi(act, u0, i, s, k, skip=0):
            loads = (u0 + s) // RAW + 1 - (SKIP % RAW == s % RAW and u0 + s > SKIP)
            act.wait_ge(S(f"w_full{s % RAW}"), i * 32 + 16 * loads)
            act.wait_ge(S("unit_done"), i * 4 + (u0 + s + 1))
            act.activation(wh[:, s % 4, 0:k, :], raw[:, s % RAW, 0:k, :], ACT.Copy
                           ).then_inc(S("w_hi"), 1 + skip)

        def split_lo(dve, u0, i, s, k, skip=0):
            dve.wait_ge(S("w_hi"), i * 4 + (u0 + s + 1))
            dve.tensor_tensor(wl[:, s % 4, 0:k, :], raw[:, s % RAW, 0:k, :], wh[:, s % 4, 0:k, :].bitcast(F32), SUB
                              ).then_inc(S("w_lo"), 1 + skip)

        def split_ready(pe, u0, i, s):
            pe.wait_ge(S("w_lo"), i * 4 + (u0 + s + 1 + RAW))

        def unit_done(eng, u0, i, s):
            eng.wait_ge(S("unit_done"), i * 4 + (u0 + s + 1 + SPL))

        def product(pe, out, s, order, right_h, right_l, before=None, opens=True, closes=True):
            for j in order:
                if before:
                    before(j)
                for n in range(2):
                    col = slice(n * H, n * H + H)
                    pe.matmul(out[:, n], wh[:, s, j], right_h[:, j, col], start=opens and j == order[0], stop=False)
                    pe.matmul(out[:, n], wh[:, s, j], right_l[:, j, col], start=False, stop=False)
                    last = pe.matmul(out[:, n], wl[:, s, j], right_h[:, j, col], start=False, stop=closes and j == order[-1])
            return last

        def tok(t):
            return slice(128 * t, 128 * t + 128) if t < 4 else slice(N - 128, N)

        def sums_pe(pe, n):
            pe.wait_ge(S("n_ssq"), n + 1)
            for t in range(5):
                m = pe.matmul(ps[:, 6, t:t + 1], ssq[:, tok(t)], ones[:, 0:1], start=True, stop=True)
            m.then_inc(S("n_sum"), 1)

        def spread_root_pe(pe, n):
            pe.wait_ge(S("n_rec"), n + 1)
            for t in range(4):
                pe.matmul(ps[:, 7, tok(t)], st[:, 2, t:t + 1].to_broadcast([P, P]), ident, start=True, stop=True)
            pe.matmul(ps[:, 6, 0:NS], st[:, 2, 4:5].to_broadcast([P, P]), ident[:, P - NS:P],
                      start=True, stop=True).then_inc(S("n_spread"), 1)

        def stats_pe(pe, n):
            sums_pe(pe, n)
            spread_root_pe(pe, n)

        def root_act(act, n):
            if n in (1, 5):
                act.wait_ge(S("n_var"), n // 4 + 1)
                act.activation(st[:, 1, 0:5], st[:, 0, 0:5], ACT.Sqrt).then_inc(S("n_root"), 1)
            else:
                act.wait_ge(S("n_sum"), n + 1)
                act.activation(st[:, 1, 0:5], ps[:, 6, 0:5], ACT.Sqrt, scale=1.0 / D, bias=C_("eps", 1)
                               ).then_inc(S("n_root"), 1)

        def stats_act(act, n):
            root_act(act, n)
            rb_act(act, n)

        def rb_act(act, n):
            act.wait_ge(S("n_spread"), n + 1)
            scale = 0.5 if n in (1, 5) else 1.0
            act.activation(rb[:, 0:512], ps[:, 7, 0:512], ACT.Copy, scale=scale)
            act.activation(rb[:, 512:N], ps[:, 6, 0:NS], ACT.Copy, scale=scale).then_inc(S("n_rb"), 1)

        def stats_dve(dve, n):
            if n in (1, 5):
                dve.wait_ge(S("n_sum"), n + 1)
                dve.wait_ge(S("n_late"), n // 4 + 1)
                dve.scalar_tensor_tensor(st[:, 0, 0:5], ps[:, 6, 0:5], 1.0 / D, st[:, 0, 8:13], MUL, ADD).then_inc(S("n_var"), 1)
            dve.wait_ge(S("n_root"), n + 1)
            if n in (0, 4):
                dve.scalar_tensor_tensor(st[:, 0, 8:13], st[:, 1, 0:5], 1e-6, st[:, 1, 0:5], MUL, MUL).then_inc(S("n_late"), 1)
            dve.reciprocal(st[:, 2, 0:5], st[:, 1, 0:5]).then_inc(S("n_rec"), 1)

        def squares_act(act, n, k, src):
            if k == 0:
                act.activation(ssq[:], src, ACT.Square).then_inc(S("n_sq"), 1)
            else:
                act.wait_ge(S("n_add"), 6 * n + max(k - 2, 0))
                act.activation(sq[:, k % 2], src, ACT.Square).then_inc(S("n_sq"), 1)

        def squares_dve(dve, n, k):
            dve.wait_ge(S("n_sq"), 8 * n + k + 1)
            dve.wait_ge(S("n_add"), 6 * n + k - 1)
            dve.tensor_tensor(ssq[:], ssq[:], sq[:, k % 2], ADD).then_inc(S("n_ssq" if k == KD - 1 else "n_add"), 1)

        def x_wait(eng, n, k):
            if n == 0:
                eng.wait_ge(S(f"in_x{k}"), 16)
            else:
                eng.wait_ge(S("x_ready"), KD * (n // 2 - 1) + k + 1)

        def late_act(act, n):
            for k in range(KD):
                x_wait(act, n, k)
                act.activation(xh[:, k], x[:, k], ACT.Copy, scale=par_(f"g{n}", k)).then_inc(S("n_xh"), 1)

        def late_squares_act(act, n):
            for k in range(KD):
                squares_act(act, n, k, x[:, k])

        def late_dve(dve, n, k):
            dve.wait_ge(S("n_xh"), KD * (n // 2) + k + 1)
            dve.scalar_tensor_tensor(xl[:, k], x[:, k], par_(f"g{n}", k), xh[:, k].bitcast(F32), MUL, SUB
                                     ).then_inc(S("n_xl"), 1)

        def late_squares_dve(dve, n):
            for k in range(1, KD):
                squares_dve(dve, n, k)

        def by_dve(n, k):
            return n == 5 and k in (2, 5, 7)

        def post_pool(pool, n):
            b = KD * (n // 2)
            for k in range(KD):
                if by_dve(n, k):
                    continue
                pool.wait_ge(S("n_t"), b + k + 1)
                pool.tensor_tensor(x[:, k], x[:, k], tb3[:, k % 3] if n == 5 else tb[:, k % 2], ADD).then_inc(S("x_ready"), 1)

        def post_dve(dve, n):
            b = KD * (n // 2)
            stats_dve(dve, n)
            dve.wait_ge(S("n_rb"), n + 1)
            for k in range(KD if n == 5 else 0):
                if k >= 3 and by_dve(n, k - 3):
                    dve.wait_ge(S("x_last"), sum(by_dve(n, j) for j in range(k - 2)))
                elif k >= 3:
                    dve.wait_ge(S("x_ready"), b + sum(not by_dve(n, j) for j in range(k - 2)))
                dve.scalar_tensor_tensor(tb3[:, k % 3], f[:, k], par_(f"g{n}", k), rb[:], MUL, MUL).then_inc(S("n_t"), 1)
                if by_dve(n, k):
                    dve.wait_ge(S("n_t"), b + k + 1)
                    dve.tensor_tensor(x[:, k], x[:, k], tb3[:, k % 3], ADD).then_inc(S("x_last"), 1)
            for k in range(KD + 2 if n < 5 else 0):
                if k < KD:
                    if k >= 2:
                        dve.wait_ge(S("x_ready"), b + k - 1)
                    dve.scalar_tensor_tensor(tb[:, k % 2], f[:, k], par_(f"g{n}", k), rb[:], MUL, MUL
                                             ).then_inc(S("n_t"), 1)
                if k >= 2 and n < 5:
                    late_dve(dve, n + 1, k - 2)

        def ffn_sp(sp, q, u0):
            u = u0
            for g, (f0, nf) in enumerate(GROUPS):
                with sp.Fori(0, nf // 2) as i:
                    for s in range(4):
                        load(sp, u, i, s, a[f"w_gu{q}"][bass.ds(i * 4 + (2 * f0 + s), 1)].rearrange("a p n -> p (a n)"), KD)
                u += 2 * nf
                with sp.Fori(0, 2) as i:
                    for s in range(4):
                        load(sp, u, i, s, a[f"w_d{q}_{g}"][bass.ds(i * 4 + s, 1)].rearrange("a p n -> p (a n)"), nf)
                u += KD

        def ffn_pe(pe, q, u0, n):
            u, dn = u0, 0

            def input_ready(j):
                pe.wait_ge(S("n_xl"), KD * (n // 2) + j + 1)

            for s in range(4):
                split_ready(pe, u, 0, s)
                if s == 3:
                    pe.wait_ge(S("n_rb"), n + 1)
                if s == 2:
                    product(pe, pair(s), s, range(KD // 2), xh, xl, closes=False)
                    spread_root_pe(pe, n)
                    product(pe, pair(s), s, range(KD // 2, KD), xh, xl, opens=False).then_inc(S("unit_done"), 1)
                    continue
                product(pe, pair(s), s, range(KD), xh, xl, input_ready if s == 0 else None).then_inc(S("unit_done"), 1)
                if s == 1:
                    pe.wait_ge(S("in_con"), 48)
                    sums_pe(pe, n)
            for g, (f0, nf) in enumerate(GROUPS):
                with pe.Fori(0 if g else 1, nf // 2) as i:
                    for s in range(4):
                        split_ready(pe, u, i, s)
                        pe.wait_ge(S(f"h_mul{q}"), i * 2 + (f0 + s // 2 + 1))
                        pe.wait_ge(S(f"d_out{q}"), dn + s + 1)
                        product(pe, pair(s), s, range(KD), xh, xl).then_inc(S("unit_done"), 1)
                u += 2 * nf

                def hidden_ready(j):
                    pe.wait_ge(S(f"h_lo{q}"), f0 + j + 1 + 2)

                with pe.Fori(0, 2) as i:
                    for s in range(4):
                        split_ready(pe, u, i, s)
                        pe.wait_ge(S(f"h_mul{q}"), f0 + nf + 2 - (s < 2))
                        pe.wait_ge(S(f"d_out{q}"), i * 4 + (dn + s + 1))
                        product(pe, pair(s), s, range(nf), hh, hl, hidden_ready if s == 0 else None
                                ).then_inc(S("unit_done"), 1)
                u += KD
                dn += KD

        def silu_act(act, q, i, f0, s):
            act.wait_ge(S(f"gate{q}"), i * 2 + (f0 + s + 1))
            act.activation(silu[:, s % 2], silu[:, s % 2], ACT.Silu).then_inc(S(f"silu{q}"), 1)

        def hidden_dve(dve, q, u, i, f0, s):
            unit_done(dve, u, i, 2 * s)
            dve.wait_ge(S(f"h_mul{q}"), i * 2 + (f0 + s + 1))
            dve.wait_ge(S("n_rb"), 5 * q if q else 1)
            dve.tensor_tensor(halves(silu[:, s % 2]), pair(2 * (s % 2)), halves(rb[:]), MUL).then_inc(S(f"gate{q}"), 1)
            unit_done(dve, u, i, 2 * s + 1)
            dve.wait_ge(S(f"silu{q}"), i * 2 + (f0 + s + 1))
            dve.wait_ge(S(f"h_lo{q}"), i * 2 + (f0 + s + 1))
            dve.tensor_tensor(halves(h32[:, s % 2]), halves(silu[:, s % 2]), pair(2 * (s % 2) + 1), MUL
                              ).then_inc(S(f"h_mul{q}"), 1)
            dve.wait_ge(S(f"h_mul{q}"), i * 2 + (f0 + s + 1 + 2))
            j = bass.ds(i * 2 + s, 1) if not isinstance(i, int) else slice(s, s + 1)
            one = "p a n -> p (a n)"
            dve.tensor_copy(hh[:, j].rearrange(one), h32[:, s % 2]).then_inc(S(f"h_hi{q}"), 1)
            dve.wait_ge(S(f"h_hi{q}"), i * 2 + (f0 + s + 1))
            dve.tensor_tensor(hl[:, j].rearrange(one), h32[:, s % 2], hh[:, j].rearrange(one).bitcast(F32), SUB
                              ).then_inc(S(f"h_lo{q}"), 1)

        def down_dve(dve, q, u, g, d, n):
            unit_done(dve, u, 0, d)
            if g == 0:
                dve.tensor_copy(halves(f[:, d]), pair(d % 4)).then_inc(S(f"d_out{q}"), 1)
            else:
                dve.wait_ge(S(f"d_out{q}"), 4 + KD * (g - 1) + d + 1)
                dve.tensor_tensor(halves(f[:, d]), pair(d % 4), halves(f[:, d]), ADD).then_inc(S(f"d_out{q}"), 1)
            if g == 2 and d >= 2:
                squares_dve(dve, n, d - 1)

        def down_act(act, q, g, d, n):
            if g == 2:
                act.wait_ge(S(f"d_out{q}"), 4 + 2 * KD + d + 1)
                squares_act(act, n, d, f[:, d])

        def ffn_act(act, q, u0, n, nxt, nk):
            u = u0
            late_squares_act(act, n - 1)
            for g, (f0, nf) in enumerate(GROUPS):
                for s in range(4):
                    if not (g == 0 and s < 2):
                        split_hi(act, u, 0, s, KD)
                    if g == 0 and s == 3:
                        stats_act(act, n - 1)
                silu_act(act, q, 0, f0, 0)
                with act.Fori(0, nf // 2 - 1) as i:
                    for s in range(4):
                        split_hi(act, u + 4, i, s, KD)
                        if s % 2:
                            silu_act(act, q, i, f0, 1 + s // 2)
                u += 2 * nf
                for s in range(KD):
                    split_hi(act, u, 0, s, nf)
                    if s == 1:
                        silu_act(act, q, 0, f0, nf - 1)
                    if s >= 2:
                        down_act(act, q, g, s - 2, n)
                u += KD
                if g == 2:
                    for s in range(2):
                        if nxt is not None:
                            split_hi(act, nxt, 0, s, nk)
                        down_act(act, q, g, KD - 2 + s, n)

        def ffn_dve(dve, q, u0, n, nxt, nk):
            u = u0
            late_squares_dve(dve, n - 1)
            for g, (f0, nf) in enumerate(GROUPS):
                for s in range(4):
                    if not (g == 0 and s < 2):
                        split_lo(dve, u, 0, s, KD)
                    if g == 0 and s == 3:
                        stats_dve(dve, n - 1)
                    if g and s < 2:
                        down_dve(dve, q, u - KD, g - 1, KD - 2 + s, n)
                hidden_dve(dve, q, u, 0, f0, 0)
                with dve.Fori(0, nf // 2 - 1) as i:
                    for s in range(4):
                        split_lo(dve, u + 4, i, s, KD)
                        if s % 2:
                            hidden_dve(dve, q, u, i, f0, 1 + s // 2)
                u += 2 * nf
                for s in range(KD):
                    split_lo(dve, u, 0, s, nf)
                    if s == 1:
                        hidden_dve(dve, q, u - 2 * nf, 0, f0, nf - 1)
                    if s >= 2:
                        down_dve(dve, q, u, g, s - 2, n)
                u += KD
                if g == 2:
                    for s in range(2):
                        if nxt is not None:
                            split_lo(dve, nxt, 0, s, nk)
                        down_dve(dve, q, u - KD, g, KD - 2 + s, n)
                    squares_dve(dve, n, KD - 1)

        def in_pair(m):
            return 2 if m == 2 else m % 2

        OUT_R = 9
        OUT0 = NIN

        def in_out(eng, m):
            eng.wait_ge(S("in_dve"), m + 1)

        def steps(t, at_, pad):
            return t[..., at_:at_ + NB * (pad + NT)].rearrange("p (b c) -> p b c", c=pad + NT)[:, :, pad:]

        def comp(t):
            return t.rearrange("p (b c) -> p b c", c=NT)

        def pieces(dst, m, at_, pad):
            src = pair(in_pair(m))
            return ((dst[:, pad:pad + H], src[:, 0], rb[:, 0:H]), (dst[:, pad + H:pad + NP_], src[:, 1, 0:HP], rb[:, H:NP_]),
                    (steps(dst, at_, pad), comp(src[:, 1, HP:H]), comp(rb[:, NP_:N])))

        class Chain:

            def __init__(self, eng, name):
                self.eng, self.name, self.n = eng, name, 0

            def __call__(self, ins):
                self.n += 1
                ins.then_inc(S(self.name), 1)
                self.eng.wait_ge(S(self.name), self.n)

        def mixer_sp(sp):
            for m in range(NIN):
                load(sp, MIX0, 0, m, a["w_in"][m], KD)
            sp.wait_ge(S("so"), 1)
            sp.dma_start(o["o_shift"], so[:, 0:7 * (1 + NB)].rearrange("p (i c) -> p i c", i=7)).then_inc(S("out_r"), 16)
            sp.wait_ge(S("au"), 2)
            us = ub[:, :, 514:].rearrange("p i (b c) -> p i b c", c=6)
            for i in range(2):
                sp.dma_start(o["o_a"][:, i, 0:2], ub[:, i, 512:514]).then_inc(S("out_r"), 16)
                sp.dma_start(o["o_a"][:, i, 2:].rearrange("p (b c) -> p b c", c=2), us[:, i, :, 4:]).then_inc(S("out_r"), 16)
            in_out(sp, DD1)
            ds_ = db[:, :, 527:].rearrange("p i (b c) -> p i b c", c=19)
            for i in range(2):
                sp.dma_start(o["o_d"][:, i, 0:15], db[:, i, 512:527]).then_inc(S("out_r"), 16)
                sp.dma_start(o["o_d"][:, i, 15:].rearrange("p (b c) -> p b c", c=15), ds_[:, i, :, 4:]).then_inc(S("out_r"), 16)
            for m in range(4):
                load(sp, MIX0, 0, OUT0 + m, a["w_out"][m], KD)
            sp.wait_ge(S("out_r"), OUT_R * 16)
            sp.wait_ge(S("diff"), 2)
            sp.dma_start(s0t[:], a["s0"]).then_inc(S("in_s0"), 16)
            sp.wait_ge(S("glu"), 2)
            zs = zb[:, :, 542:].rearrange("p i (b c) -> p i b c", c=34)
            for i in range(2):
                sp.dma_start(o["o_b"][:, i, 0:30], zb[:, i, 512:542]).then_inc(S("out"), 16)
                sp.dma_start(o["o_b"][:, i, 30:].rearrange("p (b c) -> p b c", c=30), zs[:, i, :, 4:]).then_inc(S("out"), 16)
            for m in range(4, KD):
                load(sp, MIX0, 0, OUT0 + m, a["w_out"][m], KD)
            sp.wait_ge(S("r_end"), 1)
            sp.dma_start(o["o_sp"], sst[:, :, NC_ - 1]).then_inc(S("out"), 16)
            sp.wait_ge(S("q_s1"), 2)
            sp.dma_start(o["o_ss"], s1t[:]).then_inc(S("out"), 16)

        def mixer_pool(pool):
            pool.wait_ge(S("in_sta"), 16)
            pool.wait_ge(S("n_rb"), 3)
            z = lambda name, k, c: stap[:, SCOL[name]:SCOL[name] + 2 * NB * c].rearrange("p (i b c) -> p i b c", i=2, c=c)[:, k]
            pool.memset(pc[:, :, 0:1], 0.0)
            pool.tensor_copy(pc[:, :, 513:].rearrange("p i (b c) -> p i b c", c=5)[:, :, :, 0],
                             stap[:, 0:7 * NB].rearrange("p (i b) -> p i b", b=NB)).then_inc(S("pads"), 1)
            pool.memset(ub[:, :, 0:2], 0.0)
            pool.memset(zb[:, :, 0:30], 0.0)
            for i in range(2):
                pool.tensor_copy(ub[:, i, 514:].rearrange("p (b c) -> p b c", c=6)[:, :, 0:2], z("u", i, 2))
                last = pool.tensor_copy(zb[:, i, 542:].rearrange("p (b c) -> p b c", c=34)[:, :, 0:30], z("z", i, 30))
            last.then_inc(S("pads"), 1)
            in_out(pool, V1)
            s3 = so[:, 0:7 * (1 + NB)].rearrange("p (i c) -> p i c", i=7)
            pool.tensor_copy(s3[:, :, 0:1], pc[:, :, 512:513])
            pool.tensor_copy(s3[:, :, 1:], pc[:, :, 513:].rearrange("p i (b c) -> p i b c", c=5)[:, :, :, 4]).then_inc(S("so"), 1)
            pool.wait_ge(S("xm"), 7)
            pool.wait_ge(S("so"), 1)
            pool.memset(db[:, :, 0:15], 0.0)
            for i in range(2):
                last = pool.tensor_copy(db[:, i, 527:].rearrange("p (b c) -> p b c", c=19)[:, :, 0:15], z("d", i, 15))
            last.then_inc(S("pads"), 1)
            in_out(pool, DD1)
            pool.wait_ge(S("lora"), 6)
            pool.wait_ge(S("pads"), 3)
            pool.tensor_tensor(d1[:, :, 1:], db[:, :, 1:], db[:, :, :-1], ADD).then_inc(S("pool_d"), 1)
            pool.wait_ge(S("pool_d"), 1)
            pool.tensor_tensor(d2[:, :, 3:], d1[:, :, 3:], d1[:, :, 1:-2], ADD).then_inc(S("pool_d"), 1)
            pool.wait_ge(S("pool_d"), 2)
            pool.tensor_tensor(d1[:, 1, 7:], d2[:, 1, 7:], d2[:, 1, 3:-4], ADD).then_inc(S("pool_d"), 1)
            pool.wait_ge(S("pool_d"), 3)
            pool.tensor_tensor(d2[64:P, 1, 15:], d1[64:P, 1, 15:], d1[64:P, 1, 7:-8], ADD).then_inc(S("pool_d"), 1)
            for t in range(4):
                for l in range(6):
                    for p in range(2):
                        pool.wait_ge(S("r2"), 2 * t + p + 1)
                        if l >= 2:
                            wait_job(pool, t, 2 * l, p)
                        elif t:
                            wait_job(pool, t - 1, 10 + 2 * l, p)
                        pool.tensor_tensor(nlv[:, l % 2, p], nrb[:, p, :, 0],
                                           C_("lev", k=l * P).unsqueeze(1).to_broadcast([P, 2, P]), MUL
                                           ).then_inc(S("lev"), 1)
                    if (t, l) == (2, 3):
                        for k in range(2):
                            for p in range(2):
                                pool.wait_ge(S("q2"), p + 1)
                                pool.tensor_tensor(qnlv[0:NS, k, p], qnrb[0:NS, p, :, 0],
                                                   C_("lev", NS, k * P, NS).unsqueeze(1).to_broadcast([NS, 2, NS]), MUL
                                                   ).then_inc(S("q_lev"), 1)

        NSTAGE = 20

        def wait_job(eng, t, s, p):
            eng.wait_ge(S("job"), (t * NSTAGE + s) * 2 + p + 1)

        def bank(s, p):
            return ps[:, (2 * s + p) % 4]

        def bank_free(pe, t, s, p):
            if s >= 2:
                pe.wait_ge(S(f"r{s - 2}"), 2 * t + p + 1)
            elif t:
                pe.wait_ge(S(f"r{NSTAGE + s - 2}"), 2 * (t - 1) + p + 1)

        def wkv_pe(pe, t, beside):
            tok_ = slice(P * t, P * t + P)
            hp = [slice(0, 64), slice(64, P)]

            def job(s, p):
                bank_free(pe, t, s, p)
                return bank(s, p)

            for p in range(2):
                b = job(0, p)
                for k, src in enumerate((v[:, p], bh[:, p], kh[:, p], ar[:, p, 0])):
                    last = pe.transpose(b[:, P * k:P * k + P], src[:, tok_], ident)
                last.then_inc(S("job"), 1)
            beside(t, 0)
            for h in range(2):
                for p in range(2):
                    b = job(1 + h, p)
                    for k, left in enumerate((bt, kt)):
                        last = pe.matmul(b[:, 256 * k:256 * k + 256].rearrange("p (a b) -> p a b", a=2), left[hp[h], p, tok_],
                                         ar[hp[h], p, :, tok_], start=True, stop=True)
                    last.then_inc(S("job"), 1)
                beside(t, 1 + h)
            for p in range(2):
                b = job(3, p)
                pe.wait_ge(S("lev"), t * 12 + p + 1)
                for h in range(2):
                    last = pe.matmul(b[:, P * h:P * h + P], nlv[:, 0, p, h], ident, start=True, stop=True)
                last.then_inc(S("job"), 1)
            beside(t, 3)
            for l in range(1, 6):
                for p in range(2):
                    b = job(2 + 2 * l, p)
                    pe.wait_ge(S("lev"), t * 12 + 2 * l + p + 1)
                    pe.wait_ge(S(f"r{1 + 2 * l}"), 2 * t + p + 1)
                    for h in range(2):
                        last = pe.matmul(b[:, P * h:P * h + P], nlv[:, l % 2, p, h], tt_[:, p, 0, h], start=True, stop=True)
                    last.then_inc(S("job"), 1)
                beside(t, 2 + 2 * l)
                for p in range(2):
                    b = job(3 + 2 * l, p)
                    pe.wait_ge(S(f"r{2 + 2 * l}"), 2 * t + p + 1)
                    for h in range(2):
                        if l < 5:
                            pe.matmul(b[:, P * h:P * h + P], tt_[:, p, 1, h], xx[:, p, h], start=True, stop=True)
                        last = pe.matmul(b[:, 256 + P * h:256 + P * h + P], xx[:, p, h], tt_[:, p, 1, h], start=True, stop=True)
                    last.then_inc(S("job"), 1)
                beside(t, 3 + 2 * l)
            for p in range(2):
                b = job(14, p)
                pe.wait_ge(S("r2"), 2 * t + p + 1)
                pe.wait_ge(S("r0"), 2 * t + p + 1)
                for h in range(2):
                    last = pe.matmul(b[:, C * h:C * h + C], akr[:, p, h, 0], bkv[:, p, 0, C * h:C * h + C], start=True, stop=True)
                last.then_inc(S("job"), 1)
            beside(t, 14)
            for p in range(2):
                b = job(15, p)
                pe.wait_ge(S("r13"), 2 * t + p + 1)
                pe.wait_ge(S("r14"), 2 * t + p + 1)
                for h in range(2):
                    last = pe.matmul(b[:, P * h:P * h + P], tt_[:, p, 1, h], rhs[:, p, h], start=True, stop=True)
                last.then_inc(S("job"), 1)
            beside(t, 15)
            for p in range(2):
                b = job(16, p)
                pe.wait_ge(S("r15"), 2 * t + p + 1)
                for h in range(2):
                    last = pe.matmul(b[hp[h], 0:P], tu[:, p, h, 0:C], nrb[:, p, h, 1], start=True, stop=True)
                for h in range(2):
                    last = pe.matmul(b[hp[h], P:2 * P].rearrange("p (c n) -> p c n", c=2), tu[:, p, h, 0:C],
                                     bkv[:, p, 1:5, C * h:C * h + C].rearrange("p (c k) n -> p c k n", c=2)[:, :, 0],
                                     start=True, stop=True)
                last.then_inc(S("job"), 1)
            beside(t, 16)
            for c in range(2):
                ch = 2 * t + c
                for p in range(2):
                    b = job(17 + c, p)
                    for h in range(2):
                        out = b[hp[h], 0:C]
                        pe.matmul(out, bkv[:, p, 1 + 2 * c, C * h:C * h + C], tu[:, p, h, C:P], start=True, stop=False)
                        last = pe.matmul(out, bkv[:, p, 2 + 2 * c, C * h:C * h + C], bkv[:, p, 0, C * h:C * h + C],
                                         start=False, stop=ch == 0)
                        if ch:
                            if h == 0:
                                pe.wait_ge(S("r16"), 2 * t + p + 1)
                                wait_state(pe, ch - 1, p)
                            last = pe.matmul(out, mt[hp[h], p, c], sst[hp[h], p, ch - 1], start=False, stop=True)
                    last.then_inc(S("job"), 1)
                beside(t, 17 + c)
            for p in range(2):
                b = job(19, p)
                pe.wait_ge(S("r16"), 2 * t + p + 1)
                for h in range(2):
                    out = b[hp[h], 0:P]
                    pe.matmul(out, tu[:, p, h, C:P], nrb[:, p, h, 1], start=True, stop=False)
                    last = pe.matmul(out, bkv[:, p, 0, C * h:C * h + C], akr[:, p, h, 1], start=False, stop=False)
                    for c in range(2):
                        ch = 2 * t + c
                        if ch:
                            wait_state(pe, ch - 1, p)
                            cols = slice(C * c, C * c + C)
                            last = pe.matmul(b[hp[h], cols], sst[hp[h], p, ch - 1], qt[hp[h], p, cols], start=False, stop=c == 1)
                last.then_inc(S("job"), 1)
            beside(t, 19)

        def wait_state(pe, ch, p):
            pe.wait_ge(S(f"r{17 + ch % 2}"), 2 * (ch // 2) + p + 1)

        def wkv_act(act, t, beside):
            def done(s, p):
                wait_job(act, t, s, p)
                return bank(s, p)

            for p in range(2):
                b = done(0, p)
                if t:
                    wait_job(act, t - 1, 19, p)
                act.activation(bkv[:, p, 0], b[:, 0:P], ACT.Copy)
                for c in range(2):
                    act.activation(bkv[:, p, 1 + 2 * c:3 + 2 * c], b[:, P:3 * P].rearrange("p (k c) -> p k c", k=2), ACT.Copy,
                                   scale=hb[:, C * c:C * c + 1])
                act.activation(rhs[:, p, :, 0:C], b[:, 3 * P:].rearrange("p (h c) -> p h c", h=2), ACT.Copy).then_inc(S("r0"), 1)
            for s in range(4):
                beside(t, s)
            for l in range(1, 6):
                for p in range(2):
                    s = 2 + 2 * l
                    b = done(s, p)
                    if l > 1:
                        wait_job(act, t, s - 1, p)
                    elif t:
                        wait_job(act, t - 1, 13, p)
                    act.activation(xx[:, p], b[:, 0:2 * P].rearrange("p (h c) -> p h c", h=2), ACT.Copy).then_inc(S(f"r{s}"), 1)
                beside(t, 2 + 2 * l)
                beside(t, 3 + 2 * l)
            for p in range(2):
                b = done(14, p)
                act.activation(rhs[:, p, :, C:P], b[:, 0:P].rearrange("p (h c) -> p h c", h=2), ACT.Copy).then_inc(S("r14"), 1)
            beside(t, 14)
            for p in range(2):
                b = done(15, p)
                act.activation(tu[:, p], b[:, 0:2 * P].rearrange("p (h c) -> p h c", h=2), ACT.Copy).then_inc(S("r15"), 1)
            beside(t, 15)
            beside(t, 16)
            for c in range(2):
                for p in range(2):
                    b = done(17 + c, p)
                    act.activation(sst[:, p, 2 * t + c], b[:, 0:C], ACT.Copy).then_inc(S(f"r{17 + c}"), 1)
                beside(t, 17 + c)
            for p in range(2):
                b = done(19, p)
                act.activation(yc[:, p, P * t:P * t + P], b[:, 0:P], ACT.Copy).then_inc(S("r19"), 1)
            beside(t, 19)
            if t == 3:
                act.wait_ge(S("r18"), 8)
                act.sem_inc(S("r_end"), 1)

        yc = ar[:, :, 0, :]

        def wkv_dve(dve, t, fill, beside):
            tok_ = slice(P * t, P * t + P)

            def done(s, p):
                wait_job(dve, t, s, p)
                return bank(s, p)

            mask = C_("mask", 2 * P).unsqueeze(1).to_broadcast([P, 2, 2 * P])
            for h in range(2):
                for p in range(2):
                    b = done(1 + h, p)
                    if t:
                        wait_job(dve, t - 1, 19, p)
                        dve.wait_ge(S("lev"), (t - 1) * 12 + 10 + p + 1)
                    dve.tensor_tensor(nak[:, p, h].rearrange("p w k c -> p w (k c)"), b.rearrange("p (w c) -> p w c", w=2), mask, MUL
                                      ).then_inc(S(f"r{1 + h}"), 1)
                if h:
                    fill()
            for s in range(3):
                beside(t, s)
            for p in range(2):
                b = done(3, p)
                if t:
                    wait_job(dve, t - 1, 15, p)
                idb = ident.unsqueeze(1).to_broadcast([P, 2, P])
                dve.tensor_tensor(tt_[:, p, 1], nlv[:, 0, p], idb, ADD)
                dve.tensor_tensor(tt_[:, p, 0], b[:, 0:2 * P].rearrange("p (h c) -> p h c", h=2), idb, ADD).then_inc(S("r3"), 1)
            fill()
            beside(t, 3)
            for l in range(1, 6):
                for p in range(2):
                    s = 3 + 2 * l
                    b = done(s, p)
                    dve.wait_ge(S(f"r{s - 2}"), 2 * t + p + 1)
                    k = 0 if l < 5 else 1
                    both = tt_[:, p, k:2].rearrange("p k h c -> p (k h c)")
                    dve.tensor_tensor(both, b[:, 256 * k:512], both, ADD).then_inc(S(f"r{s}"), 1)
                fill()
                beside(t, s - 1)
                beside(t, s)
            for s in (14, 15):
                beside(t, s)
            for p in range(2):
                b = done(16, p)
                if t:
                    wait_job(dve, t - 1, 19, p)
                dve.tensor_tensor(qt[:, p], b[:, 0:P], ar[:, p, 1, tok_], ADD)
                for c in range(2):
                    ch = 2 * t + c
                    last = dve.scalar_tensor_tensor(mt[:, p, c], C_("idc", C), pend[:, p, ch:ch + 1], b[:, P + C * c:P + C * c + C],
                                                    MUL, ADD)
                last.then_inc(S("r16"), 1)
            fill()
            for s in (16, 17, 18, 19):
                beside(t, s)

        BESIDE = {(1, 3): "y0", (1, 5): "y1", (1, 7): "y2", (1, 9): "y3", (1, 11): "w2", (1, 13): "w3",
                  (2, 4): "q0", (2, 5): "q1", (2, 7): "q2", (2, 9): "q3", (2, 11): "q4", (2, 13): "q5", (2, 14): "q6",
                  (2, 16): "q7", (2, 18): "q8", (3, 7): "b_mean", (3, 9): "b_var", (3, 11): "b_root",
                  (3, 14): "x0", (3, 15): "x1", (3, 16): "x2", (3, 17): "x3", (3, 18): "s0", (3, 19): "s1"}
        DT = slice(NP_, N)
        TWO = "p (h c) -> p h c"

        def wait_q(eng, s, p):
            eng.wait_ge(S("q_job"), 2 * s + p + 1)

        def qbank(s, p):
            return ps[:, 4 + 2 * (s % 2) + p]

        def q_pe(pe, step):
            hp = [slice(0, 64), slice(64, P)]

            def job(s, p):
                if s >= 2:
                    pe.wait_ge(S(f"q{s - 2}"), p + 1)
                return qbank(s, p)

            for p in range(2):
                if step == "q0":
                    b = job(0, p)
                    for k, src in enumerate((v[:, p], bh[:, p], kh[:, p], ar[:, p, 0])):
                        last = pe.transpose(b[0:NS, P * k:P * k + P], src[:, DT], ident)
                    last.then_inc(S("q_job"), 1)
                if step in ("q1", "q2"):
                    h = int(step[1]) - 1
                    b = job(1 + h, p)
                    for k, left in enumerate((bt, kt)):
                        last = pe.matmul(b[0:NS, 64 * k:64 * k + 64].rearrange("p (a b) -> p a b", a=2), left[hp[h], p, DT],
                                         ar[hp[h], p, :, DT], start=True, stop=True)
                    last.then_inc(S("q_job"), 1)
                if step == "q3":
                    b = job(3, p)
                    pe.wait_ge(S("q_lev"), p + 1)
                    for h in range(2):
                        last = pe.matmul(b[0:NS, NS * h:NS * h + NS], qnlv[0:NS, 0, p, h], ident[0:NS, 0:NS], start=True, stop=True)
                    last.then_inc(S("q_job"), 1)
                if step == "q4":
                    b = job(4, p)
                    pe.wait_ge(S("q_lev"), 2 + p + 1)
                    pe.wait_ge(S("q3"), p + 1)
                    for h in range(2):
                        last = pe.matmul(b[0:NS, NS * h:NS * h + NS], qnlv[0:NS, 1, p, h], qtt[0:NS, p, 0, h], start=True, stop=True)
                    last.then_inc(S("q_job"), 1)
                if step == "q5":
                    b = job(5, p)
                    pe.wait_ge(S("q4"), p + 1)
                    for h in range(2):
                        last = pe.matmul(b[0:NS, NS * h:NS * h + NS], qxx[0:NS, p, h], qtt[0:NS, p, 1, h], start=True, stop=True)
                    last.then_inc(S("q_job"), 1)
                if step == "q6":
                    b = job(6, p)
                    pe.wait_ge(S("q2"), p + 1)
                    pe.wait_ge(S("q0"), p + 1)
                    for h in range(2):
                        last = pe.matmul(b[0:NS, C * h:C * h + C], qakr[0:NS, p, h, 0], qbkv[0:NS, p, 0, C * h:C * h + C],
                                         start=True, stop=True)
                    last.then_inc(S("q_job"), 1)
                if step == "q7":
                    b = job(7, p)
                    pe.wait_ge(S("q5"), p + 1)
                    pe.wait_ge(S("q6"), p + 1)
                    for h in range(2):
                        last = pe.matmul(b[0:NS, P * h:P * h + P], qtt[0:NS, p, 1, h], qrhs[0:NS, p, h], start=True, stop=True)
                    last.then_inc(S("q_job"), 1)
                if step == "q8":
                    b = job(8, p)
                    pe.wait_ge(S("q7"), p + 1)
                    for h in range(2):
                        last = pe.matmul(b[hp[h], 0:NS], qtu[0:NS, p, h, 0:C], qnrb[0:NS, p, h, 1], start=True, stop=True)
                    last.then_inc(S("q_job"), 1)
            if step[0] == "x":
                p, h = divmod(int(step[1]), 2)
                b9, b10 = job(9, p), job(10, p)
                pe.wait_ge(S("b_norm"), 2)
                pe.wait_ge(S("b_rec"), 1)
                pe.wait_ge(S("ex"), 2 * p + h + 1)
                out = b10[hp[h], 0:NB * C]
                pe.matmul(b9[hp[h], 0:NB * C], qtu[0:NS, p, h, 0:C], ex3[h][2][0:NS], start=True, stop=True)
                pe.matmul(out, qbkv[0:NS, p, 1, C * h:C * h + C], ex3[h][0][0:NS], start=True, stop=False)
                pe.matmul(out, qbkv[0:NS, p, 2, C * h:C * h + C], ex3[h][1][0:NS], start=False, stop=False).then_inc(S("ex_used"), 1)
            if step[0] == "s":
                p = int(step[1])
                pe.wait_ge(S("in_s0"), 16)
                pe.wait_ge(S("q9"), p + 1)
                for h in range(2):
                    for n in range(NB):
                        last = pe.matmul(qbank(10, p)[hp[h], C * n:C * n + C], smt[hp[h], p, n], s0t[hp[h], p, n],
                                         start=False, stop=n == NB - 1)
                last.then_inc(S("q_sum"), 1)
            if step == "y":
                for p in range(2):
                    b = job(11, p)
                    pe.wait_ge(S("q8"), p + 1)
                    for h in range(2):
                        out = b[hp[h], 0:NS]
                        pe.matmul(out, qtu[0:NS, p, h, C:P], qnrb[0:NS, p, h, 1], start=True, stop=False)
                        pe.matmul(out, qbkv[0:NS, p, 0, C * h:C * h + C], qakr[0:NS, p, h, 1], start=False, stop=False)
                        for n in range(NB):
                            cols = slice(NT * n, NT * n + NT)
                            last = pe.matmul(b[hp[h], cols], s0t[hp[h], p, n], qqt[hp[h], p, cols], start=False, stop=n == NB - 1)
                    last.then_inc(S("q_sum"), 1)
            if step == "b_mean":
                pe.wait_ge(S("q7"), 2)
                pe.wait_ge(S("conv"), 1)
                for p in range(2):
                    for n in range(2):
                        last = pe.matmul(pair(3)[:, n], ones, yb[:, p, n * H:n * H + H], start=p == 0, stop=p == 1)
                last.then_inc(S("b_mean"), 1)
            if step == "b_var":
                pe.wait_ge(S("q8"), 2)
                pe.wait_ge(S("b_sq"), 2)
                for t in range(5):
                    for p in range(2):
                        last = pe.matmul(ps[:, 4, t:t + 1], tmp2[:, p, tok(t)], ones[:, 0:1], start=p == 0, stop=p == 1)
                last.then_inc(S("b_sum"), 1)
            if step == "b_root":
                pe.wait_ge(S("b_rec"), 1)
                for t in range(4):
                    pe.matmul(ps[:, 6, tok(t)], st[:, 2, t:t + 1].to_broadcast([P, P]), ident, start=True, stop=True)
                pe.matmul(ps[:, 7, 0:NS], st[:, 2, 4:5].to_broadcast([P, P]), ident[:, P - NS:P], start=True, stop=True
                          ).then_inc(S("b_spread"), 1)

        def q_act(act, step):
            if step == "s0":
                for p in range(2):
                    act.wait_ge(S("b_norm"), p + 1)
                    act.activation(yb[:, p], yb[:, p], ACT.Silu, bias=par_("bn", p)).then_inc(S("b_y"), 1)
            if step == "y0":
                unit_done(act, MIX0, 0, NIN - 1)
                in_out(act, AB1)
                act.wait_ge(S("d_out_y"), 2)
            if step in ("y0", "y1", "y2", "y3"):
                split_y_hi(act, int(step[1]))
            if step in ("w2", "w3"):
                split_hi(act, MIX0, 0, OUT0 + int(step[1]), KD)
            for p in range(2):
                if step == "q0":
                    wait_q(act, 0, p)
                    b = qbank(0, p)[0:NS]
                    act.activation(qbkv[0:NS, p], b[:, 0:3 * P].rearrange("p (k c) -> p k c", k=3), ACT.Copy)
                    act.activation(qrhs[0:NS, p, :, 0:C], b[:, 3 * P:].rearrange(TWO, h=2), ACT.Copy).then_inc(S("q0"), 1)
                if step == "q4":
                    wait_q(act, 4, p)
                    act.activation(qxx[0:NS, p], qbank(4, p)[0:NS, 0:2 * NS].rearrange(TWO, h=2), ACT.Copy).then_inc(S("q4"), 1)
                if step == "q6":
                    wait_q(act, 6, p)
                    act.activation(qrhs[0:NS, p, :, C:P], qbank(6, p)[0:NS, 0:P].rearrange(TWO, h=2), ACT.Copy).then_inc(S("q6"), 1)
                if step == "q7":
                    wait_q(act, 7, p)
                    act.activation(qtu[0:NS, p], qbank(7, p)[0:NS, 0:2 * P].rearrange(TWO, h=2), ACT.Copy).then_inc(S("q7"), 1)
                if step == f"s{p}":
                    act.wait_ge(S("q_sum"), p + 1)
                    act.activation(s1t[:, p].rearrange("p b c -> p (b c)"), qbank(10, p), ACT.Copy).then_inc(S("q_s1"), 1)
                if step == "y":
                    act.wait_ge(S("q_sum"), 2 + p + 1)
                    act.activation(yc[:, p, DT], qbank(11, p)[:, 0:NS], ACT.Copy).then_inc(S("q_y"), 1)
                if step == "b_mean":
                    act.wait_ge(S("b_cen"), p + 1)
                    act.activation(tmp2[:, p], yb[:, p], ACT.Square).then_inc(S("b_sq"), 1)
            if step == "b_var":
                act.wait_ge(S("b_sum"), 1)
                act.activation(st[:, 1, 0:5], ps[:, 4, 0:5], ACT.Sqrt, scale=1.0 / G, bias=C_("eps", 1, 1)).then_inc(S("b_dev"), 1)

        def q_dve(dve, step):
            if step in ("y0", "y1", "y2", "y3"):
                split_y_lo(dve, int(step[1]))
            if step in ("w2", "w3"):
                split_lo(dve, MIX0, 0, OUT0 + int(step[1]), KD)
            for p in range(2):
                if step in ("q1", "q2"):
                    h = int(step[1]) - 1
                    wait_q(dve, 1 + h, p)
                    mask = C_("smask", 64, rows=NS).rearrange("p (k c) -> p k c", k=2)
                    for w in range(2):
                        last = dve.tensor_tensor(qnak[0:NS, p, h, w], qbank(1 + h, p)[0:NS, 64 * w:64 * w + 64].rearrange(
                            "p (k c) -> p k c", k=2), mask, MUL)
                    last.then_inc(S(step), 1)
                if step == "q3":
                    wait_q(dve, 3, p)
                    idb = C_("ident", NS, rows=NS).unsqueeze(1).to_broadcast([NS, 2, NS])
                    dve.tensor_tensor(qtt[0:NS, p, 1], qnlv[0:NS, 0, p], idb, ADD)
                    dve.tensor_tensor(qtt[0:NS, p, 0], qbank(3, p)[0:NS, 0:2 * NS].rearrange(TWO, h=2), idb, ADD).then_inc(S("q3"), 1)
                if step == "q5":
                    wait_q(dve, 5, p)
                    dve.wait_ge(S("q3"), p + 1)
                    dve.tensor_tensor(qtt[0:NS, p, 1], qbank(5, p)[0:NS, 0:2 * NS].rearrange(TWO, h=2), qtt[0:NS, p, 1], ADD
                                      ).then_inc(S("q5"), 1)
                if step == "q8":
                    wait_q(dve, 8, p)
                    dve.tensor_tensor(qqt[:, p], qbank(8, p)[:, 0:NS], ar[:, p, 1, DT], ADD).then_inc(S("q8"), 1)
                if step == ("x2", "x3")[p]:
                    dve.wait_ge(S("ex_used"), 2 * p + 2)
                    for n in range(NB):
                        last = dve.scalar_tensor_tensor(smt[:, p, n], C_("idc", C), pend[:, p, NC_ + n:NC_ + n + 1],
                                                        qbank(9, p)[:, C * n:C * n + C], MUL, ADD)
                    last.then_inc(S("q9"), 1)
            if step == "b_root":
                dve.wait_ge(S("b_spread"), 1)
                for p in range(2):
                    g = par_("bg", p)
                    dve.scalar_tensor_tensor(yb[:, p, 0:NP_], ps[:, 6], g, yb[:, p, 0:NP_], MUL, MUL)
                    dve.scalar_tensor_tensor(yb[:, p, DT], ps[:, 7, 0:NS], g, yb[:, p, DT], MUL, MUL).then_inc(S("b_norm"), 1)
            nxt = {"b_root": 0, "x0": 1, "x1": 2, "x2": 3}.get(step)
            if nxt is not None:
                p, h = divmod(nxt, 2)
                if nxt >= 2:
                    dve.wait_ge(S("ex_used"), nxt - 1)
                if nxt == 1:
                    wait_job(dve, 3, 13, 1)
                dve.wait_ge(S("q7"), p + 1)
                sel = C_("bsel", 8, rows=NS).unsqueeze(2).to_broadcast([NS, NB, C])
                for k, src in enumerate((qtu[0:NS, p, h, C:P], qbkv[0:NS, p, 0, C * h:C * h + C], qbkv[0:NS, p, 1, C * h:C * h + C])):
                    last = dve.tensor_tensor(ex3[h][k][0:NS].rearrange("p (b c) -> p b c", c=C), src.unsqueeze(1).to_broadcast([NS, NB, C]),
                                             sel, MUL)
                last.then_inc(S("ex"), 1)
            if step == "b_mean":
                dve.wait_ge(S("b_mean"), 1)
                for p in range(2):
                    dve.scalar_tensor_tensor(halves(yb[:, p]), pair(3), -1.0 / G, halves(yb[:, p]), MUL, ADD).then_inc(S("b_cen"), 1)
            if step == "b_var":
                dve.wait_ge(S("b_dev"), 1)
                dve.reciprocal(st[:, 2, 0:5], st[:, 1, 0:5]).then_inc(S("b_rec"), 1)

        Y_ORDER = (0, 1, 6, 7, 2, 3, 4, 5)
        y32 = (ya[:, 0], ya[:, 1], yb[:, 0], yb[:, 1], mixf[:, 4], mixf[:, 5], yd[:, 0], yd[:, 1])

        def split_y_hi(act, n):
            act.activation(xh[:, Y_ORDER[n]], y32[Y_ORDER[n]], ACT.Copy).then_inc(S("y_hi"), 1)

        def split_y_lo(dve, n):
            dve.wait_ge(S("y_hi"), n + 1)
            k = Y_ORDER[n]
            dve.tensor_tensor(xl[:, k], y32[k], xh[:, k].bitcast(F32), SUB).then_inc(S("y_lo"), 1)

        def mixer_pe(pe):
            A, B = pair(2), pair(3)

            def input_ready(j):
                pe.wait_ge(S("n_xl"), KD + j + 1)

            for m in range(NIN):
                split_ready(pe, MIX0, 0, m)
                if m >= 3:
                    in_out(pe, {3: 1, 4: 0}.get(m, m - 2))
                if m == 2:
                    product(pe, pair(2), 2, range(KD // 2), xh, xl, closes=False)
                    spread_root_pe(pe, 2)
                    product(pe, pair(2), 2, range(KD // 2, KD), xh, xl, opens=False).then_inc(S("unit_done"), 1)
                    continue
                product(pe, pair(in_pair(m)), m % 4, range(KD), xh, xl, input_ready if m == 0 else None
                        ).then_inc(S("unit_done"), 1)
                if m == 1:
                    sums_pe(pe, 2)
                if m in (4, 5, 6):
                    rows = (slice(0, 32), slice(32, 64), slice(64, P))[m - 4]
                    in_out(pe, 2)
                    pe.wait_ge(S("n_rb"), 3)
                    for p in range(2):
                        pe.wait_ge(S("lo2"), 1)
                        if m > 4:
                            pe.wait_ge(S("lora_out"), 2 * (m - 4) - 1 + p)
                        for n in range(2):
                            last = pe.matmul((A, B)[p][:, n], lora_w[rows, P * p:P * p + P],
                                             (lo if m == 5 else lo2)[rows, n * H:n * H + H], start=True, stop=True)
                        last.then_inc(S("lora"), 1)
                if m == 7:
                    pe.wait_ge(S("lora_out"), 5)
                    pe.wait_ge(S("kk_sq"), 2)
                    for p in range(2):
                        for t in range(5):
                            c = (p * 5 + t) * 2
                            last = pe.matmul(ps[:, 4, c:c + 2], kt[:, p, tok(t)], hsel, start=True, stop=True)
                    last.then_inc(S("kk_sum"), 1)
                if m == 8:
                    pe.wait_ge(S("kk_rec"), 1)
                    pe.wait_ge(S("lora_out"), 6)
                    for p in range(2):
                        spread_pe(pe, 4 + 2 * p, 5 + 2 * p, p).then_inc(S("kk_spread"), 1)
                if m == 10:
                    for p in range(2):
                        pe.wait_ge(S("kk"), p + 1)
                        pe.wait_ge(S("rk"), p + 1)
                        for n in range(2):
                            last = pe.matmul((A, B)[p][:, n], hb, bo[:, p, n * H:n * H + H], start=True, stop=True)
                        last.then_inc(S("bo_sum"), 1)
                if m == 17:
                    pe.wait_ge(S("bonus"), 2)
                    for p in range(2):
                        pe.wait_ge(S("diff"), p + 1)
                        for n in range(2):
                            last = pe.matmul((A, B)[p][:, n], dwbd[:, p], yd[:, p, n * H:n * H + H], start=True, stop=True)
                        last.then_inc(S("d_map"), 1)
            in_out(pe, BG1)
            pe.wait_ge(S("d_out_y"), 2)
            pe.wait_ge(S("fac"), 2)

            def beside(t, s):
                q_pe(pe, BESIDE.get((t, s), "none"))

            for t in range(4):
                wkv_pe(pe, t, beside)
            q_pe(pe, "y")
            ad, b_, late = Y_ORDER[:4], Y_ORDER[4:6], Y_ORDER[6:]

            def y_ready(j):
                pe.wait_ge(S("y_lo"), Y_ORDER.index(j) + 1)

            def part(m, order):
                product(pe, pair(m), (OUT0 + m) % 4, order, xh, xl, y_ready, opens=order is ad, closes=False)

            pe.wait_ge(S("r19"), 8)
            pe.wait_ge(S("q_s1"), 2)
            pe.wait_ge(S("q_y"), 2)
            for p in range(2):
                for n in range(2):
                    last = pe.matmul(pair(2 + p)[:, n], hb, yc[:, p, n * H:n * H + H], start=True, stop=True)
                last.then_inc(S("c_mean"), 1)
            for m in range(2):
                split_ready(pe, MIX0, 0, OUT0 + m)
            part(0, ad)
            pe.wait_ge(S("c_sq"), 2)
            for p in range(2):
                for t in range(5):
                    c = (p * 5 + t) * 2
                    last = pe.matmul(ps[:, 4, c:c + 2], kt[:, p, tok(t)], hsel, start=True, stop=True)
            last.then_inc(S("c_sum"), 1)
            part(1, ad)
            pe.wait_ge(S("c_rec"), 1)
            for p in range(2):
                spread_pe(pe, 4 + 2 * p, 5 + 2 * p, p).then_inc(S("c_spread"), 1)
            for m in range(2):
                part(m, b_)
            for m in range(2):
                product(pe, pair(m), (OUT0 + m) % 4, late, xh, xl, y_ready, opens=False).then_inc(S("unit_done"), 1)
            for m in range(2, KD):
                split_ready(pe, MIX0, 0, OUT0 + m)
                pe.wait_ge(S("o_out"), m - 1)
                product(pe, pair(m % 2), (OUT0 + m) % 4, Y_ORDER, xh, xl
                        ).then_inc(S("unit_done"), 2 if m == KD - 1 else 1)

        def spread_pe(pe, big, small, p):
            for t in range(5):
                out, right = (ps[:, big, tok(t)], ident) if t < 4 else (ps[:, small, 0:NS], ident[:, P - NS:P])
                for h in range(2):
                    c = (p * 5 + t) * 2 + h
                    last = pe.matmul(out[C * h:C * h + C], st[:, 2, c:c + 1].to_broadcast([P, C]), right, start=True, stop=True)
            return last

        def mixer_act(act):
            late_squares_act(act, 2)
            for m in (2, 3):
                split_hi(act, MIX0, 0, m, KD)
            stats_act(act, 2)
            for m in range(3, NIN + 2):
                if m >= 4:
                    split_hi(act, MIX0, 0, m, KD)
                if m >= BG0 + 2:
                    in_out(act, m - 2)
                    act.activation(yb[:, m - 2 - BG0], yb[:, m - 2 - BG0], ACT.Sigmoid).then_inc(S("b_gate"), 1)
                if m == 19:
                    for p in range(2):
                        act.wait_ge(S("d_map"), p + 1)
                        act.activation(halves(yd[:, p]), pair(2 + p), ACT.Copy, scale=par_("ds", p)).then_inc(S("d_out_y"), 1)
                if m == 3:
                    act.wait_ge(S("xm"), 1)
                    act.activation(lo2[0:32], lo[0:32], ACT.Tanh)
                    act.activation(lo2[64:P], lo[64:P], ACT.Sigmoid).then_inc(S("lo2"), 1)
                if m == 5:
                    for p in range(2):
                        act.wait_ge(S("lora"), p + 1)
                        act.activation(halves(bt[:, p]), pair(2 + p), ACT.Sigmoid, bias=par_("w0", p)).then_inc(S("lora_out"), 1)
                if m == 6:
                    for p in range(2):
                        act.wait_ge(S("lora"), 2 + p + 1)
                        act.activation(halves(bh[:, p]), pair(2 + p), ACT.Sigmoid, bias=par_("a0", p)).then_inc(S("lora_out"), 1)
                if m == 7:
                    for p in range(2):
                        act.wait_ge(S("lora"), 4 + p + 1)
                        act.activation(halves(gg[:, p]), pair(2 + p), ACT.Copy).then_inc(S("lora_out"), 1)
                    for p in range(2):
                        act.wait_ge(S("kkraw"), p + 1)
                        act.activation(kt[:, p], ar[:, p, 0], ACT.Square).then_inc(S("kk_sq"), 1)
                if m == 8:
                    act.wait_ge(S("kk_max"), 1)
                    act.activation(st[:, 1, 0:20], st[:, 0, 0:20], ACT.Sqrt).then_inc(S("kk_root"), 1)
                if m in (9, 10):
                    p = m - 9
                    act.wait_ge(S("dsum"), p + 1)
                    act.activation(pend[:, p, 0:NC_], ll[:, p, 0:NP_].rearrange("p (k c) -> p k c", c=C)[:, :, C - 1], ACT.Exp, scale=-CD)
                    act.activation(pend[:, p, NC_:], comp(ll[:, p, DT])[:, :, NT - 1], ACT.Exp, scale=-CD)
                    act.activation(kt[:, p], ll[:, p], ACT.Exp, scale=CD)
                    act.activation(bt[:, p], bt[:, p], ACT.Exp, scale=-CD)
                    act.activation(kh[:, p], kh[:, p], ACT.Exp, scale=-CD).then_inc(S("exps"), 1)
                    act.wait_ge(S("exps"), 2 * p + 1)
                    act.activation(ll[:, p], ll[:, p], ACT.Exp, scale=-CD).then_inc(S("exps"), 1)
            act.wait_ge(S("out_r"), OUT_R * 16)
            act.wait_ge(S("diff"), 2)

            def beside(t, s):
                q_act(act, BESIDE.get((t, s), "none"))

            for t in range(4):
                wkv_act(act, t, beside)
            q_act(act, "y")
            for p in range(2):
                act.wait_ge(S("c_cen"), p + 1)
                act.activation(kt[:, p], yc[:, p], ACT.Square).then_inc(S("c_sq"), 1)
            act.wait_ge(S("c_sum"), 1)
            act.activation(st[:, 1, 0:20], ps[:, 4, 0:20], ACT.Sqrt, scale=1.0 / C, bias=C_("eps", 1, 2)).then_inc(S("c_root"), 1)
            for n in (4, 5):
                act.wait_ge(S("b_y"), n - 3)
                split_y_hi(act, n)
            for p in range(2):
                act.wait_ge(S("c_y"), p + 1)
                split_y_hi(act, 6 + p)
            for m in range(2, KD + 2):
                if 4 <= m < KD:
                    split_hi(act, MIX0, 0, OUT0 + m, KD, skip=m == KD - 1)
                elif m >= KD:
                    split_hi(act, FFN2, 0, m - KD, KD)
                act.wait_ge(S("o_out"), m - 1)
                squares_act(act, 3, m - 2, f[:, m - 2])

        def mixer_dve(dve):
            do = Chain(dve, "dve_steps")
            do(dve.tensor_scalar(onemka[:], par[:, PCOL["ka"]:PCOL["ka"] + 2], -1.0, 1.0, MUL, ADD))
            taps, fills = 0, 0

            def shifted(n):
                j, w = C_TILE[n], n % 2
                dst = {LORA: lo, K0: kp[:, 0], K1: kp[:, 1], R0: ar[:, 0, 1], R1: ar[:, 1, 1], V0: v[:, 0], V1: v[:, 1]}[n]
                row, t_ = pc[:, j], tmp2[:, w]
                four = row[:, 513:].rearrange("p (b c) -> p b c", c=5)
                in_out(dve, n)
                dve.wait_ge(S("pads"), 1)
                if n >= 2:
                    dve.wait_ge(S("xm"), n - 1)
                dve.tensor_tensor(t_[:, 0:NP_], row[:, 0:NP_], row[:, 1:513], SUB)
                do(dve.tensor_tensor(comp(t_[:, DT]), four[:, :, 0:4], four[:, :, 1:5], SUB))
                mu = par_("mu", j)
                dve.scalar_tensor_tensor(dst[:, 0:NP_], t_[:, 0:NP_], mu, row[:, 1:513], MUL, ADD)
                dve.scalar_tensor_tensor(comp(dst[:, DT]), comp(t_[:, DT]), mu, four[:, :, 1:5], MUL, ADD).then_inc(S("xm"), 1)

            def conv(k0, k1):
                for k in range(k0, k1):
                    for p in range(2):
                        w = par[:, PCOL["bw"] + 2 * k + p:PCOL["bw"] + 2 * k + p + 1]
                        z1 = zb[:, p, k:k + NP_]
                        z2 = zb[:, p, 542:].rearrange("p (b c) -> p b c", c=34)[:, :, k:k + NT]
                        y1, y2 = yb[:, p, 0:NP_], comp(yb[:, p, DT])
                        if k == 0:
                            dve.wait_ge(S("glu"), p + 1)
                            dve.tensor_scalar(y1, z1, w, par_("bb", p), MUL, ADD)
                            dve.tensor_scalar(y2, z2, w, par_("bb", p), MUL, ADD).then_inc(S("taps"), 1)
                        else:
                            dve.wait_ge(S("taps"), 2 * k + p - 1)
                            dve.scalar_tensor_tensor(y1, z1, w, y1, MUL, ADD)
                            dve.scalar_tensor_tensor(y2, z2, w, y2, MUL, ADD).then_inc(S("taps" if 2 * k + p < 61 else "conv"), 1)

            def pool_means():
                dve.wait_ge(S("pool_d"), 4)
                for g in range(4):
                    i, rows = g // 2, slice(64 * (g % 2), 64 * (g % 2) + 64)
                    s_ = (d1, d2)[g % 2][rows, i]
                    z, w = db[rows, i], con[rows, CCOL["wcol"] + i:CCOL["wcol"] + i + 1]
                    cnt = con[rows, CCOL["cnt"] + 16 * i:CCOL["cnt"] + 16 * i + 16]
                    dve.scalar_tensor_tensor(yd[rows, i, 16:NP_], s_[:, 31:527], w, z[:, 31:527], MUL, SUB)
                    dve.scalar_tensor_tensor(comp(yd[rows, i, DT]), steps(s_, 527, 15), w, steps(z, 527, 15), MUL, SUB)
                    do(dve.tensor_tensor(yd[rows, i, 0:16], s_[:, 15:31], cnt, MUL))
                    last = dve.tensor_tensor(yd[rows, i, 0:16], yd[rows, i, 0:16], z[:, 15:31], SUB)
                    if g % 2:
                        last.then_inc(S("diff"), 1)
                    else:
                        do(last)

            def leave(n):
                unit_done(dve, MIX0, 0, n)
                if n <= V1:
                    parts = pieces(pc[:, C_TILE[n]], n, 513, 1)
                elif n in (BV0, BV1):
                    parts = pieces(zb[:, n - BV0], n, 542, 30)
                elif n in (AC0, AC1):
                    parts = pieces(ub[:, n - AC0], n, 514, 2)
                elif n in (DD0, DD1):
                    dve.wait_ge(S("pads"), 3)
                    parts = pieces(db[:, n - DD0], n, 527, 15)
                elif n in (AH0, AH1):
                    parts = pieces(ub[:, n - AH0], n, 514, 2)
                    in_out(dve, AC0 + n - AH0)
                    for dst, src, r in parts:
                        last = dve.tensor_tensor(dst, dst, src, MUL)
                    do(last)
                    parts = tuple((dst, dst, r) for dst, _, r in parts)
                elif n in (AB0, AB1):
                    ya_ = halves(ya[:, n - AB0])
                    do(dve.tensor_tensor(ya_, pair(in_pair(n)), ya_, MUL))
                    parts = ((ya_, ya_, halves(rb[:])),)
                else:
                    parts = ((halves(yb[:, n - BG0]), pair(in_pair(n)), halves(rb[:])),)
                for dst, src, r in parts:
                    last = dve.tensor_tensor(dst, src, r, MUL)
                last.then_inc(S("in_dve"), 1)

            late_squares_dve(dve, 2)
            for m in (2, 3):
                split_lo(dve, MIX0, 0, m, KD)
            stats_dve(dve, 2)
            dve.wait_ge(S("n_rb"), 3)
            for m in range(2, NIN + 2):
                if m >= 4:
                    split_lo(dve, MIX0, 0, m, KD)
                n = m - 2
                if n != 1:
                    leave(n)
                if n == 0:
                    leave(1)
                if n <= V1:
                    shifted(n)
                if n in (BG0, BG1):
                    i = n - BG0
                    dve.wait_ge(S("b_gate"), i + 1)
                    dve.wait_ge(S("pads"), 2)
                    z = zb[:, i]
                    dve.tensor_tensor(z[:, 30:542], z[:, 30:542], yb[:, i, 0:NP_], MUL)
                    zs = steps(z, 542, 30)
                    dve.tensor_tensor(zs, zs, comp(yb[:, i, DT]), MUL).then_inc(S("glu"), 1)
                if n in (AH0, AH1):
                    i = n - AH0
                    in_out(dve, n)
                    dve.sem_inc(S("au"), 1)
                    u1, u2 = ub[:, i, 0:514], ub[:, i, 514:].rearrange("p (b c) -> p b c", c=6)
                    for k in range(3):
                        w = par[:, PCOL["aw"] + 2 * k + i:PCOL["aw"] + 2 * k + i + 1]
                        y1, y2 = ya[:, i, 0:NP_], comp(ya[:, i, DT])
                        if k == 0:
                            dve.tensor_scalar(y1, u1[:, k:k + NP_], w, None, MUL)
                            do(dve.tensor_scalar(y2, u2[:, :, k:k + NT], w, None, MUL))
                        else:
                            dve.scalar_tensor_tensor(y1, u1[:, k:k + NP_], w, y1, MUL, ADD)
                            do(dve.scalar_tensor_tensor(y2, u2[:, :, k:k + NT], w, y2, MUL, ADD))
                if m == 5:
                    for p in range(2):
                        dve.wait_ge(S("xm"), p + 2)
                        dve.tensor_scalar(ar[:, p, 0], kp[:, p], par_("kk", p), None, MUL).then_inc(S("kkraw"), 1)
                if m == 7:
                    for p in range(2):
                        dve.wait_ge(S("lora_out"), p + 1)
                        do(dve.tensor_tensor_scan(ll[:, p], C_("scan", N), bt[:, p], 0.0, MUL, ADD))
                        dve.tensor_tensor(bt[:, p], ll[:, p], bt[:, p], SUB)
                        l1, l2 = ll[:, p, 0:NP_].rearrange("p (k c) -> p k c", c=C), comp(ll[:, p, DT])
                        dve.tensor_tensor(kh[:, p, 0:NP_].rearrange("p (k c) -> p k c", c=C),
                                          l1[:, :, C - 1:C].to_broadcast([P, NC_, C]), l1, SUB)
                        dve.tensor_tensor(comp(kh[:, p, DT]), l2[:, :, NT - 1:NT].to_broadcast([P, NB, NT]), l2, SUB
                                          ).then_inc(S("dsum"), 1)
                if m == 8:
                    for p in range(2):
                        dve.wait_ge(S("lora_out"), 4)
                        dve.wait_ge(S("xm"), 7)
                        do(dve.tensor_scalar(tmp2[:, p], bh[:, p], par_("ka", p), onemka[:, p:p + 1], MUL, ADD))
                        do(dve.tensor_tensor(kp[:, p], kp[:, p], tmp2[:, p], MUL))
                        dve.scalar_tensor_tensor(bo[:, p], ar[:, p, 1], par_("rk", p), kp[:, p], MUL, MUL).then_inc(S("rk"), 1)
                    dve.wait_ge(S("kk_sum"), 1)
                    dve.tensor_scalar(st[:, 0, 0:20], ps[:, 4, 0:20], 1e-24, None, ALU.max).then_inc(S("kk_max"), 1)
                    dve.wait_ge(S("kk_root"), 1)
                    dve.reciprocal(st[:, 2, 0:20], st[:, 1, 0:20]).then_inc(S("kk_rec"), 1)
                if m == 10:
                    for p in range(2):
                        dve.wait_ge(S("kk_spread"), p + 1)
                        dve.tensor_tensor(ar[:, p, 0, 0:NP_], ps[:, 4 + 2 * p], ar[:, p, 0, 0:NP_], MUL)
                        dve.tensor_tensor(ar[:, p, 0, DT], ps[:, 5 + 2 * p, 0:NS], ar[:, p, 0, DT], MUL).then_inc(S("kk"), 1)
                        dve.wait_ge(S("kk"), p + 1)
                        do(dve.scalar_tensor_tensor(bh[:, p], ar[:, p, 0], -1.0, bh[:, p], MUL, MUL))
                if m == 12:
                    for p in range(2):
                        dve.wait_ge(S("bo_sum"), p + 1)
                        dve.tensor_tensor(halves(bo[:, p]), pair(2 + p), halves(v[:, p]), MUL).then_inc(S("bonus"), 1)
                if m in (12, 13):
                    p = m - 12
                    dve.wait_ge(S("exps"), 2 * p + 2)
                    dve.tensor_tensor(ar[:, p, 1], ar[:, p, 1], ll[:, p], MUL)
                    do(dve.tensor_tensor(ar[:, p, 0], ar[:, p, 0], bt[:, p], MUL))
                    do(dve.tensor_tensor(bt[:, p], bh[:, p], kt[:, p], MUL))
                    dve.tensor_tensor(bh[:, p], bh[:, p], kh[:, p], MUL)
                    dve.tensor_tensor(kt[:, p], kp[:, p], kt[:, p], MUL)
                    dve.tensor_tensor(kh[:, p], kp[:, p], kh[:, p], MUL).then_inc(S("fac"), 1)
                if m == 16:
                    pool_means()
            def fill():
                nonlocal taps, fills
                k0, fills = taps, fills + 1
                taps = min(CONVB, taps + 1 + (fills % 6 == 0))
                conv(k0, taps)

            def beside(t, s):
                q_dve(dve, BESIDE.get((t, s), "none"))

            dve.wait_ge(S("out_r"), OUT_R * 16)
            for t in range(4):
                wkv_dve(dve, t, fill, beside)
            for p in range(2):
                dve.wait_ge(S("c_mean"), p + 1)
                dve.scalar_tensor_tensor(halves(yc[:, p]), pair(2 + p), -1.0 / C, halves(yc[:, p]), MUL, ADD).then_inc(S("c_cen"), 1)
            dve.wait_ge(S("c_root"), 1)
            dve.reciprocal(st[:, 2, 0:20], st[:, 1, 0:20]).then_inc(S("c_rec"), 1)
            for n in (4, 5):
                split_y_lo(dve, n)
            for p in range(2):
                g = par_("cg", p)
                dve.wait_ge(S("c_spread"), p + 1)
                dve.scalar_tensor_tensor(yc[:, p, 0:NP_], ps[:, 4 + 2 * p], g, yc[:, p, 0:NP_], MUL, MUL)
                dve.scalar_tensor_tensor(yc[:, p, DT], ps[:, 5 + 2 * p, 0:NS], g, yc[:, p, DT], MUL, MUL).then_inc(S("c_norm"), 1)
                dve.wait_ge(S("c_norm"), p + 1)
                do(dve.scalar_tensor_tensor(mixf[:, 4 + p], yc[:, p], par_("cb", p), bo[:, p], ADD, ADD))
                dve.tensor_tensor(mixf[:, 4 + p], mixf[:, 4 + p], gg[:, p], MUL).then_inc(S("c_y"), 1)
            for n in (6, 7):
                split_y_lo(dve, n)
            for m in range(2, KD + 2):
                if 4 <= m < KD:
                    split_lo(dve, MIX0, 0, OUT0 + m, KD, skip=m == KD - 1)
                elif m >= KD:
                    split_lo(dve, FFN2, 0, m - KD, KD)
                d = m - 2
                unit_done(dve, MIX0, 0, OUT0 + d)
                dve.tensor_copy(halves(f[:, d]), pair(d % 2)).then_inc(S("o_out"), 1)
                if d >= 2:
                    squares_dve(dve, 3, d - 1)
            squares_dve(dve, 3, KD - 1)

        @block.sync
        def _(sp):
            sp.dma_start(par[:], a["par"]).then_inc(S("in_par"), 16)
            ffn_sp(sp, 0, 0)
            mixer_sp(sp)
            ffn_sp(sp, 1, FFN2)
            for k in range(KD):
                if by_dve(5, k):
                    sp.wait_ge(S("x_last"), sum(by_dve(5, j) for j in range(k + 1)))
                else:
                    sp.wait_ge(S("x_ready"), 2 * KD + sum(not by_dve(5, j) for j in range(k + 1)))
                sp.dma_start(o["y"][:, k], x[:, k]).then_inc(S("out"), 16)
            sp.wait_ge(S("out"), (6 + KD) * 16)

        @block.tensor
        def _(pe):
            pe.sem_inc(S("unit_done"), SPL)
            ffn_pe(pe, 0, 0, 0)
            stats_pe(pe, 1)
            mixer_pe(pe)
            stats_pe(pe, 3)
            ffn_pe(pe, 1, FFN2, 4)
            stats_pe(pe, 5)

        @block.gpsimd
        def _(pool):
            post_pool(pool, 1)
            mixer_pool(pool)
            post_pool(pool, 3)
            post_pool(pool, 5)

        @block.scalar
        def _(act):
            for k in range(KD):
                act.dma_start(x[:, k], a["x"][:, k]).then_inc(S(f"in_x{k}"), 16)
            act.dma_start(con[:], a["con"]).then_inc(S("in_con"), 16)
            act.dma_start(lora_w[:], a["lora"]).then_inc(S("in_con"), 16)
            act.dma_start(dwbd[:], a["dw"]).then_inc(S("in_con"), 16)
            act.dma_start(stap[:], a["sta"]).then_inc(S("in_sta"), 16)
            split_hi(act, 0, 0, 0, KD)
            act.wait_ge(S("in_par"), 16)
            late_act(act, 0)
            split_hi(act, 0, 0, 1, KD)
            act.wait_ge(S("in_con"), 48)
            ffn_act(act, 0, 0, 1, MIX0, KD)
            stats_act(act, 1)
            late_act(act, 2)
            mixer_act(act)
            stats_act(act, 3)
            late_act(act, 4)
            ffn_act(act, 1, FFN2, 5, None, 0)
            stats_act(act, 5)

        @block.vector
        def _(dve):
            dve.sem_inc(S("w_lo"), RAW)
            for q in range(2):
                dve.sem_inc(S(f"h_mul{q}"), 2)
                dve.sem_inc(S(f"h_lo{q}"), 2)
                dve.sem_inc(S(f"d_out{q}"), 4)
            split_lo(dve, 0, 0, 0, KD)
            for k in range(KD):
                late_dve(dve, 0, k)
            split_lo(dve, 0, 0, 1, KD)
            ffn_dve(dve, 0, 0, 1, MIX0, KD)
            post_dve(dve, 1)
            mixer_dve(dve)
            post_dve(dve, 3)
            ffn_dve(dve, 1, FFN2, 5, None, 0)
            post_dve(dve, 5)


def _tiles(w):
    k, n = w.shape
    return np.ascontiguousarray(w.reshape(k // P, P, n // P, P).transpose(2, 1, 0, 3).reshape(n // P, P, k))


def _cols(v):
    return np.asarray(v).reshape(-1, P).T


def pack(inp):
    i = {k: np.asarray(v) for k, v in inp.items()}
    one = {k: v[0] for k, v in i.items() if v.shape[0] == 1}
    out = {}
    tokens = np.concatenate([i["x_prompt"].reshape(NP_, D), i["x_sample"].reshape(NS, D)])
    out["x"] = np.ascontiguousarray(tokens.T.reshape(KD, P, N).transpose(1, 0, 2))
    for q, n in enumerate(("ffn1", "ffn2")):
        g, u = _tiles(one[n + "_w_gate"]), _tiles(one[n + "_w_up"])
        out[f"w_gu{q}"] = np.ascontiguousarray(np.stack([g, u], 1).reshape(2 * FT, P, D))
        for g, (f0, nf) in enumerate(GROUPS):
            out[f"w_d{q}_{g}"] = _tiles(one[n + "_w_down"][f0 * P:(f0 + nf) * P])
    out["w_in"] = np.ascontiguousarray(_tiles(one["w_in"])[list(IN_TILES)])
    out["w_out"] = _tiles(one["w_out"])
    rows = {"g0": "ffn1_pre_g", "g1": "ffn1_post_g", "g2": "mix_pre_g", "g3": "mix_post_g", "g4": "ffn2_pre_g",
            "g5": "ffn2_post_g", "mu": "c_mu", "w0": "c_w0", "a0": "c_a0", "kk": "c_k_k", "ka": "c_k_a", "rk": "c_r_k",
            "cg": "c_ln_g", "cb": "c_ln_b", "bb": "b_conv_b", "bg": "b_ln_g", "bn": "b_ln_b", "ds": "d_scale",
            "aw": "a_conv_w", "bw": "b_conv_w"}
    out["par"] = np.ascontiguousarray(np.concatenate([_cols(one[rows[k]]) for k in PCOL], 1))
    out["lora"] = np.concatenate([one["c_w2"], one["c_a2"], one["c_g2"]])
    dw = np.zeros((P, 2, P), np.float32)
    for g in range(4):
        r = 64 * (g % 2)
        dw[r:r + 64, g // 2, r:r + 64] = one["d_w"][g]
    out["dw"] = dw
    out["con"] = constants()

    def feat(v):
        b, r, n = v.shape
        return v.reshape(b, r, n // P, P).transpose(3, 2, 0, 1).reshape(P, -1)
    out["sta"] = np.ascontiguousarray(np.concatenate([
        feat(i["state_shift_c"][0][:, None]), feat(i["state_conv_a"][0]), feat(i["state_conv_b"][0]),
        feat(i["state_pool_d"][0])], 1))
    w = i["state_wkv_c"][0].reshape(NB, 2, 2, C, C)
    out["s0"] = np.ascontiguousarray(w.transpose(2, 4, 1, 0, 3).reshape(P, 2, NB, C))
    return out


OUTS = {"y": (P, KD, N), "o_a": (P, 2, 2 + 2 * NB), "o_b": (P, 2, 30 + 30 * NB), "o_shift": (P, 7, 1 + NB),
        "o_d": (P, 2, 15 + 15 * NB), "o_sp": (P, 2, C), "o_ss": (P, 2, NB, C)}


def unpack(r):
    y = r["y"].transpose(1, 0, 2).reshape(D, N).T
    out = [y[:NP_].reshape(1, NP_, D), y[NP_:].reshape(NB, NT, D)]

    def rows(v, n):
        w = v.transpose(2, 1, 0).reshape(v.shape[2], -1)
        return w[:n][None, None], w[n:].reshape(1, NB, n, -1)
    a, b, d = rows(r["o_a"], 2), rows(r["o_b"], 30), rows(r["o_d"], 15)
    s = rows(r["o_shift"], 1)
    sp = r["o_sp"].reshape(2, C, 2, C).transpose(2, 0, 3, 1).reshape(1, 1, 4, C, C)
    ss = r["o_ss"].reshape(2, C, 2, NB, C).transpose(3, 2, 0, 4, 1).reshape(1, NB, 4, C, C)
    p = (a[0], b[0], s[0][:, :, 0], sp, d[0])
    q = (a[1], b[1], s[1][:, :, 0], ss, d[1])
    return tuple(np.ascontiguousarray(v) for v in (*out, *p, *q))


def kernel(**inputs):
    import concourse.bacc as bacc
    from concourse.bass_utils import run_bass_kernel_spmd as run

    nc = bacc.Bacc("TRN2", target_bir_lowering=False, num_devices=1)
    arrays = pack(inputs)
    a = {n: nc.dram_tensor("in_" + n, v.shape, F32, kind="ExternalInput").ap() for n, v in arrays.items()}
    o = {n: nc.dram_tensor("out_" + n, s, F32, kind="ExternalOutput").ap() for n, s in OUTS.items()}
    program(nc, a, o)
    r = run(nc, [{"in_" + n: v for n, v in arrays.items()}], core_ids=[0])
    return unpack({n: np.asarray(r.results[0]["out_" + n]) for n in OUTS})
```
